# Optimizing a Trainium2 kernel written in Bass

```python
import jax, jax.numpy as jnp
from jax import lax
import numpy as np

D_MODEL = 1024
BATCH = 1
SEQ = 256
DEPTH = 2

GRID_W = 64
CTX_LEN = 256
N_MIXERS = 2
N_HEADS = 16
N_KV_HEADS = 4
HEAD_DIM = D_MODEL // N_HEADS
GROUP = N_HEADS // N_KV_HEADS
Q_DIM = N_HEADS * HEAD_DIM
KV_DIM = N_KV_HEADS * HEAD_DIM
WINDOW = 128
BLOCK = 128
ROPE_THETA = 10000.0
ROPE_QUARTER = HEAD_DIM // 4
CONV_WIDTH = 3
D_FF = 2816
N_MOD = 9
RMS_EPS = 1e-6
NEG_INF = -1e30
HALF_STEP = 0.5


def rmsnorm(x, g):
    xf = x.astype(jnp.float32)
    y = xf * lax.rsqrt(jnp.mean(xf * xf, axis=-1, keepdims=True) + RMS_EPS)
    return (y * g.astype(jnp.float32)).astype(x.dtype)

def adaln_in(x, g, shift, scale):
    return rmsnorm(x, g) * (1 + scale) + shift

def adaln_out(x, y, g, gate, weight):
    return x + weight * gate * rmsnorm(y, g)

def swiglu(h, w_gu, w_down):
    gu = h @ w_gu
    return (jax.nn.silu(gu[..., :D_FF]) * gu[..., D_FF:]) @ w_down

def ffn_sublayer(x, mod, k, g_pre, g_post, w_gu, w_down):
    h = adaln_in(x, g_pre, mod[k], mod[k + 1])
    return adaln_out(x, swiglu(h, w_gu, w_down), g_post, mod[k + 2], HALF_STEP)

def short_conv_mixer(h, w_in, w_conv, w_out):
    bcu = h @ w_in
    b, cg, u = bcu[..., :D_MODEL], bcu[..., D_MODEL:2 * D_MODEL], bcu[..., 2 * D_MODEL:]
    up = jnp.pad(cg * u, ((0, 0), (1, 1), (0, 0)))
    y = w_conv[0] * up[:, :-2] + w_conv[1] * up[:, 1:-1] + w_conv[2] * up[:, 2:]
    return (b * y) @ w_out

def axial_rope_tables(n_tokens, dtype):
    rows = n_tokens // GRID_W
    row = jnp.broadcast_to(jnp.arange(rows)[:, None], (rows, GRID_W)).reshape(-1).astype(jnp.float32)
    col = jnp.broadcast_to(jnp.arange(GRID_W)[None, :], (rows, GRID_W)).reshape(-1).astype(jnp.float32)
    inv_freq = ROPE_THETA ** (-jnp.arange(ROPE_QUARTER, dtype=jnp.float32) / ROPE_QUARTER)
    ang = jnp.stack([row[:, None] * inv_freq, col[:, None] * inv_freq], axis=1)
    return jnp.cos(ang)[:, None].astype(dtype), jnp.sin(ang)[:, None].astype(dtype)

def apply_rope(t, cos, sin):
    t4 = t.reshape(t.shape[:-1] + (2, 2, ROPE_QUARTER))
    x1, x2 = t4[..., 0, :], t4[..., 1, :]
    out = jnp.stack([x1 * cos - x2 * sin, x2 * cos + x1 * sin], axis=-2)
    return out.reshape(t.shape)

def banded_blocks(t, nb):
    B = t.shape[0]
    tp = jnp.pad(t, ((0, 0), (BLOCK, BLOCK), (0, 0), (0, 0)))
    tp = tp.reshape(B, nb + 2, BLOCK, N_KV_HEADS, HEAD_DIM)
    return jnp.concatenate([tp[:, :-2], tp[:, 1:-1], tp[:, 2:]], axis=2)

def band_mask(nb, n_tokens):
    a = jnp.arange(BLOCK)[:, None]
    b = jnp.arange(3 * BLOCK)[None, :]
    off = b - a
    in_win = (off >= BLOCK - WINDOW) & (off <= BLOCK + WINDOW)
    key_pos = (jnp.arange(nb)[:, None] - 1) * BLOCK + b
    valid = (key_pos >= 0) & (key_pos < n_tokens)
    return in_win[None] & valid[:, None, :]

def window_attention_mixer(hx, hz, w_qkv, w_o, sink, cos, sin, ctx_queries):
    B, S, _ = hx.shape
    C = hz.shape[1]
    nb = S // BLOCK
    nk = 3 * BLOCK
    scale = HEAD_DIM ** -0.5
    qkv = hx @ w_qkv
    q = apply_rope(qkv[..., :Q_DIM].reshape(B, S, N_HEADS, HEAD_DIM), cos, sin) * scale
    k = apply_rope(qkv[..., Q_DIM:Q_DIM + KV_DIM].reshape(B, S, N_KV_HEADS, HEAD_DIM), cos, sin)
    v = qkv[..., Q_DIM + KV_DIM:].reshape(B, S, N_KV_HEADS, HEAD_DIM)
    kvz = hz @ w_qkv[:, Q_DIM:]
    kz = kvz[..., :KV_DIM].reshape(B, C, N_KV_HEADS, HEAD_DIM)
    vz = kvz[..., KV_DIM:].reshape(B, C, N_KV_HEADS, HEAD_DIM)
    sink_l = sink.reshape(N_KV_HEADS, GROUP).astype(jnp.float32)

    qb = q.reshape(B, nb, BLOCK, N_KV_HEADS, GROUP, HEAD_DIM)
    kb = banded_blocks(k, nb)
    vb = banded_blocks(v, nb)
    s_win = jnp.einsum('bnqhgd,bnkhd->bnhgqk', qb, kb).astype(jnp.float32)
    s_win = jnp.where(band_mask(nb, S)[None, :, None, None], s_win, NEG_INF)
    s_ctx = jnp.einsum('bnqhgd,bchd->bnhgqc', qb, kz).astype(jnp.float32)
    s_sink = jnp.broadcast_to(sink_l[None, None, :, :, None, None], s_win.shape[:-1] + (1,))
    p = jax.nn.softmax(jnp.concatenate([s_win, s_ctx, s_sink], axis=-1), axis=-1).astype(v.dtype)
    o = (jnp.einsum('bnhgqk,bnkhd->bnqhgd', p[..., :nk], vb)
         + jnp.einsum('bnhgqc,bchd->bnqhgd', p[..., nk:nk + C], vz))
    yx = o.reshape(B, S, Q_DIM) @ w_o

    yz = None
    if ctx_queries:
        qz = (hz @ w_qkv[:, :Q_DIM]).reshape(B, C, N_KV_HEADS, GROUP, HEAD_DIM) * scale
        sz = jnp.einsum('bqhgd,bkhd->bhgqk', qz, kz).astype(jnp.float32)
        sz_sink = jnp.broadcast_to(sink_l[None, :, :, None, None], sz.shape[:-1] + (1,))
        pz = jax.nn.softmax(jnp.concatenate([sz, sz_sink], axis=-1), axis=-1).astype(vz.dtype)
        oz = jnp.einsum('bhgqk,bkhd->bqhgd', pz[..., :C], vz)
        yz = oz.reshape(B, C, Q_DIM) @ w_o
    return yx, yz

def first_inputs(seed: int = 0) -> dict:
    key = jax.random.key(seed)
    ks = jax.random.split(key, 16)
    n_conv = (DEPTH + 1) // N_MIXERS
    n_attn = DEPTH // N_MIXERS

    def w(k, shape, fan_in, gain=1.0):
        return gain * fan_in ** -0.5 * jax.random.normal(k, shape, jnp.float32)

    return {
        'x': jax.random.normal(ks[0], (BATCH, SEQ, D_MODEL), jnp.float32),
        'c': jax.random.normal(ks[1], (BATCH, D_MODEL), jnp.float32),
        'ctx': jax.random.normal(ks[2], (BATCH, CTX_LEN, D_MODEL), jnp.float32),
        'c_ctx': jax.random.normal(ks[3], (D_MODEL,), jnp.float32),
        'w_mod': w(ks[4], (DEPTH, D_MODEL, N_MOD * D_MODEL), D_MODEL, 0.5),
        'b_mod': 0.02 * jax.random.normal(ks[5], (DEPTH, N_MOD * D_MODEL), jnp.float32),
        'norm_g': 1.0 + 0.05 * jax.random.normal(ks[6], (DEPTH, 6, D_MODEL), jnp.float32),
        'ffn_w_gu': w(ks[7], (DEPTH, 2, D_MODEL, 2 * D_FF), D_MODEL),
        'ffn_w_down': w(ks[8], (DEPTH, 2, D_FF, D_MODEL), D_FF),
        'conv_w_in': w(ks[9], (n_conv, D_MODEL, 3 * D_MODEL), D_MODEL),
        'conv_w': w(ks[10], (n_conv, CONV_WIDTH, D_MODEL), CONV_WIDTH),
        'conv_w_out': w(ks[11], (n_conv, D_MODEL, D_MODEL), D_MODEL),
        'attn_w_qkv': w(ks[12], (n_attn, D_MODEL, Q_DIM + 2 * KV_DIM), D_MODEL),
        'attn_w_o': w(ks[13], (n_attn, Q_DIM, D_MODEL), Q_DIM),
        'attn_sink': 0.5 * jax.random.normal(ks[14], (n_attn, N_HEADS), jnp.float32),
    }

def first_block(x, c, ctx, c_ctx, w_mod, b_mod, norm_g, ffn_w_gu, ffn_w_down,
              conv_w_in, conv_w, conv_w_out, attn_w_qkv, attn_w_o, attn_sink):
    B, S, D = x.shape
    cos, sin = axial_rope_tables(S, x.dtype)
    z = ctx
    for i in range(DEPTH):
        last = i == DEPTH - 1
        use_attn = (i % N_MIXERS) == 1
        j = i // N_MIXERS
        g = norm_g[i]
        mx = (jax.nn.silu(c) @ w_mod[i] + b_mod[i]).reshape(B, N_MOD, 1, D).transpose(1, 0, 2, 3)
        mz = (jax.nn.silu(c_ctx) @ w_mod[i] + b_mod[i]).reshape(N_MOD, D)
        ctx_needed = (not last) or use_attn

        x = ffn_sublayer(x, mx, 0, g[0], g[1], ffn_w_gu[i, 0], ffn_w_down[i, 0])
        if ctx_needed:
            z = ffn_sublayer(z, mz, 0, g[0], g[1], ffn_w_gu[i, 0], ffn_w_down[i, 0])

        hx = adaln_in(x, g[2], mx[3], mx[4])
        if use_attn:
            hz = adaln_in(z, g[2], mz[3], mz[4])
            yx, yz = window_attention_mixer(hx, hz, attn_w_qkv[j], attn_w_o[j], attn_sink[j],
                                            cos, sin, not last)
        else:
            yx = short_conv_mixer(hx, conv_w_in[j], conv_w[j], conv_w_out[j])
            yz = None
            if not last:
                hz = adaln_in(z, g[2], mz[3], mz[4])
                yz = short_conv_mixer(hz, conv_w_in[j], conv_w[j], conv_w_out[j])
        x = adaln_out(x, yx, g[3], mx[5], 1.0)

        x = ffn_sublayer(x, mx, 6, g[4], g[5], ffn_w_gu[i, 1], ffn_w_down[i, 1])
        if not last:
            z = adaln_out(z, yz, g[3], mz[5], 1.0)
            z = ffn_sublayer(z, mz, 6, g[4], g[5], ffn_w_gu[i, 1], ffn_w_down[i, 1])
    return x


DEPTH_2 = 1

HEAD_DIM_2 = 64
ROPE_DIM = HEAD_DIM_2 // 4
ROPE_THETA_2 = 500000.0
NORM_EPS = 1e-6
ATTN_SCALE = HEAD_DIM_2 ** -0.5

NSA_HEADS = 8
NSA_GROUPS = 2
NSA_REP = NSA_HEADS // NSA_GROUPS
CMP_LEN = 32
CMP_STRIDE = 16
CMP_HIDDEN = 256
SEL_BLOCK = 64
SEL_TOPN = 8
WINDOW_2 = 512
WIN_QBLOCK = 128
NSA_QCHUNK = 64

MOBA_HEADS = 8
MOBA_BLOCK = 256
MOBA_TOPK = 3
MOBA_QCHUNK = 16

PAD_MULT = 256
D_FF_2 = ((-(-8 * D_MODEL // 3)) + 255) // 256 * 256
PLE_DIM = 256

IN_SPLITS = ((NSA_HEADS * HEAD_DIM_2,) + (NSA_GROUPS * HEAD_DIM_2,) * 6 + (3 * NSA_HEADS,)
             + (MOBA_HEADS * HEAD_DIM_2,) * 3 + (D_MODEL, D_MODEL))
IN_COLS = sum(IN_SPLITS)
IN_CUTS = tuple(int(c) for c in np.cumsum(IN_SPLITS)[:-1])


def rms_norm(x, g):
    xf = x.astype(jnp.float32)
    y = xf * lax.rsqrt(jnp.mean(xf * xf, axis=-1, keepdims=True) + NORM_EPS)
    return (y * g.astype(jnp.float32)).astype(x.dtype)

def partial_rope(t, pos):
    half = ROPE_DIM // 2
    inv_freq = ROPE_THETA_2 ** (-jnp.arange(half, dtype=jnp.float32) / half)
    ang = pos.astype(jnp.float32)[..., None] * inv_freq
    cos, sin = jnp.cos(ang), jnp.sin(ang)
    tr = t[..., :ROPE_DIM].astype(jnp.float32)
    t1, t2 = tr[..., :half], tr[..., half:]
    rot = jnp.concatenate([t1 * cos - t2 * sin, t2 * cos + t1 * sin], axis=-1)
    return jnp.concatenate([rot.astype(t.dtype), t[..., ROPE_DIM:]], axis=-1)

def masked_softmax(scores, mask):
    s = jnp.where(mask, scores.astype(jnp.float32), -jnp.inf)
    m = jnp.max(s, axis=-1, keepdims=True)
    m = jnp.where(jnp.isfinite(m), m, 0.0)
    e = jnp.where(mask, jnp.exp(s - m), 0.0)
    return e / jnp.maximum(jnp.sum(e, axis=-1, keepdims=True), 1e-30)

def to_heads(t, n):
    b, s, _ = t.shape
    return t.reshape(b, s, n, HEAD_DIM_2).transpose(0, 2, 1, 3)

def from_heads(t):
    b, n, s, d = t.shape
    return t.transpose(0, 2, 1, 3).reshape(b, s, n * d)

def compress_blocks(t, pe, w1, w2):
    b, g, sp, d = t.shape
    n_sub, per = sp // CMP_STRIDE, CMP_LEN // CMP_STRIDE
    sub = t.reshape(b, g, n_sub, CMP_STRIDE, d)
    nc = n_sub - per + 1
    blocks = jnp.concatenate([sub[:, :, i:i + nc] for i in range(per)], axis=3)
    flat = (blocks + pe).reshape(b, g, nc, CMP_LEN * d)
    return jax.nn.silu(flat @ w1) @ w2

def nsa_mixer(q_in, kc_in, vc_in, ks_in, vs_in, kw_in, vw_in, gate_in, pos_pad,
              q_gain, kc_gain, ks_gain, kw_gain, pe_k, pe_v, ck_w1, ck_w2, cv_w1, cv_w2):
    b, sp, _ = q_in.shape
    G, R, dh = NSA_GROUPS, NSA_REP, HEAD_DIM_2
    pos_h = pos_pad[:, None, :]
    t_idx = jnp.arange(sp)
    q = partial_rope(rms_norm(to_heads(q_in, NSA_HEADS), q_gain), pos_h).reshape(b, G, R, sp, dh)

    kc = rms_norm(compress_blocks(to_heads(kc_in, G), pe_k, ck_w1, ck_w2), kc_gain)
    vc = compress_blocks(to_heads(vc_in, G), pe_v, cv_w1, cv_w2)
    nc = kc.shape[2]
    cmp_start = jnp.arange(nc) * CMP_STRIDE
    cmp_end = cmp_start + CMP_LEN - 1
    kc = partial_rope(kc, pos_pad[:, cmp_end][:, None, :])
    s_c = jnp.einsum('bgrtd,bgcd->bgrtc', q, kc) * ATTN_SCALE
    p_c = masked_softmax(s_c, cmp_end[None, :] <= t_idx[:, None])
    o_c = jnp.einsum('bgrtc,bgcd->bgrtd', p_c.astype(vc.dtype), vc)

    ns = sp // SEL_BLOCK
    j = jnp.arange(ns)
    overlap = ((cmp_start[:, None] <= j[None, :] * SEL_BLOCK + SEL_BLOCK - 1)
               & (cmp_end[:, None] >= j[None, :] * SEL_BLOCK)).astype(jnp.float32)
    imp = jnp.einsum('bgrtc,cj->bgtj', p_c, overlap)
    cur = (t_idx // SEL_BLOCK)[:, None]
    forced = (j[None, :] == 0) | (j[None, :] == cur) | (j[None, :] == cur - 1)
    imp = jnp.where(forced, jnp.inf, jnp.where(j[None, :] > cur, -jnp.inf, imp))
    n_top = min(SEL_TOPN, ns)
    _, sel_idx = lax.top_k(imp, n_top)

    ks = partial_rope(rms_norm(to_heads(ks_in, G), ks_gain), pos_h)
    vs = to_heads(vs_in, G)
    ks_blk = ks.reshape(b, G, ns, SEL_BLOCK, dh)
    vs_blk = vs.reshape(b, G, ns, SEL_BLOCK, dh)
    nq = sp // NSA_QCHUNK
    bi = jnp.arange(b)[:, None, None, None]
    gi = jnp.arange(G)[None, :, None, None]
    m_sel = n_top * SEL_BLOCK

    def sel_chunk(args):
        qc, ic, tc = args
        kg = ks_blk[bi, gi, ic].reshape(b, G, NSA_QCHUNK, m_sel, dh)
        vg = vs_blk[bi, gi, ic].reshape(b, G, NSA_QCHUNK, m_sel, dh)
        kpos = (ic[..., None] * SEL_BLOCK + jnp.arange(SEL_BLOCK)).reshape(b, G, NSA_QCHUNK, m_sel)
        mask = (kpos <= tc[None, None, :, None])[:, :, None]
        s = jnp.einsum('bgrcd,bgcmd->bgrcm', qc, kg) * ATTN_SCALE
        pr = masked_softmax(s, mask)
        return jnp.einsum('bgrcm,bgcmd->bgrcd', pr.astype(vg.dtype), vg)

    q_ch = q.reshape(b, G, R, nq, NSA_QCHUNK, dh).transpose(3, 0, 1, 2, 4, 5)
    idx_ch = sel_idx.reshape(b, G, nq, NSA_QCHUNK, n_top).transpose(2, 0, 1, 3, 4)
    o_s = lax.map(sel_chunk, (q_ch, idx_ch, t_idx.reshape(nq, NSA_QCHUNK)))
    o_s = o_s.transpose(1, 2, 3, 0, 4, 5).reshape(b, G, R, sp, dh)

    kw = partial_rope(rms_norm(to_heads(kw_in, G), kw_gain), pos_h)
    vw = to_heads(vw_in, G)
    nw, nprev = sp // WIN_QBLOCK, WINDOW_2 // WIN_QBLOCK
    band = (nprev + 1) * WIN_QBLOCK

    def banded(t):
        tb = jnp.pad(t.reshape(b, G, nw, WIN_QBLOCK, dh), ((0, 0), (0, 0), (nprev, 0), (0, 0), (0, 0)))
        return jnp.concatenate([tb[:, :, i:i + nw] for i in range(nprev + 1)], axis=3).transpose(2, 0, 1, 3, 4)

    def win_block(args):
        qb, kb, vb, w = args
        qpos = w * WIN_QBLOCK + jnp.arange(WIN_QBLOCK)
        kpos = (w - nprev) * WIN_QBLOCK + jnp.arange(band)
        diff = qpos[:, None] - kpos[None, :]
        mask = (diff >= 0) & (diff < WINDOW_2) & (kpos[None, :] >= 0)
        s = jnp.einsum('bgrqd,bgkd->bgrqk', qb, kb) * ATTN_SCALE
        pr = masked_softmax(s, mask)
        return jnp.einsum('bgrqk,bgkd->bgrqd', pr.astype(vb.dtype), vb)

    q_w = q.reshape(b, G, R, nw, WIN_QBLOCK, dh).transpose(3, 0, 1, 2, 4, 5)
    o_w = lax.map(win_block, (q_w, banded(kw), banded(vw), jnp.arange(nw)))
    o_w = o_w.transpose(1, 2, 3, 0, 4, 5).reshape(b, G, R, sp, dh)

    g = jax.nn.sigmoid(gate_in.reshape(b, sp, NSA_HEADS, 3)).transpose(0, 2, 1, 3).reshape(b, G, R, sp, 3)
    o = g[..., 0:1] * o_c + g[..., 1:2] * o_s + g[..., 2:3] * o_w
    return from_heads(o.reshape(b, NSA_HEADS, sp, dh))

def moba_mixer(q_in, k_in, v_in, pos_pad, q_gain, k_gain):
    b, sp, _ = q_in.shape
    H, dh, BS, C = MOBA_HEADS, HEAD_DIM_2, MOBA_BLOCK, MOBA_QCHUNK
    pos_h = pos_pad[:, None, :]
    t_idx = jnp.arange(sp)
    q = partial_rope(rms_norm(to_heads(q_in, H), q_gain), pos_h)
    k = partial_rope(rms_norm(to_heads(k_in, H), k_gain), pos_h)
    v = to_heads(v_in, H)
    nb = sp // BS
    k_blk = k.reshape(b, H, nb, BS, dh)
    v_blk = v.reshape(b, H, nb, BS, dh)
    k_mean = jnp.mean(k_blk.astype(jnp.float32), axis=3)
    score = jnp.einsum('bhtd,bhnd->bhtn', q.astype(jnp.float32), k_mean)
    own = (t_idx // BS)[:, None]
    score = jnp.where(jnp.arange(nb)[None, :] < own, score, -jnp.inf)
    n_top = min(MOBA_TOPK, nb)
    _, sel_idx = lax.top_k(score, n_top)
    bi = jnp.arange(b)[:, None, None, None]
    hi = jnp.arange(H)[None, :, None, None]
    nq = sp // C
    m_sel = n_top * BS

    def chunk(args):
        qc, ic, c = args
        start = c * C
        blk = start // BS
        k_own = lax.dynamic_slice_in_dim(k, blk * BS, BS, axis=2)
        v_own = lax.dynamic_slice_in_dim(v, blk * BS, BS, axis=2)
        qpos = start + jnp.arange(C)
        m_own = jnp.broadcast_to(blk * BS + jnp.arange(BS)[None, :] <= qpos[:, None], (b, H, C, BS))
        m_sel_mask = jnp.broadcast_to((ic < blk)[..., None], (b, H, C, n_top, BS)).reshape(b, H, C, m_sel)
        kg = k_blk[bi, hi, ic].reshape(b, H, C, m_sel, dh)
        vg = v_blk[bi, hi, ic].reshape(b, H, C, m_sel, dh)
        s = jnp.concatenate([jnp.einsum('bhcd,bhpd->bhcp', qc, k_own),
                             jnp.einsum('bhcd,bhcmd->bhcm', qc, kg)], axis=-1) * ATTN_SCALE
        pr = masked_softmax(s, jnp.concatenate([m_own, m_sel_mask], axis=-1)).astype(v.dtype)
        return (jnp.einsum('bhcp,bhpd->bhcd', pr[..., :BS], v_own)
                + jnp.einsum('bhcm,bhcmd->bhcd', pr[..., BS:], vg))

    q_ch = q.reshape(b, H, nq, C, dh).transpose(2, 0, 1, 3, 4)
    idx_ch = sel_idx.reshape(b, H, nq, C, n_top).transpose(2, 0, 1, 3, 4)
    o = lax.map(chunk, (q_ch, idx_ch, jnp.arange(nq)))
    o = o.transpose(1, 2, 0, 3, 4).reshape(b, H, sp, dh)
    return from_heads(o)

def second_inputs(seed: int = 0) -> dict:
    key = jax.random.key(seed)
    ks = jax.random.split(key, 25)

    def normal(k, shape, scale):
        return jax.random.normal(k, shape, jnp.float32) * scale

    def gain(k, n):
        return 1.0 + 0.1 * jax.random.normal(k, (DEPTH_2, n), jnp.float32)

    L, dh = DEPTH_2, HEAD_DIM_2
    nsa_w, moba_w = NSA_HEADS * dh, MOBA_HEADS * dh
    return {
        'x': normal(ks[0], (BATCH, SEQ, D_MODEL), 1.0),
        'p': normal(ks[1], (DEPTH_2, BATCH, SEQ, PLE_DIM), 1.0),
        'positions': jnp.tile(jnp.arange(SEQ, dtype=jnp.int32)[None, :], (BATCH, 1)),
        'g_mix': gain(ks[2], D_MODEL),
        'w_in': normal(ks[3], (L, D_MODEL, IN_COLS), D_MODEL ** -0.5),
        'nsa_q_gain': gain(ks[4], dh),
        'nsa_kc_gain': gain(ks[5], dh),
        'nsa_ks_gain': gain(ks[6], dh),
        'nsa_kw_gain': gain(ks[7], dh),
        'nsa_pe_k': normal(ks[8], (L, CMP_LEN, dh), 0.1),
        'nsa_pe_v': normal(ks[9], (L, CMP_LEN, dh), 0.1),
        'nsa_ck_w1': normal(ks[10], (L, CMP_LEN * dh, CMP_HIDDEN), (CMP_LEN * dh) ** -0.5),
        'nsa_ck_w2': normal(ks[11], (L, CMP_HIDDEN, dh), CMP_HIDDEN ** -0.5),
        'nsa_cv_w1': normal(ks[12], (L, CMP_LEN * dh, CMP_HIDDEN), (CMP_LEN * dh) ** -0.5),
        'nsa_cv_w2': normal(ks[13], (L, CMP_HIDDEN, dh), CMP_HIDDEN ** -0.5),
        'moba_q_gain': gain(ks[14], dh),
        'moba_k_gain': gain(ks[15], dh),
        'w_up_nsa': normal(ks[16], (L, nsa_w, D_MODEL), nsa_w ** -0.5),
        'w_up_moba': normal(ks[17], (L, moba_w, D_MODEL), moba_w ** -0.5),
        'w_out': normal(ks[18], (L, D_MODEL, D_MODEL), D_MODEL ** -0.5),
        'g_ffn': gain(ks[19], D_MODEL),
        'w_ffn_in': normal(ks[20], (L, D_MODEL, 2 * D_FF_2), D_MODEL ** -0.5),
        'w_ffn_out': normal(ks[21], (L, D_FF_2, D_MODEL), D_FF_2 ** -0.5),
        'g_ple': gain(ks[22], D_MODEL),
        'w_ple_gate': normal(ks[23], (L, D_MODEL, D_MODEL), D_MODEL ** -0.5),
        'w_ple_proj': normal(ks[24], (L, PLE_DIM, D_MODEL), PLE_DIM ** -0.5),
    }

def second_block(x, p, positions, g_mix, w_in, nsa_q_gain, nsa_kc_gain, nsa_ks_gain, nsa_kw_gain,
              nsa_pe_k, nsa_pe_v, nsa_ck_w1, nsa_ck_w2, nsa_cv_w1, nsa_cv_w2,
              moba_q_gain, moba_k_gain, w_up_nsa, w_up_moba, w_out,
              g_ffn, w_ffn_in, w_ffn_out, g_ple, w_ple_gate, w_ple_proj):
    b, s, _ = x.shape
    sp = -(-s // PAD_MULT) * PAD_MULT
    extra = jnp.arange(1, sp - s + 1, dtype=positions.dtype)
    pos_pad = jnp.concatenate([positions, positions[:, -1:] + extra[None, :]], axis=1)
    for i in range(DEPTH_2):
        proj = rms_norm(x, g_mix[i]) @ w_in[i]
        proj = jnp.pad(proj, ((0, 0), (0, sp - s), (0, 0)))
        (q_n, kc_n, vc_n, ks_n, vs_n, kw_n, vw_n, gate_n,
         q_m, k_m, v_m, gate_a, gate_b) = jnp.split(proj, IN_CUTS, axis=-1)
        y_nsa = nsa_mixer(q_n, kc_n, vc_n, ks_n, vs_n, kw_n, vw_n, gate_n, pos_pad,
                          nsa_q_gain[i], nsa_kc_gain[i], nsa_ks_gain[i], nsa_kw_gain[i],
                          nsa_pe_k[i], nsa_pe_v[i], nsa_ck_w1[i], nsa_ck_w2[i],
                          nsa_cv_w1[i], nsa_cv_w2[i])[:, :s]
        y_moba = moba_mixer(q_m, k_m, v_m, pos_pad, moba_q_gain[i], moba_k_gain[i])[:, :s]
        merged = (jax.nn.sigmoid(gate_a[:, :s]) * (y_nsa @ w_up_nsa[i])
                  + jax.nn.sigmoid(gate_b[:, :s]) * (y_moba @ w_up_moba[i]))
        x = x + merged @ w_out[i]
        gate, up = jnp.split(rms_norm(x, g_ffn[i]) @ w_ffn_in[i], 2, axis=-1)
        x = x + (jax.nn.silu(gate) * up) @ w_ffn_out[i]
        ple_gate = jax.nn.sigmoid(rms_norm(x, g_ple[i]) @ w_ple_gate[i])
        x = x + ple_gate * (p[i] @ w_ple_proj[i])
    return x


def setup_inputs(seed=0):
    out = dict(first_inputs(seed))
    for name, value in second_inputs(seed + 1).items():
        if name != "x":
            out[name + "_2"] = value
    return out


def reference(
    x, c, ctx, c_ctx, w_mod, b_mod, norm_g, ffn_w_gu, ffn_w_down, conv_w_in, conv_w, conv_w_out,
    attn_w_qkv, attn_w_o, attn_sink, p_2, positions_2, g_mix_2, w_in_2, nsa_q_gain_2,
    nsa_kc_gain_2, nsa_ks_gain_2, nsa_kw_gain_2, nsa_pe_k_2, nsa_pe_v_2, nsa_ck_w1_2,
    nsa_ck_w2_2, nsa_cv_w1_2, nsa_cv_w2_2, moba_q_gain_2, moba_k_gain_2, w_up_nsa_2,
    w_up_moba_2, w_out_2, g_ffn_2, w_ffn_in_2, w_ffn_out_2, g_ple_2, w_ple_gate_2, w_ple_proj_2,
):
    x = first_block(
        x, c, ctx, c_ctx, w_mod, b_mod, norm_g, ffn_w_gu, ffn_w_down, conv_w_in, conv_w,
        conv_w_out, attn_w_qkv, attn_w_o, attn_sink,
    )
    return second_block(
        x, p_2, positions_2, g_mix_2, w_in_2, nsa_q_gain_2, nsa_kc_gain_2, nsa_ks_gain_2,
        nsa_kw_gain_2, nsa_pe_k_2, nsa_pe_v_2, nsa_ck_w1_2, nsa_ck_w2_2, nsa_cv_w1_2,
        nsa_cv_w2_2, moba_q_gain_2, moba_k_gain_2, w_up_nsa_2, w_up_moba_2, w_out_2, g_ffn_2,
        w_ffn_in_2, w_ffn_out_2, g_ple_2, w_ple_gate_2, w_ple_proj_2,
    )


_drawn_inputs = setup_inputs


def setup_inputs(seed=0):
    import zlib

    import numpy as np

    out = dict(_drawn_inputs(seed))
    spreads = {}
    factors = {'attn_sink': 8.0,
     'nsa_q_gain_2': 7.18,
     'nsa_kc_gain_2': 8.0,
     'nsa_ks_gain_2': 8.0,
     'nsa_kw_gain_2': 8.0,
     'nsa_pe_k_2': 8.0,
     'nsa_pe_v_2': 3.951,
     'moba_q_gain_2': 7.178,
     'moba_k_gain_2': 8.0,
     'g_ple_2': 3.98}
    for name, (base, spread) in spreads.items():
        noise = np.random.default_rng([zlib.crc32(name.encode()), seed]).standard_normal(out[name].shape)
        drawn = base * np.exp(spread * noise) if base else spread * noise
        out[name] = __import__('jax').numpy.asarray(drawn.astype(out[name].dtype))
    for name, factor in factors.items():
        out[name] = (out[name] * factor).astype(out[name].dtype)
    return out
```

```python
from contextlib import ExitStack

import concourse.bass as bass
from concourse import mybir

F32 = mybir.dt.float32
F32R = mybir.dt.float32r
I32 = mybir.dt.int32
ALU = mybir.AluOpType
ACT = mybir.ActivationFunctionType
ENG = mybir.EngineType

P = 128
D = 1024
NC = D // P
S = 256
T2 = 2 * S
D_FF = 2816
FFN_HALVES = (12, 10)
assert sum(FFN_HALVES) * P == D_FF
N_MOD = 9
HD = 64
EPS = 1e-6
CREDIT = 2
UNIT = 2048
NEG = -1e30
TWO_PI_HI = 6.28125
TWO_PI_MID = 0.0019350051879882812
TWO_PI_LO = 3.019916050561733e-07
PI_SAFE = 3.1415925


class Count:

    def __init__(self, nc, name):
        self.sem = nc.alloc_semaphore(name)
        self.n = 0

    def inc(self, ins, by=1):
        ins.then_inc(self.sem, by)
        self.n += by
        return self.n


def wait(eng, count, value=None):
    value = count.n if value is None else value
    if not isinstance(value, int) or value > 0:
        eng.wait_ge(count.sem, value)


def build(nc, t, out, vec_at, stop=None):
    pe, dve, act, sp, pool = nc.tensor, nc.vector, nc.scalar, nc.sync, nc.gpsimd
    mem = ExitStack()

    def sb(name, shape, dt=F32, stack=None):
        return (stack or mem).enter_context(nc.sbuf_tensor(name, list(shape), dt))

    n_vec = t["vecs"].shape[1]
    vecs = sb("vecs", [P, n_vec])
    mats = sb("mats", [P, 4, P])
    swap2 = sb("swap2", [P, P])
    ident, ones, head_ones, swap1 = (mats[:, j, :] for j in range(4))
    w_raw = [sb(f"w_raw{j}", [P, UNIT]) for j in range(2)]
    w_hi = [sb(f"w_hi{j}", [P, UNIT], F32R) for j in range(2)]
    w_lo = [sb(f"w_lo{j}", [P, UNIT], F32R) for j in range(2)]
    x = sb("x", [P, NC, T2])
    gate_tmp = sb("gate_tmp", [P, 2, T2])
    prod = sb("prod", [P, 2, T2])
    sq = sb("sq", [P, 2, T2])
    rstd = sb("rstd", [P, T2])
    stats = sb("stats", [P, 5, 64])
    y = sb("y", [P, NC, T2])
    ps_g = mem.enter_context(nc.psum_tensor("ps_g", [P, 4, 512], F32))
    ps_s = mem.enter_context(nc.psum_tensor("ps_s", [P, 4, 512], F32))

    def vec(name, j=0, n=1):
        a = vec_at[name] + j
        return vecs[:, a:a + n]

    loaded = [Count(nc, f"loaded{j}") for j in range(2)]
    split_hi = Count(nc, "split_hi")
    split_lo = Count(nc, "split_lo")
    unit_done = Count(nc, "unit_done")
    evac = Count(nc, "evac")
    gate_made = Count(nc, "gate_made")
    out_hi = Count(nc, "out_hi")
    out_lo = Count(nc, "out_lo")
    consts_in = Count(nc, "consts_in")
    v_ = Count(nc, "vector_steps")
    a_ = Count(nc, "scalar_steps")
    p_ = Count(nc, "tensor_steps")
    g_ = Count(nc, "pool_steps")
    mod_loaded = [Count(nc, f"mod_loaded{j}") for j in range(2)]
    mod_done = Count(nc, "mod_done")
    mod_kept = Count(nc, "mod_kept")

    def V(ins):
        return v_.inc(ins)

    def A(ins):
        return a_.inc(ins)

    def PEs(ins):
        return p_.inc(ins)

    for c in (evac, out_lo):
        for _ in range(CREDIT):
            c.inc(dve.memset(stats[:, 0, 0:1], 0.0))
            wait(dve, c)

    for dst, src in ((vecs[:], t["vecs"]), (mats[:], t["mats"]), (swap2[:], t["swap2"]),
                     (x[:, :, 0:S], t["x"]), (x[:, :, S:T2], t["ctx"])):
        consts_in.inc(act.dma_start(dst, src), 16)
    for e in (pe, dve, act):
        wait(e, consts_in)

    class Phase:

        def __init__(self, w, n_units, elems, pe_unit, evacuate, mod=0):
            self.w, self.n, self.elems = w, n_units, elems
            self.pe_unit, self.evacuate, self.mod = pe_unit, evacuate, mod

        def load(self):
            self.u0 = loaded[0].n // 16 * 2
            nb = (self.n + 1) // 2

            def body(i, slots=2):
                for j in range(slots):
                    u = self.u0 + 2 * i + j
                    wait(sp, split_lo, 2 * u - 2)
                    sp.dma_start(w_raw[j][:, 0:self.elems], self.w[2 * i + j]).then_inc(loaded[j].sem, 16)
                for m in range(self.mod):
                    mod_load(mod_u0 + i * self.mod + m, m % 2)
            mod_u0 = mod_loaded[0].n // 16 * 2
            if self.n == 1:
                body(0, 1)
            elif nb == 1:
                body(0)
            else:
                body(0)
                with nc.Fori(1, nb, engines=(ENG.SP,)) as i:
                    body(i)
            for j in range(2):
                loaded[j].n += 16 * nb
                mod_loaded[j].n += 16 * nb * self.mod // 2

        def split(self, ul, slot):
            u = self.u0 + ul
            half = self.elems // 2
            wait(act, loaded[slot], (u // 2 + 1) * 16 if isinstance(ul, int) else self.loaded_at(ul, slot))
            wait(act, unit_done, u - 1)
            for h in range(2):
                a, b = h * half, (h + 1) * half
                act.activation(w_hi[slot][:, a:b], w_raw[slot][:, a:b], ACT.Copy).then_inc(split_hi.sem, 1)
            for h in range(2):
                a, b = h * half, (h + 1) * half
                wait(dve, split_hi, 2 * u + h + 1)
                dve.tensor_tensor(w_lo[slot][:, a:b], w_raw[slot][:, a:b], w_hi[slot][:, a:b].bitcast(F32),
                                  ALU.subtract).then_inc(split_lo.sem, 1)

        def loaded_at(self, ul, slot):
            return (self.u0 // 2 + 1) * 16 + (ul - slot) * 8

        def multiply(self):
            nb = (self.n + 1) // 2
            mod_u0 = mod_done.n

            def body(i, slots=2):
                for j in range(slots):
                    u = self.u0 + 2 * i + j
                    wait(pe, split_lo, 2 * u + 2)
                    wait(pe, evac, CREDIT + u - 1)
                    self.pe_unit(2 * i + j, j).then_inc(unit_done.sem, 1)
                    for m in range(j * self.mod // 2, (j + 1) * self.mod // 2):
                        mod_multiply(mod_u0 + i * self.mod + m, m % 2)
            if self.n <= 2:
                body(0, self.n)
            else:
                body(0)
                with nc.Fori(1, nb, engines=(ENG.PE,)) as i:
                    body(i)

        def run(self, after=None):
            self.multiply()
            nb = (self.n + 1) // 2
            mod_u0 = mod_kept.n

            def mods(i, j):
                for m in range(j * self.mod // 2, (j + 1) * self.mod // 2):
                    mod_keep(mod_u0 + i * self.mod + m, m % 2)

            def body(i):
                for j in range(2):
                    self.split(2 * i + 2 + j, j)
                    self.evacuate(2 * i + j, j)
                    mods(i, j)
            if nb > 1:
                with nc.Fori(0, nb - 1, engines=(ENG.DVE, ENG.Activation)) as i:
                    body(i)
            split_hi.n = split_lo.n = 2 * (self.u0 + self.n)
            unit_done.n = self.u0 + self.n
            for j in range(2 if self.n > 1 else 1):
                if after is not None and j < after.n:
                    after.split(j, j)
                self.evacuate(self.n - (2 if self.n > 1 else 1) + j, j)
                mods(nb - 1, j)
            evac.n = CREDIT + self.u0 + self.n
            mod_done.n += nb * self.mod
            mod_kept.n = mod_done.n

        def first_splits(self):
            self.split(0, 0)
            if self.n > 1:
                self.split(1, 1)

    mod_raw = [sb(f"mod_raw{j}", [P, NC, P]) for j in range(2)]
    mod_sb = sb("mod_sb", [P, 2 * N_MOD * NC, 2])
    cond = sb("cond", [P, NC, 2])

    def mod_load(m, slot):
        wait(sp, mod_done, m - 1)
        sp.dma_start(mod_raw[slot][:], t["w_mod"][m]).then_inc(mod_loaded[slot].sem, 16)

    def mod_multiply(m, slot):
        wait(pe, mod_loaded[slot], (m - slot) * 8 + 16)
        wait(pe, mod_kept, m - 1)
        for k in range(NC):
            mm = pe.matmul(ps_s[:, 2 + slot, 0:2], mod_raw[slot][:, k, :], cond[:, k, :],
                           start=(k == 0), stop=(k == NC - 1))
        mm.then_inc(mod_done.sem, 1)

    def mod_keep(m, slot):
        wait(dve, mod_done, m + 1)
        a = vec_at["b_mod"]
        dve.tensor_tensor(mod_sb[:, m, :], ps_s[:, 2 + slot, 0:2],
                          vecs[:, a:a + 4 * N_MOD * NC].rearrange("p (m s) -> p m s", s=2)[:, m, :],
                          ALU.add).then_inc(mod_kept.sem, 1)

    def mean_square_rstd(src, T, n=NC, size=D, weights=None):
        first = p_.n
        for c in range(n):
            if c >= 2:
                wait(act, p_, first + c - 1)
            wait(pe, a_, A(act.activation(sq[:, c % 2, 0:T], src(c), ACT.Square)))
            PEs(pe.matmul(ps_s[:, 0, 0:T], ones, sq[:, c % 2, 0:T], start=(c == 0), stop=(c == n - 1)))
        finish_rstd(rstd[:, 0:T], ps_s[:, 0, 0:T], size)

    def finish_rstd(dst, psum, size):
        wait(dve, p_)
        wait(act, v_, V(dve.tensor_scalar(dst, psum, 1.0 / size, EPS, ALU.mult, ALU.add)))
        wait(dve, a_, A(act.activation(dst, dst, ACT.Sqrt)))
        wait(dve, v_, V(dve.reciprocal(dst, dst)))

    def norm_in(h_hi, h_lo, streams, scale, shift):
        T = S * streams
        wait(act, v_)
        mean_square_rstd(lambda c: x[:, c, 0:T], T)
        j = 0
        hist = []
        for c in range(NC):
            for s in range(streams):
                cols = slice(S * s, S * s + S)
                buf = sq[:, j % 4 // 2, S * (j % 2):S * (j % 2) + S]
                sc, sh = scale(c, s), shift(c, s)
                if j >= 4:
                    wait(dve, v_, hist[j - 4])
                else:
                    wait(dve, p_)
                wait(act, v_, V(dve.scalar_tensor_tensor(buf, x[:, c, cols], sc, rstd[:, cols],
                                                         ALU.mult, ALU.mult)))
                if sh is None:
                    made = A(act.activation(h_hi[:, c, cols], buf, ACT.Copy))
                    wait(dve, a_, made)
                    hist.append(V(dve.tensor_tensor(h_lo[:, c, cols], buf, h_hi[:, c, cols].bitcast(F32),
                                                    ALU.subtract)))
                else:
                    made = A(act.activation(h_hi[:, c, cols], buf, ACT.Identity, bias=sh))
                    wait(dve, a_, made)
                    hist.append(V(dve.scalar_tensor_tensor(h_lo[:, c, cols], buf, sh,
                                                           h_hi[:, c, cols].bitcast(F32),
                                                           ALU.add, ALU.subtract)))
                j += 1
        wait(pe, v_)

    def norm_out(streams, scale):
        T = S * streams
        wait(act, evac)
        wait(dve, evac)
        mean_square_rstd(lambda c: y[:, c, 0:T], T)
        hist = []
        j = 0
        for c in range(NC):
            for s in range(streams):
                cols = slice(S * s, S * s + S)
                buf = sq[:, j % 4 // 2, S * (j % 2):S * (j % 2) + S]
                if j >= 4:
                    wait(dve, v_, hist[j - 4])
                n = V(dve.scalar_tensor_tensor(buf, y[:, c, cols], scale(c, s), rstd[:, cols],
                                               ALU.mult, ALU.mult))
                wait(dve, v_, n)
                hist.append(V(dve.tensor_tensor(x[:, c, cols], x[:, c, cols], buf, ALU.add)))
                j += 1
        wait(dve, v_)

    PARTS = ((0, 0), (0, 1), (1, 0))

    def features(acts, kc, mt, T, k0=0):
        def unit(ul, slot):
            w = [w_[slot][:, 0:kc * mt * P].rearrange("p (k n) -> p k n", k=kc) for w_ in (w_hi, w_lo)]
            for m in range(mt):
                for k in range(kc):
                    for n, (wp, ap) in enumerate(PARTS):
                        mm = pe.matmul(ps_g[:, 2 * slot + m, 0:T], w[wp][:, k, m * P:(m + 1) * P],
                                       acts[ap][:, k0 + k, 0:T], start=(k == 0 and n == 0),
                                       stop=(k == kc - 1 and n == 2))
            return mm
        return unit

    def tokens(acts, n_tiles):
        def unit(ul, slot):
            w = [w_[slot][:, 0:UNIT].rearrange("p (k n) -> p k n", k=NC) for w_ in (w_hi, w_lo)]
            for i in range(n_tiles):
                for k in range(NC):
                    for n, (wp, ap) in enumerate(PARTS):
                        mm = pe.matmul(ps_g[:, 2 * slot + i // 2, S * (i % 2):S * (i % 2) + S],
                                       acts[ap][:, k, i * P:(i + 1) * P], w[wp][:, k, :],
                                       start=(k == 0 and n == 0), stop=(k == NC - 1 and n == 2))
            return mm
        return unit

    def gated_split(dst, T, func):
        base = [gate_made.n, out_lo.n, out_hi.n]

        def go(ul, slot):
            u = phase_u0(go) + ul
            wait(act, unit_done, u + 1)
            wait(act, evac, CREDIT + u - 1)
            act.activation(gate_tmp[:, slot, 0:T], ps_g[:, 2 * slot, 0:T], func).then_inc(gate_made.sem, 1)
            wait(dve, gate_made, base[0] + ul + 1)
            wait(dve, out_lo, base[1] + ul - 1)
            dve.tensor_tensor(prod[:, slot, 0:T], gate_tmp[:, slot, 0:T], ps_g[:, 2 * slot + 1, 0:T],
                              ALU.mult).then_inc(evac.sem, 1)
            wait(act, evac, CREDIT + u + 1)
            act.activation(dst[0][:, ul, 0:T], prod[:, slot, 0:T], ACT.Copy).then_inc(out_hi.sem, 1)
            wait(dve, out_hi, base[2] + ul + 1)
            dve.tensor_tensor(dst[1][:, ul, 0:T], prod[:, slot, 0:T], dst[0][:, ul, 0:T].bitcast(F32),
                              ALU.subtract).then_inc(out_lo.sem, 1)
        return go

    owners = {}

    def phase_u0(fn):
        return owners[fn].u0

    def phase(w, n, elems, pe_unit, evacuate, mod=0):
        ph = Phase(w, n, elems, pe_unit, evacuate, mod)
        owners[evacuate] = ph
        ph.load()
        return ph

    def keep(dst, T, mt=2, func=ACT.Copy, step=None):
        def go(ul, slot):
            u = phase_u0(go) + ul
            wait(act, unit_done, u + 1)
            act.activation(dst[:, bass.ds(ul * mt, mt), 0:T], ps_g[:, 2 * slot:2 * slot + mt, 0:T],
                           func).then_inc(evac.sem, 1)
        return go

    def add_to(dst, T, mt=1):
        def go(ul, slot):
            u = phase_u0(go) + ul
            wait(dve, unit_done, u + 1)
            d = dst[:, bass.ds(ul * mt, mt), 0:T]
            dve.tensor_tensor(d, d, ps_g[:, 2 * slot:2 * slot + mt, 0:T], ALU.add).then_inc(evac.sem, 1)
        return go

    def ffn(w_gu, w_down, acts, hid, streams, mods=(0, 0), norm=None, into=None, after=None):
        T = S * streams
        n0, n1 = FFN_HALVES
        dn0, dn1 = (t[w_down + "a"], t[w_down + "b"])
        g0 = gated_split(hid, T, ACT.Silu)
        ph = phase(t[w_gu], n0, UNIT, features(acts, NC, 2, T), g0, mods[0])
        ph.first_splits()
        if norm is not None:
            norm()
        d0 = phase(dn0, NC, n0 * P, features(hid, n0, 1, T),
                   keep(y, T, 1) if into is None else add_to(into, T, 1))
        ph.run(d0)
        gate_made.n += n0
        out_hi.n += n0
        out_lo.n += n0
        wait(pe, out_lo)
        g1 = gated_split(hid, T, ACT.Silu)
        ph1 = phase(t[w_gu][n0:n0 + n1], n1, UNIT, features(acts, NC, 2, T), g1, mods[1])
        d0.run(ph1)
        d1 = phase(dn1, NC, n1 * P, features(hid, n1, 1, T),
                   add_to(y if into is None else into, T, 1))
        ph1.run(d1)
        gate_made.n += n1
        out_hi.n += n1
        out_lo.n += n1
        wait(pe, out_lo)
        d1.run(None)

    def dump(ap):
        d = Count(nc, "dumped")
        for e in (v_, a_, evac, out_lo):
            wait(sp, e)
        d.inc(sp.dma_start(out, ap), 16)
        wait(sp, d)
        b1.close()
        mem.close()

    ab = sb("ab", [P, 3, NC, 2])
    b1 = ExitStack()
    h = [sb(f"h{j}", [P, NC, T2], F32R, b1) for j in range(2)]
    hid = [sb(f"hid{j}", [P, FFN_HALVES[0], T2], F32R, b1) for j in range(2)]
    wide = sb("wide", [P, NC, 2, S + 2], F32, b1)
    band = mod_raw[0][:].rearrange("p a b -> p (a b)").rearrange("p (q n) -> p q n", q=2)
    rope1 = mod_raw[1][:, 0:4, :].rearrange("p a b -> p (a b)").rearrange("p (q n) -> p q n", q=2)
    score_slots = [gate_tmp[:, 0, :], gate_tmp[:, 1, :], sq[:, 0, :]]

    wait(pe, a_, A(act.activation(cond[:], vec("cond", 0, 2 * NC).rearrange("p (k s) -> p k s", s=2), ACT.Silu)))
    n_first = 3 * NC
    mod_load(0, 0)
    mod_load(1, 1)
    with nc.Fori(1, n_first // 2, engines=(ENG.SP,)) as i:
        for j in range(2):
            mod_load(2 * i + j, j)
    mod_multiply(0, 0)
    mod_multiply(1, 1)
    with nc.Fori(1, n_first // 2, engines=(ENG.PE,)) as i:
        for j in range(2):
            mod_multiply(2 * i + j, j)
    with nc.Fori(0, n_first // 2, engines=(ENG.DVE,)) as i:
        for j in range(2):
            mod_keep(2 * i + j, j)
    for j in range(2):
        mod_loaded[j].n += 8 * n_first
    mod_done.n = mod_kept.n = n_first

    def mod_at(layer, k):
        a = (layer * N_MOD + k) * NC
        return mod_sb[:, a:a + NC, :]

    def g_at(layer, n):
        a = vec_at["norm_g"] + (layer * 6 + n) * 2 * NC
        return vecs[:, a:a + 2 * NC].rearrange("p (c s) -> p c s", s=2)

    def adaln(layer, k, n, weight, streams):
        def before():
            wait(dve, mod_kept)
            V(dve.scalar_tensor_tensor(ab[:, 0], mod_at(layer, k + 1), 1.0, g_at(layer, n), ALU.add, ALU.mult))
            V(dve.scalar_tensor_tensor(ab[:, 2], mod_at(layer, k + 2), weight, g_at(layer, n + 1),
                                       ALU.mult, ALU.mult))
            wait(dve, v_)
            norm_in(h[0], h[1], streams, lambda c, s: ab[:, 0, c, s:s + 1],
                    lambda c, s: mod_at(layer, k)[:, c, s:s + 1])

        def after(streams=streams):
            norm_out(streams, lambda c, s: ab[:, 2, c, s:s + 1])
        return before, after

    before, after = adaln(0, 0, 0, 0.5, 2)
    ffn("gu00", "dn00", h, hid, 2, (4, 4), before)
    after()
    if stop == 1:
        return dump(x[:, :, :])

    def conv_layer():
        before, after = adaln(0, 3, 2, 1.0, 2)
        gm0 = gate_made.n

        def product_wide(ul, slot):
            u = phase_u0(product_wide) + ul
            wait(act, unit_done, u + 1)
            wait(act, evac, CREDIT + u - 1)
            act.activation(gate_tmp[:, slot, :], ps_g[:, 2 * slot, :], ACT.Copy).then_inc(gate_made.sem, 1)
            wait(dve, gate_made, gm0 + ul + 1)
            dve.tensor_tensor(wide[:, ul, :, 1:S + 1],
                              gate_tmp[:, slot, :].rearrange("p (s n) -> p s n", s=2),
                              ps_g[:, 2 * slot + 1, :].rearrange("p (s n) -> p s n", s=2),
                              ALU.mult).then_inc(evac.sem, 1)
        c1 = phase(t["conv_cu"], NC, UNIT, features(h, NC, 2, T2), product_wide, 2)
        c1.first_splits()
        before()
        V(dve.memset(wide[:, :, :, 0:1], 0.0))
        V(dve.memset(wide[:, :, :, S + 1:S + 2], 0.0))
        base, base_hi = out_lo.n, out_hi.n

        def times_b(ul, slot):
            u = phase_u0(times_b) + ul
            wait(dve, unit_done, u + 1)
            wait(dve, out_lo, base + ul)
            dve.tensor_tensor(prod[:], y[:, bass.ds(2 * ul, 2), :], ps_g[:, 2 * slot:2 * slot + 2, :],
                              ALU.mult).then_inc(evac.sem, 1)
            wait(act, evac, CREDIT + u + 1)
            act.activation(hid[0][:, bass.ds(2 * ul, 2), :], prod[:], ACT.Copy).then_inc(out_hi.sem, 1)
            wait(dve, out_hi, base_hi + ul + 1)
            dve.tensor_tensor(hid[1][:, bass.ds(2 * ul, 2), :], prod[:],
                              hid[0][:, bass.ds(2 * ul, 2), :].bitcast(F32), ALU.subtract).then_inc(out_lo.sem, 1)
        c2 = phase(t["conv_b"], NC // 2, UNIT, features(h, NC, 2, T2), times_b)
        c1.run(c2)
        gate_made.n += NC
        wait(dve, evac)
        wait(dve, v_)
        for c in range(NC):
            yc = y[:, c, :].rearrange("p (s n) -> p s n", s=2)
            for tap in (1, 0, 2):
                src = wide[:, c, :, tap:tap + S]
                w_tap = vec("conv_w", tap * NC + c)
                if tap == 1:
                    V(dve.tensor_scalar(yc, src, w_tap, None, ALU.mult))
                else:
                    V(dve.scalar_tensor_tensor(yc, src, w_tap, yc, ALU.mult, ALU.add))
                wait(dve, v_)
        c3 = phase(t["conv_out"], NC // 2, UNIT, features(hid, NC, 2, T2), keep(y, T2))
        c2.run(c3)
        out_hi.n += NC // 2
        out_lo.n += NC // 2
        wait(pe, out_lo)
        wait(act, out_lo)
        c3.run(None)
        after()

    conv_layer()
    if stop == 2:
        return dump(x[:, :, :])
    before, after = adaln(0, 6, 4, 0.5, 2)
    ffn("gu01", "dn01", h, hid, 2, (4, 4), before)
    after()
    if stop == 3:
        return dump(x[:, :, :])

    before, after = adaln(1, 0, 0, 0.5, 2)
    ffn("gu10", "dn10", h, hid, 2, (4, 0), before)
    after()
    if stop == 4:
        return dump(x[:, :, :])

    sem_s = Count(nc, "item_scores")
    sem_m = Count(nc, "item_max")
    sem_e = Count(nc, "item_exp")
    sem_r = Count(nc, "item_normed")
    sem_t = Count(nc, "item_turned")
    sem_c = Count(nc, "item_copied")
    sem_o = Count(nc, "item_out")
    sem_k = Count(nc, "tile_kept")

    def attention(items, o_dst, scratch, probs):
        N = len(items)
        b_s, b_m, b_e, b_r, b_t, b_c, b_o, b_k = (c.n for c in (sem_s, sem_m, sem_e, sem_r, sem_t, sem_c, sem_o, sem_k))
        tiles_done = {}
        order = []
        for i, it in enumerate(items):
            if it["close"]:
                tiles_done[i] = len(order)
                order.append(it["tile"])

        def s_scores(i):
            it = items[i]
            if i >= 2:
                wait(pe, sem_m, b_m + i - 1)
            sem_s.inc(pe.matmul(ps_g[:, i % 2, 0:it["n"]], it["q"], it["k"], start=True, stop=True))

        def s_max(i):
            it = items[i]
            n = it["n"]
            wait(dve, sem_s, b_s + i + 1)
            if i >= 3:
                wait(dve, sem_t, b_t + i - 2)
            V(dve.tensor_tensor_reduce(scratch[i % 3][:, 0:n], ps_g[:, i % 2, 0:n], it["mask"], 1.0, -3.0e38,
                                       ALU.add, ALU.max, stats[:, 0, i:i + 1]))
            wait(dve, v_)
            if it["sink"] is None:
                sem_m.inc(dve.tensor_scalar(stats[:, 1, i:i + 1], stats[:, 0, i:i + 1], -0.125, None, ALU.mult))
            else:
                sem_m.inc(dve.tensor_scalar(stats[:, 1, i:i + 1], stats[:, 0, i:i + 1], -0.125,
                                            it["neg_sink"], ALU.mult, ALU.min))

        def s_exp(i):
            it = items[i]
            n = it["n"]
            wait(act, sem_m, b_m + i + 1)
            ins = act.activation(scratch[i % 3][:, 0:n], scratch[i % 3][:, 0:n], ACT.Exp,
                                 bias=stats[:, 1, i:i + 1], scale=0.125, accum_out=stats[:, 2, i:i + 1])
            if it["sink"] is not None:
                A(ins)
                ins = act.activation(stats[:, 3, i:i + 1], it["sink"], ACT.Exp, bias=stats[:, 1, i:i + 1])
            sem_e.inc(ins)

        def s_norm(i):
            it = items[i]
            n = it["n"]
            wait(dve, sem_e, b_e + i + 1)
            if it["sink"] is not None:
                V(dve.tensor_tensor(stats[:, 2, i:i + 1], stats[:, 2, i:i + 1], stats[:, 3, i:i + 1], ALU.add))
                wait(dve, v_)
            V(dve.reciprocal(stats[:, 4, i:i + 1], stats[:, 2, i:i + 1]))
            wait(dve, v_)
            p = scratch[i % 3][:, 0:n]
            if it["weight"] is None:
                sem_r.inc(dve.tensor_scalar(p, p, stats[:, 4, i:i + 1], None, ALU.mult))
            else:
                sem_r.inc(dve.tensor_scalar(p, p, stats[:, 4, i:i + 1], it["weight"], ALU.mult, ALU.mult))

        def s_turn(i):
            it = items[i]
            wait(pe, sem_r, b_r + i + 1)
            if i >= 2:
                wait(pe, sem_c, b_c + i - 1)
            k = 0
            while k * P < it["n"]:
                w = min(P, it["n"] - k * P)
                ins = pe.transpose(ps_g[0:w, 2 + i % 2, k * P:(k + 1) * P],
                                   scratch[i % 3][:, k * P:k * P + w], ident)
                k += 1
            sem_t.inc(ins)

        def s_copy(i):
            it = items[i]
            n = it["n"]
            w = min(P, n)
            m = -(-n // P) * P
            wait(act, sem_t, b_t + i + 1)
            if i >= 2:
                wait(act, sem_o, b_o + i - 1)
            sem_c.inc(act.activation(probs[0:w, i % 2, 0:m], ps_g[0:w, 2 + i % 2, 0:m], ACT.Copy))

        def s_out(i):
            it = items[i]
            n = it["n"]
            w = min(P, n)
            wait(pe, sem_c, b_c + i + 1)
            closed = [j for j in tiles_done if j < i]
            if it["open"] and len(closed) >= 2:
                wait(pe, sem_k, b_k + len(closed) - 1)
            bank = len(closed) % 2
            last = -(-n // P)
            for k in range(last):
                ins = pe.matmul(ps_s[it["half"] * HD:(it["half"] + 1) * HD, bank, it["qt"] * P:(it["qt"] + 1) * P],
                                it["v"](k), probs[0:w, i % 2, k * P:(k + 1) * P],
                                start=(it["first"] and k == 0), stop=(it["last"] and k == last - 1))
            sem_o.inc(ins)

        def s_keep(i):
            if i not in tiles_done:
                return
            n = tiles_done[i]
            tile = order[n]
            wait(act, sem_o, b_o + i + 1)
            A(act.activation(o_dst[0][:, tile, 0:S], ps_s[:, n % 2, 0:S], ACT.Copy))
            wait(dve, a_)
            sem_k.inc(dve.tensor_tensor(o_dst[1][:, tile, 0:S], ps_s[:, n % 2, 0:S],
                                        o_dst[0][:, tile, 0:S].bitcast(F32), ALU.subtract))

        for e in (v_, a_, evac):
            wait(pe, e)
        for e in (a_, evac):
            wait(dve, e)
        for e in (v_, p_):
            wait(act, e)
        for s in range(N + 6):
            for stage, lag in ((s_scores, 0), (s_max, 0), (s_exp, 0), (s_norm, 1), (s_turn, 2), (s_copy, 2),
                               (s_out, 3), (s_keep, 4)):
                if 0 <= s - lag < N:
                    stage(s - lag)
        wait(pe, sem_k)

    def attn_layer():
        before, after = adaln(1, 3, 2, 1.0, 2)
        wait(act, mod_done)
        for dst, src in ((band, t["band"]), (rope1, t["rope1"])):
            consts_in.inc(act.dma_start(dst, src), 16)
        wf = wide[:].rearrange("p a b c -> p (a b c)")
        k_raw = wf[:, 0:4 * S].rearrange("p (a n) -> p a n", a=2)
        v_tok = wf[:, 4 * S:8 * S].rearrange("p (a n) -> p a n", a=4)
        q_raw = wf[:, 8 * S:16 * S].rearrange("p (a n) -> p a n", a=8)
        yf = y[:].rearrange("p a b -> p (a b)")
        q = yf[:, 0:8 * S].rearrange("p (a n) -> p a n", a=8)
        k = yf[:, 8 * S:12 * S].rearrange("p (a n) -> p a n", a=2)
        m1 = yf[:, 12 * S:14 * S].rearrange("p (a n) -> p a n", a=2)

        k_unit, v_unit = features(h, NC, 2, T2), tokens(h, 4)

        def kv_keep(ul, slot):
            u = phase_u0(kv_keep) + ul
            wait(act, unit_done, u + 1)
            dst = (k_raw, v_tok.rearrange("p (a b) n -> p a (b n)", a=2))[slot]
            act.activation(dst, ps_g[:, 2 * slot:2 * slot + 2, :], ACT.Copy).then_inc(evac.sem, 1)
        kv = phase(t["attn_kv"], 2, UNIT, lambda ul, slot: (k_unit, v_unit)[slot](ul, slot), kv_keep)
        kv.first_splits()
        before()
        qp = phase(t["attn_q"], NC // 2, UNIT, features(h, NC, 2, S), keep(q_raw, S))
        kv.run(qp)
        wo = phase(t["attn_o"], NC // 2, UNIT, features(hid, NC, 2, S), keep(y, S))
        qp.run(wo)

        wait(pe, evac)
        wait(dve, evac)
        wait(dve, consts_in)
        cos = rope1[:, 0:1, :].to_broadcast([P, 2, S])
        sin = rope1[:, 1:2, :].to_broadcast([P, 2, S])
        for n in range(5):
            src, dst = (q_raw[:, 2 * n:2 * n + 2, :], q[:, 2 * n:2 * n + 2, :]) if n < 4 else \
                (k_raw[:, :, 0:S], k[:, :, 0:S])
            bank = ps_s[:, n % 2, :].rearrange("p (a n) -> p a n", a=2)
            if n >= 2:
                wait(pe, v_)
            wait(dve, p_, PEs(pe.matmul(bank, swap1, src, start=True, stop=True)))
            V(dve.tensor_tensor(dst, src, cos, ALU.mult))
            wait(dve, v_, V(dve.tensor_tensor(m1, bank, sin, ALU.mult)))
            wait(dve, v_, V(dve.tensor_tensor(dst, dst, m1, ALU.add)))
        V(dve.tensor_copy(k[:, :, S:T2], k_raw[:, :, S:T2]))

        items = []
        for tile in range(NC):
            for half in range(2):
                head = (tile // 4) * 8 + half * 4 + tile % 4
                kvh = head // 4
                for qt in range(2):
                    rows = slice(half * HD, (half + 1) * HD)
                    items.append(dict(
                        q=q[rows, tile, qt * P:(qt + 1) * P], k=k[rows, kvh // 2, :], n=T2, mask=band[:, qt, :],
                        sink=vec("sink", head), neg_sink=vec("neg_sink", head), weight=None,
                        v=lambda kt, kvh=kvh: v_tok[:, kt, kvh * HD:(kvh + 1) * HD],
                        tile=tile, half=half, qt=qt, first=True, last=True,
                        open=(half == 0 and qt == 0), close=(half == 1 and qt == 1)))
        assert len(items) <= 64
        V(dve.tensor_scalar(vec("neg_sink", 0, 16), vec("sink", 0, 16), -1.0, None, ALU.mult))
        attention(items, hid, score_slots, prod)
        wait(act, sem_k)
        wo.run(None)
        after(1)

    attn_layer()
    if stop == 5:
        return dump(x[:, :, :])
    before, after = adaln(1, 6, 4, 0.5, 1)
    ffn("gu11", "dn11", h, hid, 1, (0, 0), before)
    after()
    if stop == 6:
        return dump(x[:, :, :])

    for e in (v_, a_, evac):
        wait(act, e)
    b1.close()
    b2 = ExitStack()
    h = [sb(f"b2_h{j}", [P, NC, S], F32R, b2) for j in range(2)]
    hid = [sb(f"b2_hid{j}", [P, FFN_HALVES[0], S], F32R, b2) for j in range(2)]
    qk = sb("qk", [P, 18, S], F32, b2)
    gates = sb("gates", [P, 2 * NC, S], F32, b2)
    v_tok = sb("v_tok", [P, 2, 3 * S], F32, b2)
    flat = sb("flat", [P, 2, 16, 2, 15], F32, b2)
    rope2 = sb("rope2", [P, 2, S], F32, b2)
    causal = sb("causal", [P, S + 30], F32, b2)
    gn = [sb(f"gn{j}", [P, NC * 24], F32R, b2) for j in range(2)]
    small = sb("small", [P, 320], F32, b2)
    branch = small[:, 0:48].rearrange("p (q n) -> p q n", q=2)
    hid_c = small[:, 48:168].rearrange("p (k m n) -> p k m n", k=2, m=2)
    kc = small[:, 168:183]
    kc_tmp = small[:, 184:199]
    yt = y[:].rearrange("p a b -> p (a b)").rearrange("p (a n) -> p a n", n=S)

    loads2 = [
        (x[:, :, S:T2], t["cw1"][0].rearrange("p (k n) -> p k n", k=8)),
        (mod_raw[0][:].rearrange("p a b -> p (a b)"), t["cw1"][1][:, 0:1024]),
        (mod_raw[1][:].rearrange("p a b -> p (a b)"), t["cw1"][1][:, 1024:2048]),
        (y[:, 0:4, :].rearrange("p a b -> p (a b)"), t["cw1"][2]),
        (y[:, 4:8, :].rearrange("p a b -> p (a b)"), t["cw1"][3]),
        (causal[:], t["causal"]),
        (prod[:, 0, 0:NC * 24], t["gate_n"]),
        (prod[:, 1, 0:S].bitcast(I32), t["positions"].partition_broadcast(P)),
    ]
    for dst, src in loads2:
        consts_in.inc(act.dma_start(dst, src), 16)

    def compress_w(kv, jp, m):
        cols = slice(m * P, (m + 1) * P)
        if kv == 1:
            return yt[:, jp, cols]
        if jp < 8:
            return x[:, jp, S + m * P:S + (m + 1) * P]
        return mod_raw[(jp - 8) // 4][:, 2 * (jp % 4) + m, :]

    def norm2(name):
        norm_in(h[0], h[1], 1, lambda c, s: vec(name, c), lambda c, s: None)

    feat = features(h, NC, 2, S)
    tok2 = tokens(h, 2)

    def tok_keep(col):
        def go(ul, slot):
            u = phase_u0(go) + ul
            wait(act, unit_done, u + 1)
            c = col(ul)
            act.activation(v_tok[:, :, c:c + S], ps_g[:, 2 * slot, :].rearrange("p (a n) -> p a n", a=2),
                           ACT.Copy).then_inc(evac.sem, 1)
        return go

    qk_keep = keep(qk, S)
    ph_a = phase(t["w_in_a"], 8, UNIT, feat, qk_keep)
    ph_a.first_splits()
    norm2("g_mix")

    vs_keep = tok_keep(lambda ul: 0)

    def b_keep(ul, slot):
        if slot == 0:
            u = phase_u0(b_keep) + ul
            wait(act, unit_done, u + 1)
            act.activation(qk[:, 16:18, :], ps_g[:, 0:2, 0:S], ACT.Copy).then_inc(evac.sem, 1)
        else:
            owners[vs_keep] = owners[b_keep]
            vs_keep(ul, slot)
    ph_b = phase(t["w_in_b"], 2, UNIT, lambda ul, slot: (feat, tok2)[slot](ul, slot), b_keep)
    ph_a.run(ph_b)
    ph_c = phase(t["w_in_c"], 2, UNIT, tok2, tok_keep(lambda ul: S + ul * S))
    ph_b.run(ph_c)
    ph_d = phase(t["w_in_d"], 8, UNIT, feat, keep(gates, S, 2, ACT.Sigmoid))
    ph_c.run(ph_d)

    wait(act, consts_in)
    wait(dve, a_, A(act.activation(gn[0][:], prod[:, 0, 0:NC * 24], ACT.Copy)))
    wait(pe, v_, V(dve.tensor_tensor(gn[1][:], prod[:, 0, 0:NC * 24], gn[0][:].bitcast(F32), ALU.subtract)))
    for qt in range(2):
        for k in range(NC):
            for n, (wp, ap) in enumerate(PARTS):
                mm = pe.matmul(ps_s[:, 2 + qt, 0:24], h[ap][:, k, qt * P:(qt + 1) * P],
                               gn[wp][:, k * 24:(k + 1) * 24], start=(k == 0 and n == 0),
                               stop=(k == NC - 1 and n == 2))
    PEs(mm)

    def up_unit(ul, slot):
        w = [w_[slot][:].rearrange("p (k n) -> p k n", k=NC) for w_ in (w_hi, w_lo)]
        for m in range(2):
            for src in range(2):
                for k in range(4):
                    for n, (wp, ap) in enumerate(PARTS):
                        mm = pe.matmul(ps_g[:, 2 * slot + m, src * S:(src + 1) * S],
                                       w[wp][:, 4 * src + k, m * P:(m + 1) * P], hid[ap][:, 4 * src + k, 0:S],
                                       start=(k == 0 and n == 0), stop=(k == 3 and n == 2))
        return mm

    merge = Count(nc, "merge")
    merge.inc(dve.memset(small[:, 319:320], 0.0))

    def merge_keep(ul, slot):
        u = phase_u0(merge_keep) + ul
        pa, pb, pc = (prod[:, 0, :].rearrange("p (m n) -> p m n", m=2), prod[:, 1, :].rearrange("p (m n) -> p m n", m=2),
                      gate_tmp[:, 0, :].rearrange("p (m n) -> p m n", m=2))
        wait(dve, unit_done, u + 1)
        wait(dve, merge, 3 * ul + 1)
        dve.tensor_tensor(pa, gates[:, bass.ds(2 * ul, 2), :], ps_g[:, 2 * slot:2 * slot + 2, 0:S],
                          ALU.mult).then_inc(merge.sem, 1)
        dve.tensor_tensor(pb, gates[:, bass.ds(2 * ul + NC, 2), :], ps_g[:, 2 * slot:2 * slot + 2, S:T2],
                          ALU.mult).then_inc(evac.sem, 1)
        wait(dve, merge, 3 * ul + 2)
        wait(dve, evac, CREDIT + u + 1)
        dve.tensor_tensor(pc, pa, pb, ALU.add).then_inc(merge.sem, 1)
        wait(act, merge, 3 * ul + 3)
        act.activation(h[0][:, bass.ds(2 * ul, 2), :], pc, ACT.Copy).then_inc(out_hi.sem, 1)
        wait(dve, out_hi, hi0 + ul + 1)
        dve.tensor_tensor(h[1][:, bass.ds(2 * ul, 2), :], pc, h[0][:, bass.ds(2 * ul, 2), :].bitcast(F32),
                          ALU.subtract).then_inc(merge.sem, 1)
    hi0 = out_hi.n
    ph_up = phase(t["w_up"], 4, UNIT, up_unit, merge_keep)
    ph_d.run(ph_up)

    wait(act, p_)
    wait(dve, a_, A(act.activation(branch, ps_s[:, 2:4, 0:24], ACT.Sigmoid)))
    comp = branch.rearrange("p q (h b) -> p q h b", b=3)
    V(dve.tensor_scalar(comp[:, 0, :, 0], comp[:, 0, :, 0], vec("any_block"), None, ALU.mult))

    wait(dve, consts_in)
    wait(dve, evac)
    pos_f, turns, kf, ang = (sq[:, 0, 0:S], sq[:, 0, S:T2], sq[:, 1, 0:S], sq[:, 1, S:T2])
    k_int = prod[:, 1, S:T2].bitcast(I32)

    def step(ins):
        V(ins)
        wait(dve, v_)
    step(dve.tensor_copy(pos_f, prod[:, 1, 0:S].bitcast(I32)))
    step(dve.tensor_scalar(ang, pos_f, vec("inv_freq"), None, ALU.mult))
    for n, (quarter_turn, shift) in enumerate(((0.25, 1.5707963267948966), (0.0, 0.0))):
        r = rope2[:, n, :]
        step(dve.tensor_scalar(turns, ang, 0.15915494309189535, quarter_turn, ALU.mult, ALU.add))
        step(dve.tensor_copy(k_int, turns))
        step(dve.tensor_copy(kf, k_int))
        step(dve.scalar_tensor_tensor(r, kf, -TWO_PI_HI, ang, ALU.mult, ALU.add))
        step(dve.scalar_tensor_tensor(r, kf, -TWO_PI_MID, r, ALU.mult, ALU.add))
        step(dve.scalar_tensor_tensor(r, kf, -TWO_PI_LO, r, ALU.mult, ALU.add))
        step(dve.tensor_scalar(r, r, shift, PI_SAFE, ALU.add, ALU.min))
        step(dve.tensor_scalar(r, r, -PI_SAFE, None, ALU.max))
    wait(act, v_)
    A(act.activation(rope2[:], rope2[:], ACT.Sin))

    for kv in range(2):
        pe_col = vec("pe_k" if kv == 0 else "pe_v", 0, 16)
        for g in range(2):
            for odd in range(2):
                rows = slice(odd * HD, (odd + 1) * HD)
                by16 = qk[rows, 14 + 2 * kv + g, :].rearrange("p (c j) -> p j c", j=16)
                for late in range(2):
                    V(dve.tensor_tensor(flat[rows, kv, 8 * late:8 * late + 8, g, :],
                                        by16[:, odd:16:2, late:late + 15],
                                        pe_col[rows, 8 * late:8 * late + 8].unsqueeze(2).to_broadcast([HD, 8, 15]),
                                        ALU.add))
    wait(pe, v_)
    wait(pe, consts_in)
    for kv in range(2):
        for m in range(2):
            for jp in range(16):
                mm = pe.matmul(ps_s[:, kv, m * 32:m * 32 + 30], compress_w(kv, jp, m),
                               flat[:, kv, jp, :, :].rearrange("p g c -> p (g c)"),
                               start=(jp == 0), stop=(jp == 15))
        PEs(mm)
        wait(act, p_)
        A(act.activation(hid_c[:, kv, :, :], ps_s[:, kv, 0:64].rearrange("p (m n) -> p m n", m=2)[:, :, 0:30], ACT.Silu))
    wait(pe, a_)
    for g in range(2):
        for m in range(2):
            mm = pe.matmul(ps_s[g * HD:(g + 1) * HD, 2, 0:15], vec("cw2_k", m * HD, HD),
                           hid_c[:, 0, m, g * 15:g * 15 + 15], start=(m == 0), stop=(m == 1))
    PEs(mm)
    for g in range(2):
        for m in range(2):
            mm = pe.matmul(ps_s[0:15, 3, g * HD:(g + 1) * HD], hid_c[:, 1, m, g * 15:g * 15 + 15],
                           vec("cw2_v", m * HD, HD), start=(m == 0), stop=(m == 1))
    PEs(mm)
    v_cmp = flat[0:15, 1, 0:5, :, :].rearrange("p a b c -> p (a b c)")[:, 0:2 * HD]
    wait(act, p_)
    wait(dve, a_, A(act.activation(kc, ps_s[:, 2, 0:15], ACT.Copy)))
    A(act.activation(v_cmp, ps_s[0:15, 3, 0:2 * HD], ACT.Copy))

    NT = 14
    for e in (p_, v_, a_, evac):
        wait(act, e)
    A(act.activation(yt[:, 0:NT, :], qk[:, 0:NT, :], ACT.Square))
    A(act.activation(kc_tmp, kc, ACT.Square))
    wait(pe, a_)
    banks = [ps_g[:, j, :] for j in range(4)] + [ps_s[:, j, :] for j in range(4)]
    for j in range(NT // 2):
        PEs(pe.matmul(banks[j], head_ones, yt[:, 2 * j:2 * j + 2, :], start=True, stop=True))
    PEs(pe.matmul(banks[7][:, 0:15], head_ones, kc_tmp, start=True, stop=True))
    wait(dve, p_)
    for j in range(NT // 2):
        V(dve.tensor_scalar(yt[:, 2 * j:2 * j + 2, :].rearrange("p a n -> p (a n)"), banks[j], 1.0 / HD, EPS,
                            ALU.mult, ALU.add))
    V(dve.tensor_scalar(kc_tmp, banks[7][:, 0:15], 1.0 / HD, EPS, ALU.mult, ALU.add))
    wait(act, v_)
    A(act.activation(yt[:, 0:NT, :], yt[:, 0:NT, :], ACT.Sqrt))
    A(act.activation(kc_tmp, kc_tmp, ACT.Sqrt))
    wait(dve, a_)
    V(dve.reciprocal(yt[:, 0:NT, :], yt[:, 0:NT, :]))
    V(dve.reciprocal(kc_tmp, kc_tmp))
    wait(dve, v_)
    for j in range(NT):
        V(dve.scalar_tensor_tensor(qk[:, j, :], qk[:, j, :], vec("qk_gain", j), yt[:, j, :], ALU.mult, ALU.mult))
    V(dve.scalar_tensor_tensor(kc, kc, vec("kc_gain"), kc_tmp, ALU.mult, ALU.mult))
    wait(pe, v_)
    for j in range(NT // 2):
        PEs(pe.matmul(banks[j], swap2[:], qk[:, 2 * j:2 * j + 2, :], start=True, stop=True))
    PEs(pe.matmul(banks[7][:, 0:15], swap2[:], kc, start=True, stop=True))
    wait(dve, p_)
    wait(dve, v_)
    cos2, sin2 = rope2[:, 0:1, :], rope2[:, 1:2, :]
    for j in range(NT // 2):
        V(dve.tensor_tensor(yt[:, 2 * j:2 * j + 2, :], banks[j].rearrange("p (a n) -> p a n", a=2),
                            sin2.to_broadcast([P, 2, S]), ALU.mult))
    V(dve.tensor_tensor(qk[:, 0:NT, :], qk[:, 0:NT, :], cos2.to_broadcast([P, NT, S]), ALU.mult))
    ends = slice(31, S, 16)
    V(dve.tensor_tensor(kc_tmp, banks[7][:, 0:15], rope2[:, 1, ends], ALU.mult))
    V(dve.tensor_tensor(kc, kc, rope2[:, 0, ends], ALU.mult))
    wait(dve, v_)
    V(dve.tensor_tensor(qk[:, 0:NT, :], qk[:, 0:NT, :], yt[:, 0:NT, :], ALU.add))
    V(dve.tensor_tensor(kc, kc, kc_tmp, ALU.add))
    wait(dve, v_)

    items = []
    no_sink = dict(sink=None, neg_sink=None)
    for tile in range(4):
        for half in range(2):
            head = half * 4 + tile
            rows = slice(half * HD, (half + 1) * HD)
            for qt in range(2):
                n = (qt + 1) * P
                common = dict(q=qk[rows, tile, qt * P:(qt + 1) * P], tile=tile, half=half, qt=qt, **no_sink)
                wgt = [branch[:, qt, 3 * head + b:3 * head + b + 1] for b in range(3)]
                items.append(dict(common, k=kc[rows, :], n=15, mask=causal[:, S + 15 * qt:S + 15 * qt + 15],
                                  weight=wgt[0], v=lambda kt, half=half: v_cmp[:, half * HD:(half + 1) * HD],
                                  first=True, last=False, open=(half == 0 and qt == 0), close=False))
                for b, (kt_, vc_) in enumerate(((12, 0), (13, P))):
                    items.append(dict(common, k=qk[rows, kt_, 0:n], n=n, mask=causal[:, S - n:S], weight=wgt[1 + b],
                                      v=lambda kt, c=vc_ + half * HD: v_tok[:, kt, c:c + HD],
                                      first=False, last=(b == 1), open=False,
                                      close=(b == 1 and half == 1 and qt == 1)))
    for j in range(4):
        for half in range(2):
            rows = slice(half * HD, (half + 1) * HD)
            for qt in range(2):
                n = (qt + 1) * P
                items.append(dict(q=qk[rows, 4 + j, qt * P:(qt + 1) * P], tile=4 + j, half=half, qt=qt,
                                  k=qk[rows, 8 + j, 0:n], n=n, mask=causal[:, S - n:S], weight=None, **no_sink,
                                  v=lambda kt, c=S + (2 * j + half) * HD: v_tok[:, kt, c:c + HD],
                                  first=True, last=True, open=(half == 0 and qt == 0),
                                  close=(half == 1 and qt == 1)))
    attention(items, hid, score_slots, prod)
    wait(act, sem_k)
    wait(dve, sem_c)
    wait(dve, sem_o)
    wait(dve, sem_t)

    ph_o = phase(t["w_out"], 4, UNIT, features(h, NC, 2, S), add_to(x, S, 2))
    ph_up.run(ph_o)
    merge.n += 12
    out_hi.n += 4
    wait(pe, merge)
    ph_o.run(None)
    wait(dve, evac)
    wait(act, evac)
    ffn("gu2", "dn2", h, hid, 1, (0, 0), lambda: norm2("g_ffn"), into=x)
    wait(dve, evac)
    wait(act, evac)

    ph_g = phase(t["ple_gate"], 4, UNIT, feat, keep(gates, S, 2, ACT.Sigmoid))
    ph_g.first_splits()
    wait(act, out_lo)
    consts_in.inc(act.dma_start(prod[:, 0, :].rearrange("p (a n) -> p a n", a=2), t["p"]), 16)
    norm2("g_ple")
    wait(act, consts_in)
    wait(dve, consts_in)
    pr = prod[:, 0, :].rearrange("p (a n) -> p a n", a=2)
    wait(dve, a_, A(act.activation(hid[0][:, 0:2, :], pr, ACT.Copy)))
    V(dve.tensor_tensor(hid[1][:, 0:2, :], pr, hid[0][:, 0:2, :].bitcast(F32), ALU.subtract))

    def proj_unit(ul, slot):
        w = [w_[slot][:].rearrange("p (k n) -> p k n", k=2) for w_ in (w_hi, w_lo)]
        for m in range(NC):
            for k in range(2):
                for n, (wp, ap) in enumerate(PARTS):
                    mm = pe.matmul(ps_g[:, m // 2, S * (m % 2):S * (m % 2) + S], w[wp][:, k, m * P:(m + 1) * P],
                                   hid[ap][:, k, 0:S], start=(k == 0 and n == 0), stop=(k == 1 and n == 2))
        return mm

    def proj_keep(ul, slot):
        u = phase_u0(proj_keep) + ul
        wait(dve, unit_done, u + 1)
        dve.tensor_tensor(yt[:, 0:NC, :], gates[:, 0:NC, :], ps_g[:, :, :].rearrange("p a (b n) -> p (a b) n", b=2),
                          ALU.mult).then_inc(evac.sem, 1)
    ph_p = phase(t["ple_proj"], 1, UNIT, proj_unit, proj_keep)
    ph_g.run(ph_p)
    wait(pe, evac)
    wait(pe, v_)
    wait(dve, evac)
    ph_p.run(None)
    wait(dve, evac)
    V(dve.tensor_tensor(x[:, :, 0:S], x[:, :, 0:S], yt[:, 0:NC, :], ALU.add))
    wait(sp, v_)
    stored = Count(nc, "stored")
    stored.inc(sp.dma_start(out, x[:, :, 0:S]), 16)
    wait(sp, stored)
    b2.close()
    mem.close()


def _units(w, kc, cols):
    import numpy as np
    K, N = w.shape
    assert K == kc * P and N % cols == 0
    return np.ascontiguousarray(w.reshape(kc, P, N // cols, cols).transpose(2, 1, 0, 3)
                                .reshape(N // cols, P, kc * cols))


def _chunked(v):
    return v.reshape(-1, P).T


def _fmajor(a):
    return a.T.reshape(-1, P, a.shape[0]).transpose(1, 0, 2)


def _paired(a, b):
    import numpy as np
    K = a.shape[0]
    return np.stack([a.reshape(K, -1, P), b.reshape(K, -1, P)], axis=2).reshape(K, -1)


def layout(i):
    import numpy as np
    f32 = np.float32
    t, cols, vec_at = {}, [], {}

    def add(name, a):
        vec_at[name] = sum(c.shape[1] for c in cols)
        cols.append(np.asarray(a, f32).reshape(P, -1))

    add("cond", np.stack([_chunked(i["c"][0]), _chunked(i["c_ctx"])], axis=2))
    add("b_mod", np.repeat(_chunked(i["b_mod"].reshape(-1))[:, :, None], 2, axis=2))
    add("norm_g", np.repeat(_chunked(i["norm_g"].reshape(-1))[:, :, None], 2, axis=2))
    add("conv_w", _chunked(i["conv_w"].reshape(-1)))
    add("sink", np.broadcast_to(i["attn_sink"].reshape(1, -1), (P, 16)))
    add("neg_sink", np.zeros((P, 16)))
    for name in ("g_mix", "g_ffn", "g_ple"):
        add(name, _chunked(i[name + "_2"][0]))
    two = lambda a: np.tile(a, 2)
    gains = [i["nsa_q_gain_2"][0]] * 4 + [i["moba_q_gain_2"][0]] * 4 + [i["moba_k_gain_2"][0]] * 4 \
        + [i["nsa_ks_gain_2"][0], i["nsa_kw_gain_2"][0]]
    add("qk_gain", np.stack([two(a) for a in gains], axis=1))
    add("kc_gain", two(i["nsa_kc_gain_2"][0]))
    for name in ("pe_k", "pe_v"):
        add(name, i[f"nsa_{name}_2"][0].reshape(16, P).T)
    for name in ("cw2_k", "cw2_v"):
        w2 = i["nsa_ck_w2_2" if name == "cw2_k" else "nsa_cv_w2_2"][0]
        add(name, w2.reshape(2, P, HD).transpose(1, 0, 2))
    f2 = (np.float32(500000.0) ** (-np.arange(8, dtype=f32) / np.float32(8))).astype(f32)
    add("inv_freq", np.tile(np.concatenate([f2, f2, np.zeros(HD - 16, f32)]), 2))
    add("any_block", (np.arange(P) >= 31).astype(f32))
    t["vecs"] = np.ascontiguousarray(np.concatenate(cols, axis=1))

    eye = np.eye(P, dtype=f32)
    head_ones = np.kron(np.eye(2), np.ones((HD, HD))).astype(f32)
    quarter = HD // 4

    def swap(pairs):
        m = np.zeros((P, P), f32)
        for base in (0, HD):
            for lo, hi in pairs:
                m[base + hi, base + lo] = -1.0
                m[base + lo, base + hi] = 1.0
        return m
    swap1 = swap([(b + j, b + quarter + j) for b in (0, 2 * quarter) for j in range(quarter)])
    t["mats"] = np.ascontiguousarray(np.stack([eye, np.ones((P, P), f32), head_ones, swap1], axis=1))
    t["swap2"] = swap([(j, 8 + j) for j in range(8)])
    tok = np.arange(S)
    inv = (np.float32(10000.0) ** (-np.arange(quarter, dtype=f32) / np.float32(quarter))).astype(f32)
    ang = np.stack([(tok // 64).astype(f32)[:, None] * inv, (tok % 64).astype(f32)[:, None] * inv], axis=1)
    ang = np.repeat(ang[:, :, None, :], 2, axis=2).reshape(S, HD)
    t["rope1"] = np.ascontiguousarray(np.stack([np.tile(np.cos(ang).T, (2, 1)), np.tile(np.sin(ang).T, (2, 1))], axis=1)).astype(f32)
    band = np.zeros((P, 2, T2), f32)
    for qt in range(2):
        off = np.abs(np.arange(S)[None, :] - (qt * P + np.arange(P))[:, None])
        band[:, qt, 0:S] = np.where(off <= 128, 0.0, NEG)
    t["band"] = band

    t["x"] = np.ascontiguousarray(_fmajor(i["x"][0]))
    t["ctx"] = np.ascontiguousarray(_fmajor(i["ctx"][0]))

    t["w_mod"] = np.concatenate([_units(i["w_mod"][l], NC, P) for l in range(2)]).reshape(-1, P, NC, P)
    n0, n1 = FFN_HALVES
    for l in range(2):
        for j in range(2):
            gu, dn = i["ffn_w_gu"][l, j], i["ffn_w_down"][l, j]
            t[f"gu{l}{j}"] = _units(_paired(gu[:, :D_FF], gu[:, D_FF:]), NC, 2 * P)
            t[f"dn{l}{j}a"] = _units(dn[:n0 * P], n0, P)
            t[f"dn{l}{j}b"] = _units(dn[n0 * P:], n1, P)
    cw = i["conv_w_in"][0]
    t["conv_cu"] = _units(_paired(cw[:, D:2 * D], cw[:, 2 * D:]), NC, 2 * P)
    t["conv_b"] = _units(cw[:, :D], NC, 2 * P)
    t["conv_out"] = _units(i["conv_w_out"][0], NC, 2 * P)
    wq = i["attn_w_qkv"][0]
    heads = [(tile // 4) * 8 + half * 4 + tile % 4 for tile in range(8) for half in range(2)]
    t["attn_q"] = _units(wq[:, :D].reshape(D, 16, HD)[:, heads].reshape(D, D), NC, 2 * P)
    t["attn_kv"] = _units(wq[:, D:], NC, 2 * P)
    t["attn_o"] = _units(i["attn_w_o"][0].reshape(16, HD, D)[heads].reshape(D, D), NC, 2 * P)

    tri = np.where(np.arange(P)[None, :] <= np.arange(P)[:, None], 0.0, NEG)
    blocks = [np.where(16 * np.arange(15)[None, :] + 31 <= (qt * P + np.arange(P))[:, None], 0.0, NEG) for qt in range(2)]
    t["causal"] = np.concatenate([np.zeros((P, P)), tri] + blocks, axis=1).astype(f32)
    t["positions"] = np.ascontiguousarray(i["positions_2"][0])
    t["p"] = np.ascontiguousarray(_fmajor(i["p_2"][0, 0]))
    w = i["w_in_2"][0]
    cuts = np.cumsum([0, 512] + [128] * 6 + [24] + [512] * 3 + [D, D])
    q_n, kc_, vc_, ks_, vs_, kw_, vw_, g_n, q_m, k_m, v_m, g_a, g_b = (w[:, a:b] for a, b in zip(cuts[:-1], cuts[1:]))
    order = [half * 4 + tile for tile in range(4) for half in range(2)]
    twice = lambda a: [a[:, 0:HD], a[:, 0:HD], a[:, HD:P], a[:, HD:P]]
    cat = lambda parts: np.concatenate(parts, axis=1)
    t["w_in_a"] = _units(cat([q_n.reshape(D, 8, HD)[:, order].reshape(D, 512), q_m, k_m, ks_, kw_] + twice(kc_)), NC, 2 * P)
    t["w_in_b"] = _units(cat(twice(vc_) + [vs_, vw_]), NC, 2 * P)
    t["w_in_c"] = _units(v_m, NC, 2 * P)
    t["w_in_d"] = _units(cat([g_a, g_b]), NC, 2 * P)
    t["gate_n"] = _units(g_n, NC, 24)[0]
    t["cw1"] = np.concatenate([_units(i[n][0][a:a + D], NC, 2 * P) for n in ("nsa_ck_w1_2", "nsa_cv_w1_2") for a in (0, D)])
    up_n = i["w_up_nsa_2"][0].reshape(8, HD, D)[order].reshape(512, D)
    t["w_up"] = _units(np.concatenate([up_n, i["w_up_moba_2"][0]]), NC, 2 * P)
    t["w_out"] = _units(i["w_out_2"][0], NC, 2 * P)
    gu, dn = i["w_ffn_in_2"][0], i["w_ffn_out_2"][0]
    t["gu2"] = _units(_paired(gu[:, :D_FF], gu[:, D_FF:]), NC, 2 * P)
    t["dn2a"], t["dn2b"] = _units(dn[:n0 * P], n0, P), _units(dn[n0 * P:], n1, P)
    t["ple_gate"] = _units(i["w_ple_gate_2"][0], NC, 2 * P)
    t["ple_proj"] = _units(i["w_ple_proj_2"][0], 2, D)
    return t, vec_at


def kernel(**inputs):
    import numpy as np
    import concourse.bacc as bacc
    from concourse.bass_utils import run_bass_kernel_spmd

    arrays, vec_at = layout({k: np.asarray(v) for k, v in inputs.items()})
    nc = bacc.Bacc("TRN2", target_bir_lowering=False, num_devices=1)
    t = {n: nc.dram_tensor(f"in_{n}", a.shape, mybir.dt.from_np(a.dtype), kind="ExternalInput").ap()
         for n, a in arrays.items()}
    out = nc.dram_tensor("out", (P, NC, S), F32, kind="ExternalOutput").ap()
    build(nc, t, out, vec_at)
    r = run_bass_kernel_spmd(nc, [{f"in_{n}": a for n, a in arrays.items()}], core_ids=[0])
    return r.results[0]["out"].transpose(2, 1, 0).reshape(1, S, D)
```

```python
from contextlib import ExitStack

import concourse.bass as bass
from concourse import mybir

F32 = mybir.dt.float32
F32R = mybir.dt.float32r
I32 = mybir.dt.int32
ALU = mybir.AluOpType
ACT = mybir.ActivationFunctionType
ENG = mybir.EngineType

P = 128
D = 1024
NC = D // P
S = 256
T2 = 2 * S
D_FF = 2816
FFN_HALVES = (12, 10)
assert sum(FFN_HALVES) * P == D_FF
N_MOD = 9
HD = 64
EPS = 1e-6
CREDIT = 2
UNIT = 2048
NEG = -1e30
TWO_PI_HI = 6.28125
TWO_PI_MID = 0.0019350051879882812
TWO_PI_LO = 3.019916050561733e-07
PI_SAFE = 3.1415925


class Count:

    def __init__(self, nc, name):
        self.sem = nc.alloc_semaphore(name)
        self.n = 0

    def inc(self, ins, by=1):
        ins.then_inc(self.sem, by)
        self.n += by
        return self.n


def wait(eng, count, value=None):
    value = count.n if value is None else value
    if not isinstance(value, int) or value > 0:
        eng.wait_ge(count.sem, value)


def build(nc, t, out, vec_at):
    pe, dve, act, sp, pool = nc.tensor, nc.vector, nc.scalar, nc.sync, nc.gpsimd
    mem = ExitStack()

    def sb(name, shape, dt=F32, stack=None):
        return (stack or mem).enter_context(nc.sbuf_tensor(name, list(shape), dt))

    n_vec = t["vecs"].shape[1]
    vecs = sb("vecs", [P, n_vec])
    mats = sb("mats", [P, 4, P])
    swap2 = sb("swap2", [P, P])
    ident, ones, head_ones, swap1 = (mats[:, j, :] for j in range(4))
    w_raw = [sb(f"w_raw{j}", [P, UNIT]) for j in range(2)]
    w_hi = [sb(f"w_hi{j}", [P, UNIT], F32R) for j in range(2)]
    w_lo = [sb(f"w_lo{j}", [P, UNIT], F32R) for j in range(2)]
    x = sb("x", [P, NC, T2])
    gate_tmp = sb("gate_tmp", [P, 2, T2])
    prod = sb("prod", [P, 2, T2])
    sq = sb("sq", [P, 2, T2])
    ssum = sb("ssum", [P, T2])
    tok = sb("tok", [P, 9])
    mod_acc = sb("mod_acc", [P, 2, 2, P])
    stats = mod_acc[:].rearrange("p a b n -> p (a b n)")[:, 0:5 * 64].rearrange("p (a n) -> p a n", n=64)
    y = sb("y", [P, NC, T2])
    ps_g = mem.enter_context(nc.psum_tensor("ps_g", [P, 4, 512], F32))
    ps_s = mem.enter_context(nc.psum_tensor("ps_s", [P, 4, 512], F32))

    def vec(name, j=0, n=1):
        a = vec_at[name] + j
        return vecs[:, a:a + n]

    loaded = [Count(nc, f"loaded{j}") for j in range(2)]
    split_hi = Count(nc, "split_hi")
    split_lo = Count(nc, "split_lo")
    unit_done = Count(nc, "unit_done")
    evac = Count(nc, "evac")
    gate_made = Count(nc, "gate_made")
    out_hi = Count(nc, "out_hi")
    out_lo = Count(nc, "out_lo")
    consts_in = Count(nc, "consts_in")
    v_ = Count(nc, "vector_steps")
    a_ = Count(nc, "scalar_steps")
    p_ = Count(nc, "tensor_steps")
    g_ = Count(nc, "pool_steps")
    mod_loaded = [Count(nc, f"mod_loaded{j}") for j in range(2)]
    mod_done = Count(nc, "mod_done")
    mod_kept = Count(nc, "mod_kept")
    mod_step = Count(nc, "mod_step")
    sq_made = Count(nc, "sq_made")
    sq_added = Count(nc, "sq_added")
    pool_half = Count(nc, "pool_half")

    def V(ins):
        return v_.inc(ins)

    def A(ins):
        return a_.inc(ins)

    def PEs(ins):
        return p_.inc(ins)

    for c in (evac, out_lo):
        for _ in range(CREDIT):
            c.inc(dve.memset(stats[:, 0, 0:1], 0.0))
            wait(dve, c)
    for _ in range(CREDIT):
        wait(pool, sq_added, sq_added.inc(pool.memset(ssum[:, 0:1], 0.0)))
    V(dve.memset(tok[:], 1.0))

    x_in = Count(nc, "x_in")
    for dst, src in ((vecs[:], t["vecs"]), (mats[:], t["mats"]), (swap2[:], t["swap2"])):
        consts_in.inc(act.dma_start(dst, src), 16)
    for dst, src in ((x[:, :, 0:S], t["x"]), (x[:, :, S:T2], t["ctx"])):
        x_in.inc(act.dma_start(dst, src), 16)
    for e in (pe, dve, act):
        wait(e, consts_in)

    class Phase:

        def __init__(self, w, n_units, elems, pe_unit, empty, finish=None, pool=None, mods=False):
            self.w, self.n, self.elems, self.pe_unit = w, n_units, elems, pe_unit
            self.empty, self.finish, self.pool, self.mods = empty, finish, pool, mods
            self.ready = None
            self.u0 = loaded[0].n // 16 * 2
            self.nb = (n_units + 1) // 2
            self.slots = min(2, n_units)
            self.load()

        def load(self):
            g0 = mods_sent[0]

            def body(i):
                for j in range(self.slots):
                    wait(sp, split_lo, 2 * (self.u0 + 2 * i + j) - 2)
                    sp.dma_start(w_raw[j][:, 0:self.elems], self.w[2 * i + j]).then_inc(loaded[j].sem, 16)
                    g = g0 + 2 * i + j
                    if self.mods and not (isinstance(g, int) and g == mods_ahead[0]):
                        mod_load(g, 1 - j)
            body(0)
            if self.nb > 1:
                with nc.Fori(1, self.nb, engines=(ENG.SP,)) as i:
                    body(i)
            for j in range(2):
                loaded[j].n += 16 * self.nb
            if self.mods:
                mods_sent[0] += self.n
            if self.mods == "then a gap":
                mods_ahead[0] = mods_sent[0]
                mod_load(mods_ahead[0], mods_ahead[0] % 2)

        def split(self, ul, slot):
            u = self.u0 + ul
            half = self.elems // 2
            wait(act, loaded[slot], (u - slot) * 8 + 16)
            wait(act, unit_done, u - 1)
            for n in range(2):
                cols = slice(n * half, (n + 1) * half)
                act.activation(w_hi[slot][:, cols], w_raw[slot][:, cols], ACT.Copy).then_inc(split_hi.sem, 1)
            for n in range(2):
                cols = slice(n * half, (n + 1) * half)
                wait(dve, split_hi, 2 * u + n + 1)
                dve.tensor_tensor(w_lo[slot][:, cols], w_raw[slot][:, cols], w_hi[slot][:, cols].bitcast(F32),
                                  ALU.subtract).then_inc(split_lo.sem, 1)

        def multiply(self):
            g0 = N_FIRST + mod_kept.n

            def body(i, ready=None):
                for j in range(self.slots):
                    u = self.u0 + 2 * i + j
                    wait(pe, split_lo, 2 * u + 2)
                    wait(pe, evac, CREDIT + u - 1)
                    self.pe_unit(2 * i + j, j, ready if j == 0 else None).then_inc(unit_done.sem, 1)
                    if self.mods:
                        mod_sum(g0 + 2 * i + j, 1 - j)
            body(0, self.ready)
            if self.nb > 1:
                with nc.Fori(1, self.nb, engines=(ENG.PE,)) as i:
                    body(i)

        def run(self, after=None):
            self.multiply()
            g0 = N_FIRST + mod_kept.n

            def slot_work(ul, j, following, ul_following):
                self.empty(ul, self.u0 + ul, j)
                if following is not None:
                    following.split(ul_following, j)
                if self.finish is not None:
                    self.finish(ul, self.u0 + ul, j)
                if self.mods:
                    mod_keep(g0 + ul, 1 - j)
                    mod_products(g0 + ul + 1, j)
            if self.nb > 1:
                with nc.Fori(0, self.nb - 1, engines=(ENG.DVE, ENG.Activation)) as i:
                    for j in range(2):
                        slot_work(2 * i + j, j, self, 2 * i + 2 + j)
            split_hi.n = split_lo.n = 2 * (self.u0 + self.n)
            unit_done.n = self.u0 + self.n
            for j in range(self.slots):
                ul = 2 * self.nb - 2 + j
                slot_work(ul, j, after if after is not None and j < after.n else None, j)
            if self.pool is not None:
                if self.nb > 1:
                    with nc.Fori(0, self.nb, engines=(ENG.Pool,)) as i:
                        for j in range(2):
                            self.pool(2 * i + j, j)
                else:
                    for j in range(self.slots):
                        self.pool(j, j)
                sq_made.n += self.n
                sq_added.n += self.n
            evac.n = CREDIT + self.u0 + self.n
            if self.mods:
                mod_done.n += self.n
                mod_kept.n += self.n

        def first_splits(self):
            for j in range(self.slots):
                self.split(j, j)

    N_FIRST = 2 * NC + 1
    N_MODS = 2 * N_MOD * NC
    STEPS = 2 * NC
    SUMMED = NC
    mods_sent = [N_FIRST]
    mods_ahead = [N_FIRST]
    mod_raw = [sb(f"mod_raw{j}", [P, NC, P]) for j in range(2)]
    mod_sb = sb("mod_sb", [P, N_MODS, 2])
    cond = sb("cond", [P, NC, 2])
    b_mod = vecs[:, vec_at["b_mod"]:vec_at["b_mod"] + 2 * N_MODS].rearrange("p (m s) -> p m s", s=2)

    def mod_load(g, slot):
        if isinstance(g, int) and g == N_FIRST + 1:
            wait(sp, v_, first_mods)
        wait(sp, mod_step, STEPS * (g - N_FIRST - 1))
        sp.dma_start(mod_raw[slot][:], t["w_mod"][g]).then_inc(mod_loaded[slot].sem, 16)

    def accumulate(slot, w, signal, signalled):
        for k in range(NC):
            for s in range(2):
                acc = mod_acc[:, slot, s, :]
                if k == 0:
                    ins = dve.tensor_scalar(acc, w[:, 0, :], cond[:, 0, s:s + 1], None, ALU.mult)
                else:
                    wait(dve, signal, signalled + 2 * (k - 1) + s + 1)
                    ins = dve.scalar_tensor_tensor(acc, w[:, k, :], cond[:, k, s:s + 1], acc, ALU.mult, ALU.add)
                ins.then_inc(signal.sem, 1)

    def partition_sum(bank, col, slot):
        for s in range(2):
            mm = pe.matmul(ps_s[:, bank, col + s:col + s + 1], mod_acc[:, slot, s, :], ones[:, 0:1],
                           start=True, stop=True)
        return mm

    def mod_products(g, slot):
        wait(dve, mod_loaded[slot], (g - N_FIRST - 1 - slot) * 8 + 16)
        wait(dve, mod_done, SUMMED + g - N_FIRST - 1)
        accumulate(slot, mod_raw[slot][:], mod_step, STEPS * (g - N_FIRST))

    def mod_sum(g, slot):
        wait(pe, mod_step, STEPS * (g - N_FIRST + 1))
        wait(pe, mod_kept, g - N_FIRST - 1)
        partition_sum(2 + slot, 0, slot).then_inc(mod_done.sem, 1)

    def mod_keep(g, slot):
        wait(dve, mod_done, SUMMED + g - N_FIRST + 1)
        dve.tensor_tensor(mod_sb[:, g, :], ps_s[:, 2 + slot, 0:2], b_mod[:, g, :], ALU.add).then_inc(mod_kept.sem, 1)

    def mod_first(buffers):
        src, arrived = [], []
        for n, (buf, size) in enumerate([(b, 4) for b in buffers] + [(m[:].unsqueeze(1), 1) for m in mod_raw]):
            g, c = len(src), Count(nc, f"mod_group{n}")
            c.inc(sp.dma_start(buf, t["w_mod"][g:g + size].rearrange("m p k n -> p m k n")), 16)
            src += [buf[:, j] for j in range(size)]
            arrived += [c] * size
        by_dve = [g for g in range(N_FIRST + 1) if g % 4 >= 2 or g == N_FIRST]
        by_pe = [g for g in range(N_FIRST + 1) if g not in by_dve]
        assert len(src) == N_FIRST + 1 and len(by_dve) == SUMMED + 1 == len(by_pe)
        ready = []
        for n, g in enumerate(by_dve):
            wait(dve, arrived[g])
            wait(dve, mod_done, n - 1)
            last = g == N_FIRST
            accumulate((n + 1) % 2, src[g], mod_step if last else v_, 0 if last else v_.n)
            if not last:
                v_.n += STEPS
                ready.append(v_.n)
        for n, g in enumerate(by_pe):
            wait(pe, arrived[g])
            for k in range(NC):
                mm = pe.matmul(ps_s[:, 2, 2 * g:2 * g + 2], src[g][:, k, :], cond[:, k, :],
                               start=(k == 0), stop=(k == NC - 1))
            if n > 0:
                wait(pe, v_, ready[n - 1])
                mod_done.inc(partition_sum(2, 2 * by_dve[n - 1], n % 2))
        wait(dve, mod_done)
        V(dve.tensor_tensor(mod_sb[:, 0:N_FIRST, :], ps_s[:, 2, 0:2 * N_FIRST].rearrange("p (m s) -> p m s", s=2),
                            b_mod[:, 0:N_FIRST, :], ALU.add))
        wait(dve, v_)
        return v_.n

    ring = [gate_tmp[:, 0, :], gate_tmp[:, 1, :], prod[:, 0, :], prod[:, 1, :]]

    def squares_of(c, T, hist):
        if c == 0:
            wait(act, sq_added)
            sq_made.inc(act.activation(ssum[:, 0:T], x[:, 0, 0:T], ACT.Square))
            hist.append(sq_added.n)
            return
        wait(act, sq_added, hist[max(c - 2, 0)])
        sq_made.inc(act.activation(sq[:, c % 2, 0:T], x[:, c, 0:T], ACT.Square))
        wait(pool, sq_made)
        wait(pool, sq_added)
        hist.append(sq_added.inc(pool.tensor_tensor(ssum[:, 0:T], ssum[:, 0:T], sq[:, c % 2, 0:T], ALU.add)))

    def rstd_from_sums(T, meanwhile=None):
        nt = T // P
        A(act.activation(tok[:, 8:9], tok[:, 8:9], ACT.Sqrt))
        if meanwhile is not None:
            meanwhile()
        wait(pe, sq_added)
        for j in range(nt):
            mm = pe.matmul(ps_s[:, 0, j:j + 1], ssum[:, j * P:(j + 1) * P], ones[:, 0:1], start=True, stop=True)
        wait(dve, p_, PEs(mm))
        wait(act, v_, V(dve.tensor_scalar(tok[:, 0:nt], ps_s[:, 0, 0:nt], 1.0 / D, EPS, ALU.mult, ALU.add)))
        wait(dve, a_, A(act.activation(tok[:, 0:nt], tok[:, 0:nt], ACT.Sqrt)))
        wait(pe, v_, V(dve.reciprocal(tok[:, 4:4 + nt], tok[:, 0:nt])))
        for j in range(nt):
            mm = pe.matmul(ps_s[:, 1, j * P:(j + 1) * P], tok[:, 4 + j:5 + j].to_broadcast([P, P]), ident,
                           start=True, stop=True)
        wait(dve, p_, PEs(mm))
        return ps_s[:, 1, 0:T]

    def norm_in(h_hi, h_lo, streams, scale, shift=None):
        T = S * streams
        r = rstd_from_sums(T)
        wait(dve, out_lo)
        wait(dve, evac)
        wait(dve, v_)
        wait(dve, a_)
        parts = [slice(S * s, S * s + S) for s in range(streams)]
        multiplied, high, low = [], [], []

        def multiply(c):
            if c >= 4:
                wait(dve, v_, low[c - 4])
            if shift is not None:
                ins = dve.tensor_tensor(ring[c % 4][:, 0:T], x[:, c, 0:T], r, ALU.mult)
            else:
                ins = dve.scalar_tensor_tensor(ring[c % 4][:, 0:T], x[:, c, 0:T], scale(c, 0), r, ALU.mult, ALU.mult)
            multiplied.append(V(ins))

        def to_high(c):
            buf = ring[c % 4]
            wait(act, v_, multiplied[c])
            if shift is not None:
                for s, cols in enumerate(parts):
                    A(act.activation(buf[:, cols], buf[:, cols], ACT.Identity, bias=shift(c, s), scale=scale(c, s)))
                wait(act, a_)
            high.append(A(act.activation(h_hi[:, c, 0:T], buf[:, 0:T], ACT.Copy)))

        def to_low(c):
            wait(dve, a_, high[c])
            low.append(V(dve.tensor_tensor(h_lo[:, c, 0:T], ring[c % 4][:, 0:T], h_hi[:, c, 0:T].bitcast(F32),
                                           ALU.subtract)))
        multiply(0)
        for c in range(NC + 1):
            if c + 1 < NC:
                multiply(c + 1)
            if c < NC:
                to_high(c)
            if c > 0:
                to_low(c - 1)
        return lambda k: wait(pe, v_, low[k])

    def norm_out(streams, scale):
        T = S * streams
        wait(act, evac)
        wait(act, out_lo)
        parts = [slice(S * s, S * s + S) for s in range(streams)]
        scaled, multiplied, added, hist = [], [], [], []

        def to_scaled(c):
            if c >= 4:
                wait(act, v_, added[c - 4])
            for s, cols in enumerate(parts):
                A(act.activation(ring[c % 4][:, cols], y[:, c, cols], ACT.Copy, scale=scale(c, s)))
            scaled.append(a_.n)

        def multiply(c):
            buf = ring[c % 4][:, 0:T]
            wait(dve, a_, scaled[c])
            multiplied.append(V(dve.tensor_tensor(buf, buf, r, ALU.mult)))

        def ahead():
            to_scaled(0)
            to_scaled(1)
        wait(act, v_)
        r = rstd_from_sums(T, ahead)
        wait(act, p_)
        multiply(0)
        for c in range(NC):
            if c + 1 < NC:
                multiply(c + 1)
            wait(dve, v_, multiplied[c])
            added.append(V(dve.tensor_tensor(x[:, c, 0:T], x[:, c, 0:T], ring[c % 4][:, 0:T], ALU.add)))
            if c + 2 < NC:
                to_scaled(c + 2)
            wait(act, v_, added[c])
            squares_of(c, T, hist)

    PARTS = ((0, 0), (0, 1), (1, 0))

    def features(acts, kc, mt, T, k0=0):
        def unit(ul, slot, ready=None):
            w = [w_[slot][:, 0:kc * mt * P].rearrange("p (k n) -> p k n", k=kc) for w_ in (w_hi, w_lo)]
            for m in range(mt):
                for k in range(kc):
                    if ready is not None and m == 0:
                        ready(k)
                    for n, (wp, ap) in enumerate(PARTS):
                        mm = pe.matmul(ps_g[:, 2 * slot + m, 0:T], w[wp][:, k, m * P:(m + 1) * P],
                                       acts[ap][:, k0 + k, 0:T], start=(k == 0 and n == 0),
                                       stop=(k == kc - 1 and n == 2))
            return mm
        return unit

    def tokens(acts, n_tiles):
        def unit(ul, slot, ready=None):
            w = [w_[slot][:, 0:UNIT].rearrange("p (k n) -> p k n", k=NC) for w_ in (w_hi, w_lo)]
            for i in range(n_tiles):
                for k in range(NC):
                    for n, (wp, ap) in enumerate(PARTS):
                        mm = pe.matmul(ps_g[:, 2 * slot + i // 2, S * (i % 2):S * (i % 2) + S],
                                       acts[ap][:, k, i * P:(i + 1) * P], w[wp][:, k, :],
                                       start=(k == 0 and n == 0), stop=(k == NC - 1 and n == 2))
            return mm
        return unit

    def gated_split(dst, T, func):
        made, lo, hi = gate_made.n, out_lo.n, out_hi.n

        def empty(ul, u, slot):
            wait(act, unit_done, u + 1)
            wait(act, evac, CREDIT + u - 1)
            act.activation(gate_tmp[:, slot, 0:T], ps_g[:, 2 * slot, 0:T], func).then_inc(gate_made.sem, 1)
            wait(dve, gate_made, made + ul + 1)
            wait(dve, out_lo, lo + ul - 1)
            dve.tensor_tensor(prod[:, slot, 0:T], gate_tmp[:, slot, 0:T], ps_g[:, 2 * slot + 1, 0:T],
                              ALU.mult).then_inc(evac.sem, 1)

        def finish(ul, u, slot):
            wait(act, evac, CREDIT + u + 1)
            act.activation(dst[0][:, ul, 0:T], prod[:, slot, 0:T], ACT.Copy).then_inc(out_hi.sem, 1)
            wait(dve, out_hi, hi + ul + 1)
            dve.tensor_tensor(dst[1][:, ul, 0:T], prod[:, slot, 0:T], dst[0][:, ul, 0:T].bitcast(F32),
                              ALU.subtract).then_inc(out_lo.sem, 1)
        return empty, finish

    def keep(dst, T, mt=2, func=ACT.Copy):
        def empty(ul, u, slot):
            wait(act, unit_done, u + 1)
            act.activation(dst[:, bass.ds(ul * mt, mt), 0:T], ps_g[:, 2 * slot:2 * slot + mt, 0:T],
                           func).then_inc(evac.sem, 1)
        return empty

    def add_to(dst, T, mt=1):
        def empty(ul, u, slot):
            wait(dve, unit_done, u + 1)
            d = dst[:, bass.ds(ul * mt, mt), 0:T]
            dve.tensor_tensor(d, d, ps_g[:, 2 * slot:2 * slot + mt, 0:T], ALU.add).then_inc(evac.sem, 1)
        return empty

    def sum_squares(dst, T, mt):
        made, added = sq_made.n, sq_added.n
        whole = mt * T == 2 * T2

        def where(slot):
            if whole:
                return sq[:]
            return sq[:, slot, 0:mt * T].rearrange("p (m n) -> p m n", m=mt)
        wait(pool, p_)
        wait(pool, v_)
        wait(pool, g_, g_.inc(pool.memset(ssum[:, 0:T], 0.0)))

        def finish(ul, u, slot):
            wait(act, evac, CREDIT + u + 1)
            wait(act, sq_added, added + ul - (0 if whole else 1))
            act.activation(where(slot), dst[:, bass.ds(ul * mt, mt), 0:T], ACT.Square).then_inc(sq_made.sem, 1)

        def pool_add(ul, slot):
            wait(pool, sq_made, made + ul + 1)
            for m in range(mt):
                ins = pool.tensor_tensor(ssum[:, 0:T], ssum[:, 0:T], where(slot)[:, m, :], ALU.add)
                if m == mt - 1:
                    ins.then_inc(sq_added.sem, 1)
                else:
                    ins.then_inc(pool_half.sem, 1)
                    wait(pool, pool_half, half0 + ul + 1)
            wait(pool, sq_added, added + ul + 1)
        half0 = pool_half.n
        if mt == 2:
            pool_half.n += NC // 2
        return finish, pool_add

    def ffn_first(w_gu, acts, hid, streams, mods=False):
        return Phase(t[w_gu], FFN_HALVES[0], UNIT, features(acts, NC, 2, S * streams),
                     *gated_split(hid, S * streams, ACT.Silu), mods=mods)

    def ffn(gu0, w_gu, w_down, acts, hid, streams, following, mods=False, into=None):
        T = S * streams
        n0, n1 = FFN_HALVES
        dst = y if into is None else into

        def hidden(n):
            base = out_lo.n

            def ready(k):
                wait(pe, out_lo, base + k + 1)
            gate_made.n += n
            out_hi.n += n
            out_lo.n += n
            return ready
        dn0 = Phase(t[w_down + "a"], NC, n0 * P, features(hid, n0, 1, T),
                    keep(y, T, 1) if into is None else add_to(into, T, 1), mods=mods)
        gu0.run(dn0)
        dn0.ready = hidden(n0)
        gu1 = Phase(t[w_gu][n0:n0 + n1], n1, UNIT, features(acts, NC, 2, T), *gated_split(hid, T, ACT.Silu),
                    mods=mods)
        dn0.run(gu1)
        dn1 = Phase(t[w_down + "b"], NC, n1 * P, features(hid, n1, 1, T), add_to(dst, T, 1),
                    *sum_squares(dst, T, 1), mods=mods)
        gu1.run(dn1)
        dn1.ready = hidden(n1)
        first = following()
        dn1.run(first)
        return first

    ab = sb("ab", [P, 2, NC, 2])
    b1 = ExitStack()
    h = [sb(f"h{j}", [P, NC, T2], F32R, b1) for j in range(2)]
    wide = sb("wide", [P, NC, 2, S + 2], F32, b1)
    band = mod_raw[0][:].rearrange("p a b -> p (a b)").rearrange("p (q n) -> p q n", q=2)
    rope1 = mod_raw[1][:, 0:4, :].rearrange("p a b -> p (a b)").rearrange("p (q n) -> p q n", q=2)
    score_slots = [gate_tmp[:, 0, :], gate_tmp[:, 1, :], sq[:, 0, :]]

    wait(pe, a_, A(act.activation(cond[:], vec("cond", 0, 2 * NC).rearrange("p (k s) -> p k s", s=2), ACT.Silu)))
    wait(dve, a_)
    wait(act, v_)
    with ExitStack() as early:
        by_four = [y[:].rearrange("p a (b n) -> p (a b) n", n=P).rearrange("p (m k) n -> p m k n", m=4)]
        by_four += [sb(f"w_mod{j}", [P, 4, NC, P], F32, early)[:] for j in range(3)]
        first_mods = mod_first(by_four)
    hid = [sb(f"hid{j}", [P, FFN_HALVES[0], T2], F32R, b1) for j in range(2)]

    def mod_at(layer, k):
        a = (layer * N_MOD + k) * NC
        return mod_sb[:, a:a + NC, :]

    def g_at(layer, n):
        a = vec_at["norm_g"] + (layer * 6 + n) * 2 * NC
        return vecs[:, a:a + 2 * NC].rearrange("p (c s) -> p c s", s=2)

    def adaln(layer, k, n, weight, streams):
        def before():
            wait(dve, mod_kept)
            V(dve.scalar_tensor_tensor(ab[:, 0], mod_at(layer, k + 1), 1.0, g_at(layer, n), ALU.add, ALU.mult))
            wait(act, v_)
            return norm_in(h[0], h[1], streams, lambda c, s: ab[:, 0, c, s:s + 1],
                           lambda c, s: mod_at(layer, k)[:, c, s:s + 1])

        def after(streams=streams):
            wait(dve, mod_kept)
            V(dve.scalar_tensor_tensor(ab[:, 1], mod_at(layer, k + 2), weight, g_at(layer, n + 1),
                                       ALU.mult, ALU.mult))
            norm_out(streams, lambda c, s: ab[:, 1, c, s:s + 1])
        return before, after

    first = ffn_first("gu00", h, hid, 2, True)
    for e in (act, dve):
        wait(e, x_in)
    hist = []
    for c in range(NC):
        squares_of(c, T2, hist)
    first.first_splits()
    before, after = adaln(0, 0, 0, 0.5, 2)
    first.ready = before()

    conv_step = Count(nc, "conv_step")

    def conv_first():
        made, steps = gate_made.n, conv_step.n

        def product_wide(ul, u, slot):
            wait(act, unit_done, u + 1)
            wait(act, evac, CREDIT + u - 1)
            act.activation(gate_tmp[:, slot, :], ps_g[:, 2 * slot, :], ACT.Copy).then_inc(gate_made.sem, 1)
            wait(dve, gate_made, made + ul + 1)
            dve.tensor_tensor(wide[:, ul, :, 1:S + 1],
                              gate_tmp[:, slot, :].rearrange("p (s n) -> p s n", s=2),
                              ps_g[:, 2 * slot + 1, :].rearrange("p (s n) -> p s n", s=2),
                              ALU.mult).then_inc(evac.sem, 1)

        def convolve(ul, u, slot):
            wait(dve, evac, CREDIT + u + 1)
            yc = y[:, ul, :].rearrange("p (s n) -> p s n", s=2)
            for n, tap in enumerate((1, 0, 2)):
                src = wide[:, ul, :, tap:tap + S]
                w_tap = vecs[:, bass.ds(ul + (vec_at["conv_w"] + tap * NC), 1)]
                if n == 0:
                    ins = dve.tensor_scalar(yc, src, w_tap, None, ALU.mult)
                else:
                    wait(dve, conv_step, steps + 3 * ul + n)
                    ins = dve.scalar_tensor_tensor(yc, src, w_tap, yc, ALU.mult, ALU.add)
                ins.then_inc(conv_step.sem, 1)
        return Phase(t["conv_cu"], NC, UNIT, features(h, NC, 2, T2), product_wide, convolve,
                     mods="then a gap")

    def conv_layer(c1, following):
        before, after = adaln(0, 3, 2, 1.0, 2)
        c1.ready = before()
        V(dve.memset(wide[:, :, :, 0:1], 0.0))
        V(dve.memset(wide[:, :, :, S + 1:S + 2], 0.0))
        wait(dve, v_)
        base, base_hi = out_lo.n, out_hi.n

        def times_b(ul, u, slot):
            wait(dve, unit_done, u + 1)
            wait(dve, out_lo, base + ul)
            dve.tensor_tensor(prod[:], y[:, bass.ds(2 * ul, 2), :], ps_g[:, 2 * slot:2 * slot + 2, :],
                              ALU.mult).then_inc(evac.sem, 1)

        def in_parts(ul, u, slot):
            wait(act, evac, CREDIT + u + 1)
            act.activation(hid[0][:, bass.ds(2 * ul, 2), :], prod[:], ACT.Copy).then_inc(out_hi.sem, 1)
            wait(dve, out_hi, base_hi + ul + 1)
            dve.tensor_tensor(hid[1][:, bass.ds(2 * ul, 2), :], prod[:],
                              hid[0][:, bass.ds(2 * ul, 2), :].bitcast(F32), ALU.subtract).then_inc(out_lo.sem, 1)
        c2 = Phase(t["conv_b"], NC // 2, UNIT, features(h, NC, 2, T2), times_b, in_parts)
        c1.run(c2)
        gate_made.n += NC
        conv_step.n += 3 * NC
        wait(dve, conv_step)
        c3 = Phase(t["conv_out"], NC // 2, UNIT, features(hid, NC, 2, T2), keep(y, T2), *sum_squares(y, T2, 2),
                   mods=True)
        c2.run(c3)
        out_hi.n += NC // 2
        out_lo.n += NC // 2
        wait(act, out_lo)
        c3.ready = lambda k: wait(pe, out_lo, base + k // 2 + 1)
        first = following()
        c3.run(first)
        after()
        return first

    first = ffn(first, "gu00", "dn00", h, hid, 2, conv_first, True)
    after()
    first = conv_layer(first, lambda: ffn_first("gu01", h, hid, 2, True))
    before, after = adaln(0, 6, 4, 0.5, 2)
    first.ready = before()
    first = ffn(first, "gu01", "dn01", h, hid, 2, lambda: ffn_first("gu10", h, hid, 2, True), True)
    after()

    before, after = adaln(1, 0, 0, 0.5, 2)
    first.ready = before()
    wf = wide[:].rearrange("p a b c -> p (a b c)")
    k_raw = wf[:, 0:4 * S].rearrange("p (a n) -> p a n", a=2)
    v_tok = wf[:, 4 * S:8 * S].rearrange("p (a n) -> p a n", a=4)
    q_raw = wf[:, 8 * S:16 * S].rearrange("p (a n) -> p a n", a=8)

    def kv_first():
        units = features(h, NC, 2, T2), tokens(h, 4)
        dst = k_raw, v_tok.rearrange("p (a b) n -> p a (b n)", a=2)

        def kv_keep(ul, u, slot):
            wait(act, unit_done, u + 1)
            act.activation(dst[slot], ps_g[:, 2 * slot:2 * slot + 2, :], ACT.Copy).then_inc(evac.sem, 1)
        mod_load(N_MODS - 1, 1)
        return Phase(t["attn_kv"], 2, UNIT, lambda ul, slot, ready: units[slot](ul, slot, ready), kv_keep)
    first = ffn(first, "gu10", "dn10", h, hid, 2, kv_first, True)
    assert mod_kept.n + N_FIRST == N_MODS - 1
    mod_sum(N_MODS - 1, 1)
    mod_keep(N_MODS - 1, 1)
    mod_done.n += 1
    mod_kept.n += 1
    after()

    sem_s = Count(nc, "item_scores")
    sem_m = Count(nc, "item_max")
    sem_e = Count(nc, "item_exp")
    sem_r = Count(nc, "item_normed")
    sem_t = Count(nc, "item_turned")
    sem_c = Count(nc, "item_copied")
    sem_o = Count(nc, "item_out")
    sem_k = Count(nc, "tile_kept")

    def attention(items, o_dst, scratch, probs):
        N = len(items)
        b_s, b_m, b_e, b_r, b_t, b_c, b_o, b_k = (c.n for c in (sem_s, sem_m, sem_e, sem_r, sem_t, sem_c, sem_o, sem_k))
        tiles_done = {}
        order = []
        for i, it in enumerate(items):
            if it["close"]:
                tiles_done[i] = len(order)
                order.append(it["tile"])

        def s_scores(i):
            it = items[i]
            if i >= 2:
                wait(pe, sem_m, b_m + i - 1)
            sem_s.inc(pe.matmul(ps_g[:, i % 2, 0:it["n"]], it["q"], it["k"], start=True, stop=True))

        def s_max(i):
            it = items[i]
            n = it["n"]
            wait(dve, sem_s, b_s + i + 1)
            if i >= 3:
                wait(dve, sem_t, b_t + i - 2)
            V(dve.tensor_tensor_reduce(scratch[i % 3][:, 0:n], ps_g[:, i % 2, 0:n], it["mask"], 1.0, -3.0e38,
                                       ALU.add, ALU.max, stats[:, 0, i:i + 1]))
            wait(dve, v_)
            if it["sink"] is None:
                sem_m.inc(dve.tensor_scalar(stats[:, 1, i:i + 1], stats[:, 0, i:i + 1], -0.125, None, ALU.mult))
            else:
                sem_m.inc(dve.tensor_scalar(stats[:, 1, i:i + 1], stats[:, 0, i:i + 1], -0.125,
                                            it["neg_sink"], ALU.mult, ALU.min))

        def s_exp(i):
            it = items[i]
            n = it["n"]
            wait(act, sem_m, b_m + i + 1)
            ins = act.activation(scratch[i % 3][:, 0:n], scratch[i % 3][:, 0:n], ACT.Exp,
                                 bias=stats[:, 1, i:i + 1], scale=0.125, accum_out=stats[:, 2, i:i + 1])
            if it["sink"] is not None:
                A(ins)
                ins = act.activation(stats[:, 3, i:i + 1], it["sink"], ACT.Exp, bias=stats[:, 1, i:i + 1])
            sem_e.inc(ins)

        def s_norm(i):
            it = items[i]
            n = it["n"]
            wait(dve, sem_e, b_e + i + 1)
            if it["sink"] is not None:
                V(dve.tensor_tensor(stats[:, 2, i:i + 1], stats[:, 2, i:i + 1], stats[:, 3, i:i + 1], ALU.add))
                wait(dve, v_)
            V(dve.reciprocal(stats[:, 4, i:i + 1], stats[:, 2, i:i + 1]))
            wait(dve, v_)
            p = scratch[i % 3][:, 0:n]
            if it["weight"] is None:
                sem_r.inc(dve.tensor_scalar(p, p, stats[:, 4, i:i + 1], None, ALU.mult))
            else:
                sem_r.inc(dve.tensor_scalar(p, p, stats[:, 4, i:i + 1], it["weight"], ALU.mult, ALU.mult))

        def s_turn(i):
            it = items[i]
            wait(pe, sem_r, b_r + i + 1)
            if i >= 2:
                wait(pe, sem_c, b_c + i - 1)
            k = 0
            while k * P < it["n"]:
                w = min(P, it["n"] - k * P)
                ins = pe.transpose(ps_g[0:w, 2 + i % 2, k * P:(k + 1) * P],
                                   scratch[i % 3][:, k * P:k * P + w], ident)
                k += 1
            sem_t.inc(ins)

        def s_copy(i):
            it = items[i]
            n = it["n"]
            w = min(P, n)
            m = -(-n // P) * P
            wait(act, sem_t, b_t + i + 1)
            if i >= 2:
                wait(act, sem_o, b_o + i - 1)
            sem_c.inc(act.activation(probs[0:w, i % 2, 0:m], ps_g[0:w, 2 + i % 2, 0:m], ACT.Copy))

        def s_out(i):
            it = items[i]
            n = it["n"]
            w = min(P, n)
            wait(pe, sem_c, b_c + i + 1)
            closed = [j for j in tiles_done if j < i]
            if it["open"] and len(closed) >= 2:
                wait(pe, sem_k, b_k + len(closed) - 1)
            bank = len(closed) % 2
            last = -(-n // P)
            for k in range(last):
                ins = pe.matmul(ps_s[it["half"] * HD:(it["half"] + 1) * HD, bank, it["qt"] * P:(it["qt"] + 1) * P],
                                it["v"](k), probs[0:w, i % 2, k * P:(k + 1) * P],
                                start=(it["first"] and k == 0), stop=(it["last"] and k == last - 1))
            sem_o.inc(ins)

        def s_keep(i):
            if i not in tiles_done:
                return
            n = tiles_done[i]
            tile = order[n]
            wait(act, sem_o, b_o + i + 1)
            A(act.activation(o_dst[0][:, tile, 0:S], ps_s[:, n % 2, 0:S], ACT.Copy))
            wait(dve, a_)
            sem_k.inc(dve.tensor_tensor(o_dst[1][:, tile, 0:S], ps_s[:, n % 2, 0:S],
                                        o_dst[0][:, tile, 0:S].bitcast(F32), ALU.subtract))

        for e in (v_, a_, evac):
            wait(pe, e)
        for e in (a_, evac):
            wait(dve, e)
        for e in (v_, p_):
            wait(act, e)
        for s in range(N + 6):
            for stage, lag in ((s_scores, 0), (s_max, 0), (s_exp, 0), (s_norm, 1), (s_turn, 2), (s_copy, 2),
                               (s_out, 3), (s_keep, 4)):
                if 0 <= s - lag < N:
                    stage(s - lag)
        wait(pe, sem_k)

    def attn_layer(kv, following):
        before, after = adaln(1, 3, 2, 1.0, 2)
        kv.ready = before()
        yf = y[:].rearrange("p a b -> p (a b)")
        q = yf[:, 0:8 * S].rearrange("p (a n) -> p a n", a=8)
        k = yf[:, 8 * S:12 * S].rearrange("p (a n) -> p a n", a=2)
        m1 = yf[:, 12 * S:14 * S].rearrange("p (a n) -> p a n", a=2)
        qp = Phase(t["attn_q"], NC // 2, UNIT, features(h, NC, 2, S), keep(q_raw, S))
        kv.run(qp)
        wait(act, mod_done)
        for dst, src in ((band, t["band"]), (rope1, t["rope1"])):
            consts_in.inc(act.dma_start(dst, src), 16)
        wo = Phase(t["attn_o"], NC // 2, UNIT, features(hid, NC, 2, S), keep(y, S), *sum_squares(y, S, 2))
        qp.run(wo)

        wait(pe, evac)
        wait(dve, evac)
        wait(dve, consts_in)
        cos = rope1[:, 0:1, :].to_broadcast([P, 2, S])
        sin = rope1[:, 1:2, :].to_broadcast([P, 2, S])
        for n in range(5):
            src, dst = (q_raw[:, 2 * n:2 * n + 2, :], q[:, 2 * n:2 * n + 2, :]) if n < 4 else \
                (k_raw[:, :, 0:S], k[:, :, 0:S])
            bank = ps_s[:, n % 2, :].rearrange("p (a n) -> p a n", a=2)
            if n >= 2:
                wait(pe, v_)
            wait(dve, p_, PEs(pe.matmul(bank, swap1, src, start=True, stop=True)))
            V(dve.tensor_tensor(dst, src, cos, ALU.mult))
            wait(dve, v_, V(dve.tensor_tensor(m1, bank, sin, ALU.mult)))
            wait(dve, v_, V(dve.tensor_tensor(dst, dst, m1, ALU.add)))
        V(dve.tensor_copy(k[:, :, S:T2], k_raw[:, :, S:T2]))

        items = []
        for tile in range(NC):
            for half in range(2):
                head = (tile // 4) * 8 + half * 4 + tile % 4
                kvh = head // 4
                for qt in range(2):
                    rows = slice(half * HD, (half + 1) * HD)
                    items.append(dict(
                        q=q[rows, tile, qt * P:(qt + 1) * P], k=k[rows, kvh // 2, :], n=T2, mask=band[:, qt, :],
                        sink=vec("sink", head), neg_sink=vec("neg_sink", head), weight=None,
                        v=lambda kt, kvh=kvh: v_tok[:, kt, kvh * HD:(kvh + 1) * HD],
                        tile=tile, half=half, qt=qt, first=True, last=True,
                        open=(half == 0 and qt == 0), close=(half == 1 and qt == 1)))
        assert len(items) <= 64
        V(dve.tensor_scalar(vec("neg_sink", 0, 16), vec("sink", 0, 16), -1.0, None, ALU.mult))
        attention(items, hid, score_slots, prod)
        wait(act, sem_k)
        wait(dve, sem_o)
        first = following()
        wo.run(first)
        after(1)
        return first

    first = attn_layer(first, lambda: ffn_first("gu11", h, hid, 1))
    before, after = adaln(1, 6, 4, 0.5, 1)
    first.ready = before()
    first = ffn(first, "gu11", "dn11", h, hid, 1, lambda: Phase(t["w_in_a"], 8, UNIT, None, None))
    after()

    for e in (v_, a_, evac):
        wait(act, e)
    b1.close()
    b2 = ExitStack()
    h = [sb(f"b2_h{j}", [P, NC, S], F32R, b2) for j in range(2)]
    hid = [sb(f"b2_hid{j}", [P, FFN_HALVES[0], S], F32R, b2) for j in range(2)]
    qk = sb("qk", [P, 18, S], F32, b2)
    gates = sb("gates", [P, 2 * NC, S], F32, b2)
    v_tok = sb("v_tok", [P, 2, 3 * S], F32, b2)
    flat = sb("flat", [P, 2, 16, 2, 15], F32, b2)
    rope2 = sb("rope2", [P, 2, S], F32, b2)
    causal = sb("causal", [P, S + 30], F32, b2)
    gn = [sb(f"gn{j}", [P, NC * 24], F32R, b2) for j in range(2)]
    small = sb("small", [P, 320], F32, b2)
    gate_n = sb("gate_n", [P, NC * 24], F32, b2)
    pos_i = sb("pos_i", [P, S], I32, b2)
    p_in = sb("p_in", [P, 2, S], F32, b2)
    branch = small[:, 0:48].rearrange("p (q n) -> p q n", q=2)
    hid_c = small[:, 48:168].rearrange("p (k m n) -> p k m n", k=2, m=2)
    kc = small[:, 168:183]
    kc_tmp = small[:, 184:199]
    yt = y[:].rearrange("p a b -> p (a b)").rearrange("p (a n) -> p a n", n=S)

    loads2 = [
        (x[:, :, S:T2], t["cw1"][0].rearrange("p (k n) -> p k n", k=8)),
        (mod_raw[0][:].rearrange("p a b -> p (a b)"), t["cw1"][1][:, 0:1024]),
        (mod_raw[1][:].rearrange("p a b -> p (a b)"), t["cw1"][1][:, 1024:2048]),
        (y[:, 0:4, :].rearrange("p a b -> p (a b)"), t["cw1"][2]),
        (y[:, 4:8, :].rearrange("p a b -> p (a b)"), t["cw1"][3]),
        (causal[:], t["causal"]),
        (gate_n[:], t["gate_n"]),
        (p_in[:], t["p"]),
        (pos_i[:], t["positions"].partition_broadcast(P)),
    ]
    for dst, src in loads2:
        consts_in.inc(act.dma_start(dst, src), 16)

    def compress_w(kv, jp, m):
        cols = slice(m * P, (m + 1) * P)
        if kv == 1:
            return yt[:, jp, cols]
        if jp < 8:
            return x[:, jp, S + m * P:S + (m + 1) * P]
        return mod_raw[(jp - 8) // 4][:, 2 * (jp % 4) + m, :]

    def norm2(name):
        return norm_in(h[0], h[1], 1, lambda c, s: vec(name, c))

    feat = features(h, NC, 2, S)
    tok2 = tokens(h, 2)

    def tok_keep(col):
        def go(ul, u, slot):
            wait(act, unit_done, u + 1)
            c = col(ul)
            act.activation(v_tok[:, :, c:c + S], ps_g[:, 2 * slot, :].rearrange("p (a n) -> p a n", a=2),
                           ACT.Copy).then_inc(evac.sem, 1)
        return go

    qk_keep = keep(qk, S)
    ph_a = first
    ph_a.pe_unit, ph_a.empty, ph_a.ready = feat, qk_keep, norm2("g_mix")

    vs_keep = tok_keep(lambda ul: 0)

    def b_keep(ul, u, slot):
        if slot == 0:
            wait(act, unit_done, u + 1)
            act.activation(qk[:, 16:18, :], ps_g[:, 0:2, 0:S], ACT.Copy).then_inc(evac.sem, 1)
        else:
            vs_keep(ul, u, slot)
    ph_b = Phase(t["w_in_b"], 2, UNIT, lambda ul, slot, ready: (feat, tok2)[slot](ul, slot), b_keep)
    ph_a.run(ph_b)
    ph_c = Phase(t["w_in_c"], 2, UNIT, tok2, tok_keep(lambda ul: S + ul * S))
    ph_b.run(ph_c)
    ph_d = Phase(t["w_in_d"], 8, UNIT, feat, keep(gates, S, 2, ACT.Sigmoid))
    ph_c.run(ph_d)

    wait(act, consts_in)
    wait(dve, a_, A(act.activation(gn[0][:], gate_n[:], ACT.Copy)))
    wait(pe, v_, V(dve.tensor_tensor(gn[1][:], gate_n[:], gn[0][:].bitcast(F32), ALU.subtract)))
    for qt in range(2):
        for k in range(NC):
            for n, (wp, ap) in enumerate(PARTS):
                mm = pe.matmul(ps_s[:, 2 + qt, 0:24], h[ap][:, k, qt * P:(qt + 1) * P],
                               gn[wp][:, k * 24:(k + 1) * 24], start=(k == 0 and n == 0),
                               stop=(k == NC - 1 and n == 2))
    PEs(mm)

    def up_unit(ul, slot, ready):
        w = [w_[slot][:].rearrange("p (k n) -> p k n", k=NC) for w_ in (w_hi, w_lo)]
        for m in range(2):
            for src in range(2):
                for k in range(4):
                    for n, (wp, ap) in enumerate(PARTS):
                        mm = pe.matmul(ps_g[:, 2 * slot + m, src * S:(src + 1) * S],
                                       w[wp][:, 4 * src + k, m * P:(m + 1) * P], hid[ap][:, 4 * src + k, 0:S],
                                       start=(k == 0 and n == 0), stop=(k == 3 and n == 2))
        return mm

    merge = Count(nc, "merge")
    merge.inc(dve.memset(small[:, 319:320], 0.0))

    def merge_keep(ul, u, slot):
        pa, pb, pc = (prod[:, 0, :].rearrange("p (m n) -> p m n", m=2), prod[:, 1, :].rearrange("p (m n) -> p m n", m=2),
                      gate_tmp[:, 0, :].rearrange("p (m n) -> p m n", m=2))
        wait(dve, unit_done, u + 1)
        wait(dve, merge, 3 * ul + 1)
        dve.tensor_tensor(pa, gates[:, bass.ds(2 * ul, 2), :], ps_g[:, 2 * slot:2 * slot + 2, 0:S],
                          ALU.mult).then_inc(merge.sem, 1)
        dve.tensor_tensor(pb, gates[:, bass.ds(2 * ul + NC, 2), :], ps_g[:, 2 * slot:2 * slot + 2, S:T2],
                          ALU.mult).then_inc(evac.sem, 1)
        wait(dve, merge, 3 * ul + 2)
        wait(dve, evac, CREDIT + u + 1)
        dve.tensor_tensor(pc, pa, pb, ALU.add).then_inc(merge.sem, 1)
        wait(act, merge, 3 * ul + 3)
        act.activation(h[0][:, bass.ds(2 * ul, 2), :], pc, ACT.Copy).then_inc(out_hi.sem, 1)
        wait(dve, out_hi, hi0 + ul + 1)
        dve.tensor_tensor(h[1][:, bass.ds(2 * ul, 2), :], pc, h[0][:, bass.ds(2 * ul, 2), :].bitcast(F32),
                          ALU.subtract).then_inc(merge.sem, 1)
    hi0 = out_hi.n
    ph_up = Phase(t["w_up"], 4, UNIT, up_unit, merge_keep)
    ph_d.run(ph_up)

    wait(act, p_)
    wait(dve, a_, A(act.activation(branch, ps_s[:, 2:4, 0:24], ACT.Sigmoid)))
    comp = branch.rearrange("p q (h b) -> p q h b", b=3)
    V(dve.tensor_scalar(comp[:, 0, :, 0], comp[:, 0, :, 0], vec("any_block"), None, ALU.mult))

    wait(dve, consts_in)
    wait(dve, evac)
    pos_f, turns, kf, ang = (sq[:, 0, 0:S], sq[:, 0, S:T2], sq[:, 1, 0:S], sq[:, 1, S:T2])
    k_int = prod[:, 1, S:T2].bitcast(I32)

    def step(ins):
        V(ins)
        wait(dve, v_)
    step(dve.tensor_copy(pos_f, pos_i[:]))
    step(dve.tensor_scalar(ang, pos_f, vec("inv_freq"), None, ALU.mult))
    for n, (quarter_turn, shift) in enumerate(((0.25, 1.5707963267948966), (0.0, 0.0))):
        r = rope2[:, n, :]
        step(dve.tensor_scalar(turns, ang, 0.15915494309189535, quarter_turn, ALU.mult, ALU.add))
        step(dve.tensor_copy(k_int, turns))
        step(dve.tensor_copy(kf, k_int))
        step(dve.scalar_tensor_tensor(r, kf, -TWO_PI_HI, ang, ALU.mult, ALU.add))
        step(dve.scalar_tensor_tensor(r, kf, -TWO_PI_MID, r, ALU.mult, ALU.add))
        step(dve.scalar_tensor_tensor(r, kf, -TWO_PI_LO, r, ALU.mult, ALU.add))
        step(dve.tensor_scalar(r, r, shift, PI_SAFE, ALU.add, ALU.min))
        step(dve.tensor_scalar(r, r, -PI_SAFE, None, ALU.max))
    wait(act, v_)
    A(act.activation(rope2[:], rope2[:], ACT.Sin))

    for kv in range(2):
        pe_col = vec("pe_k" if kv == 0 else "pe_v", 0, 16)
        for g in range(2):
            for odd in range(2):
                rows = slice(odd * HD, (odd + 1) * HD)
                by16 = qk[rows, 14 + 2 * kv + g, :].rearrange("p (c j) -> p j c", j=16)
                for late in range(2):
                    V(dve.tensor_tensor(flat[rows, kv, 8 * late:8 * late + 8, g, :],
                                        by16[:, odd:16:2, late:late + 15],
                                        pe_col[rows, 8 * late:8 * late + 8].unsqueeze(2).to_broadcast([HD, 8, 15]),
                                        ALU.add))
    wait(pe, v_)
    wait(pe, consts_in)
    for kv in range(2):
        for m in range(2):
            for jp in range(16):
                mm = pe.matmul(ps_s[:, kv, m * 32:m * 32 + 30], compress_w(kv, jp, m),
                               flat[:, kv, jp, :, :].rearrange("p g c -> p (g c)"),
                               start=(jp == 0), stop=(jp == 15))
        PEs(mm)
        wait(act, p_)
        A(act.activation(hid_c[:, kv, :, :], ps_s[:, kv, 0:64].rearrange("p (m n) -> p m n", m=2)[:, :, 0:30], ACT.Silu))
    wait(pe, a_)
    for g in range(2):
        for m in range(2):
            mm = pe.matmul(ps_s[g * HD:(g + 1) * HD, 2, 0:15], vec("cw2_k", m * HD, HD),
                           hid_c[:, 0, m, g * 15:g * 15 + 15], start=(m == 0), stop=(m == 1))
    PEs(mm)
    for g in range(2):
        for m in range(2):
            mm = pe.matmul(ps_s[0:15, 3, g * HD:(g + 1) * HD], hid_c[:, 1, m, g * 15:g * 15 + 15],
                           vec("cw2_v", m * HD, HD), start=(m == 0), stop=(m == 1))
    PEs(mm)
    v_cmp = flat[0:15, 1, 0:5, :, :].rearrange("p a b c -> p (a b c)")[:, 0:2 * HD]
    wait(act, p_)
    wait(dve, a_, A(act.activation(kc, ps_s[:, 2, 0:15], ACT.Copy)))
    A(act.activation(v_cmp, ps_s[0:15, 3, 0:2 * HD], ACT.Copy))

    NT = 14
    for e in (p_, v_, a_, evac):
        wait(act, e)
    A(act.activation(yt[:, 0:NT, :], qk[:, 0:NT, :], ACT.Square))
    A(act.activation(kc_tmp, kc, ACT.Square))
    wait(pe, a_)
    banks = [ps_g[:, j, :] for j in range(4)] + [ps_s[:, j, :] for j in range(4)]
    for j in range(NT // 2):
        PEs(pe.matmul(banks[j], head_ones, yt[:, 2 * j:2 * j + 2, :], start=True, stop=True))
    PEs(pe.matmul(banks[7][:, 0:15], head_ones, kc_tmp, start=True, stop=True))
    wait(dve, p_)
    for j in range(NT // 2):
        V(dve.tensor_scalar(yt[:, 2 * j:2 * j + 2, :].rearrange("p a n -> p (a n)"), banks[j], 1.0 / HD, EPS,
                            ALU.mult, ALU.add))
    V(dve.tensor_scalar(kc_tmp, banks[7][:, 0:15], 1.0 / HD, EPS, ALU.mult, ALU.add))
    wait(act, v_)
    A(act.activation(yt[:, 0:NT, :], yt[:, 0:NT, :], ACT.Sqrt))
    A(act.activation(kc_tmp, kc_tmp, ACT.Sqrt))
    wait(dve, a_)
    V(dve.reciprocal(yt[:, 0:NT, :], yt[:, 0:NT, :]))
    V(dve.reciprocal(kc_tmp, kc_tmp))
    wait(dve, v_)
    for j in range(NT):
        V(dve.scalar_tensor_tensor(qk[:, j, :], qk[:, j, :], vec("qk_gain", j), yt[:, j, :], ALU.mult, ALU.mult))
    V(dve.scalar_tensor_tensor(kc, kc, vec("kc_gain"), kc_tmp, ALU.mult, ALU.mult))
    wait(pe, v_)
    for j in range(NT // 2):
        PEs(pe.matmul(banks[j], swap2[:], qk[:, 2 * j:2 * j + 2, :], start=True, stop=True))
    PEs(pe.matmul(banks[7][:, 0:15], swap2[:], kc, start=True, stop=True))
    wait(dve, p_)
    wait(dve, v_)
    cos2, sin2 = rope2[:, 0:1, :], rope2[:, 1:2, :]
    for j in range(NT // 2):
        V(dve.tensor_tensor(yt[:, 2 * j:2 * j + 2, :], banks[j].rearrange("p (a n) -> p a n", a=2),
                            sin2.to_broadcast([P, 2, S]), ALU.mult))
    V(dve.tensor_tensor(qk[:, 0:NT, :], qk[:, 0:NT, :], cos2.to_broadcast([P, NT, S]), ALU.mult))
    ends = slice(31, S, 16)
    V(dve.tensor_tensor(kc_tmp, banks[7][:, 0:15], rope2[:, 1, ends], ALU.mult))
    V(dve.tensor_tensor(kc, kc, rope2[:, 0, ends], ALU.mult))
    wait(dve, v_)
    V(dve.tensor_tensor(qk[:, 0:NT, :], qk[:, 0:NT, :], yt[:, 0:NT, :], ALU.add))
    V(dve.tensor_tensor(kc, kc, kc_tmp, ALU.add))
    wait(dve, v_)

    items = []
    no_sink = dict(sink=None, neg_sink=None)
    for tile in range(4):
        for half in range(2):
            head = half * 4 + tile
            rows = slice(half * HD, (half + 1) * HD)
            for qt in range(2):
                n = (qt + 1) * P
                common = dict(q=qk[rows, tile, qt * P:(qt + 1) * P], tile=tile, half=half, qt=qt, **no_sink)
                wgt = [branch[:, qt, 3 * head + b:3 * head + b + 1] for b in range(3)]
                items.append(dict(common, k=kc[rows, :], n=15, mask=causal[:, S + 15 * qt:S + 15 * qt + 15],
                                  weight=wgt[0], v=lambda kt, half=half: v_cmp[:, half * HD:(half + 1) * HD],
                                  first=True, last=False, open=(half == 0 and qt == 0), close=False))
                for b, (kt_, vc_) in enumerate(((12, 0), (13, P))):
                    items.append(dict(common, k=qk[rows, kt_, 0:n], n=n, mask=causal[:, S - n:S], weight=wgt[1 + b],
                                      v=lambda kt, c=vc_ + half * HD: v_tok[:, kt, c:c + HD],
                                      first=False, last=(b == 1), open=False,
                                      close=(b == 1 and half == 1 and qt == 1)))
    for j in range(4):
        for half in range(2):
            rows = slice(half * HD, (half + 1) * HD)
            for qt in range(2):
                n = (qt + 1) * P
                items.append(dict(q=qk[rows, 4 + j, qt * P:(qt + 1) * P], tile=4 + j, half=half, qt=qt,
                                  k=qk[rows, 8 + j, 0:n], n=n, mask=causal[:, S - n:S], weight=None, **no_sink,
                                  v=lambda kt, c=S + (2 * j + half) * HD: v_tok[:, kt, c:c + HD],
                                  first=True, last=True, open=(half == 0 and qt == 0),
                                  close=(half == 1 and qt == 1)))
    attention(items, hid, score_slots, prod)
    wait(act, sem_k)
    wait(dve, sem_c)
    wait(dve, sem_o)
    wait(dve, sem_t)

    ph_o = Phase(t["w_out"], 4, UNIT, features(h, NC, 2, S), add_to(x, S, 2),
                 *sum_squares(x, S, 2))
    ph_up.run(ph_o)
    merge.n += 12
    out_hi.n += 4
    wait(pe, merge)
    first = ffn_first("gu2", h, hid, 1)
    ph_o.run(first)
    wait(dve, evac)
    wait(act, evac)
    first.ready = norm2("g_ffn")
    ph_g = ffn(first, "gu2", "dn2", h, hid, 1,
               lambda: Phase(t["ple_gate"], 4, UNIT, feat, keep(gates, S, 2, ACT.Sigmoid)), into=x)
    wait(dve, evac)
    wait(act, evac)

    ph_g.ready = norm2("g_ple")
    wait(dve, a_, A(act.activation(hid[0][:, 0:2, :], p_in[:], ACT.Copy)))
    V(dve.tensor_tensor(hid[1][:, 0:2, :], p_in[:], hid[0][:, 0:2, :].bitcast(F32), ALU.subtract))

    def proj_unit(ul, slot, ready):
        w = [w_[slot][:].rearrange("p (k n) -> p k n", k=2) for w_ in (w_hi, w_lo)]
        for m in range(NC):
            for k in range(2):
                for n, (wp, ap) in enumerate(PARTS):
                    mm = pe.matmul(ps_g[:, m // 2, S * (m % 2):S * (m % 2) + S], w[wp][:, k, m * P:(m + 1) * P],
                                   hid[ap][:, k, 0:S], start=(k == 0 and n == 0), stop=(k == 1 and n == 2))
        return mm

    def proj_keep(ul, u, slot):
        wait(dve, unit_done, u + 1)
        dve.tensor_tensor(yt[:, 0:NC, :], gates[:, 0:NC, :], ps_g[:, :, :].rearrange("p a (b n) -> p (a b) n", b=2),
                          ALU.mult).then_inc(evac.sem, 1)
    ph_p = Phase(t["ple_proj"], 1, UNIT, proj_unit, proj_keep)
    ph_g.run(ph_p)
    wait(pe, evac)
    wait(pe, v_)
    wait(dve, evac)
    ph_p.run(None)
    wait(dve, evac)
    V(dve.tensor_tensor(x[:, :, 0:S], x[:, :, 0:S], yt[:, 0:NC, :], ALU.add))
    wait(sp, v_)
    stored = Count(nc, "stored")
    stored.inc(sp.dma_start(out, x[:, :, 0:S]), 16)
    wait(sp, stored)
    b2.close()
    mem.close()


def _units(w, kc, cols):
    import numpy as np
    K, N = w.shape
    assert K == kc * P and N % cols == 0
    return np.ascontiguousarray(w.reshape(kc, P, N // cols, cols).transpose(2, 1, 0, 3)
                                .reshape(N // cols, P, kc * cols))


def _chunked(v):
    return v.reshape(-1, P).T


def _fmajor(a):
    return a.T.reshape(-1, P, a.shape[0]).transpose(1, 0, 2)


def _paired(a, b):
    import numpy as np
    K = a.shape[0]
    return np.stack([a.reshape(K, -1, P), b.reshape(K, -1, P)], axis=2).reshape(K, -1)


def layout(i):
    import numpy as np
    f32 = np.float32
    t, cols, vec_at = {}, [], {}

    def add(name, a):
        vec_at[name] = sum(c.shape[1] for c in cols)
        cols.append(np.asarray(a, f32).reshape(P, -1))

    add("cond", np.stack([_chunked(i["c"][0]), _chunked(i["c_ctx"])], axis=2))
    add("b_mod", np.repeat(_chunked(i["b_mod"].reshape(-1))[:, :, None], 2, axis=2))
    add("norm_g", np.repeat(_chunked(i["norm_g"].reshape(-1))[:, :, None], 2, axis=2))
    add("conv_w", _chunked(i["conv_w"].reshape(-1)))
    add("sink", np.broadcast_to(i["attn_sink"].reshape(1, -1), (P, 16)))
    add("neg_sink", np.zeros((P, 16)))
    for name in ("g_mix", "g_ffn", "g_ple"):
        add(name, _chunked(i[name + "_2"][0]))
    two = lambda a: np.tile(a, 2)
    gains = [i["nsa_q_gain_2"][0]] * 4 + [i["moba_q_gain_2"][0]] * 4 + [i["moba_k_gain_2"][0]] * 4 \
        + [i["nsa_ks_gain_2"][0], i["nsa_kw_gain_2"][0]]
    add("qk_gain", np.stack([two(a) for a in gains], axis=1))
    add("kc_gain", two(i["nsa_kc_gain_2"][0]))
    for name in ("pe_k", "pe_v"):
        add(name, i[f"nsa_{name}_2"][0].reshape(16, P).T)
    for name in ("cw2_k", "cw2_v"):
        w2 = i["nsa_ck_w2_2" if name == "cw2_k" else "nsa_cv_w2_2"][0]
        add(name, w2.reshape(2, P, HD).transpose(1, 0, 2))
    f2 = (np.float32(500000.0) ** (-np.arange(8, dtype=f32) / np.float32(8))).astype(f32)
    add("inv_freq", np.tile(np.concatenate([f2, f2, np.zeros(HD - 16, f32)]), 2))
    add("any_block", (np.arange(P) >= 31).astype(f32))
    t["vecs"] = np.ascontiguousarray(np.concatenate(cols, axis=1))

    eye = np.eye(P, dtype=f32)
    head_ones = np.kron(np.eye(2), np.ones((HD, HD))).astype(f32)
    quarter = HD // 4

    def swap(pairs):
        m = np.zeros((P, P), f32)
        for base in (0, HD):
            for lo, hi in pairs:
                m[base + hi, base + lo] = -1.0
                m[base + lo, base + hi] = 1.0
        return m
    swap1 = swap([(b + j, b + quarter + j) for b in (0, 2 * quarter) for j in range(quarter)])
    t["mats"] = np.ascontiguousarray(np.stack([eye, np.ones((P, P), f32), head_ones, swap1], axis=1))
    t["swap2"] = swap([(j, 8 + j) for j in range(8)])
    tok = np.arange(S)
    inv = (np.float32(10000.0) ** (-np.arange(quarter, dtype=f32) / np.float32(quarter))).astype(f32)
    ang = np.stack([(tok // 64).astype(f32)[:, None] * inv, (tok % 64).astype(f32)[:, None] * inv], axis=1)
    ang = np.repeat(ang[:, :, None, :], 2, axis=2).reshape(S, HD)
    t["rope1"] = np.ascontiguousarray(np.stack([np.tile(np.cos(ang).T, (2, 1)), np.tile(np.sin(ang).T, (2, 1))], axis=1)).astype(f32)
    band = np.zeros((P, 2, T2), f32)
    for qt in range(2):
        off = np.abs(np.arange(S)[None, :] - (qt * P + np.arange(P))[:, None])
        band[:, qt, 0:S] = np.where(off <= 128, 0.0, NEG)
    t["band"] = band

    t["x"] = np.ascontiguousarray(_fmajor(i["x"][0]))
    t["ctx"] = np.ascontiguousarray(_fmajor(i["ctx"][0]))

    t["w_mod"] = np.concatenate([_units(i["w_mod"][l], NC, P) for l in range(2)]).reshape(-1, P, NC, P)
    n0, n1 = FFN_HALVES
    for l in range(2):
        for j in range(2):
            gu, dn = i["ffn_w_gu"][l, j], i["ffn_w_down"][l, j]
            t[f"gu{l}{j}"] = _units(_paired(gu[:, :D_FF], gu[:, D_FF:]), NC, 2 * P)
            t[f"dn{l}{j}a"] = _units(dn[:n0 * P], n0, P)
            t[f"dn{l}{j}b"] = _units(dn[n0 * P:], n1, P)
    cw = i["conv_w_in"][0]
    t["conv_cu"] = _units(_paired(cw[:, D:2 * D], cw[:, 2 * D:]), NC, 2 * P)
    t["conv_b"] = _units(cw[:, :D], NC, 2 * P)
    t["conv_out"] = _units(i["conv_w_out"][0], NC, 2 * P)
    wq = i["attn_w_qkv"][0]
    heads = [(tile // 4) * 8 + half * 4 + tile % 4 for tile in range(8) for half in range(2)]
    t["attn_q"] = _units(wq[:, :D].reshape(D, 16, HD)[:, heads].reshape(D, D), NC, 2 * P)
    t["attn_kv"] = _units(wq[:, D:], NC, 2 * P)
    t["attn_o"] = _units(i["attn_w_o"][0].reshape(16, HD, D)[heads].reshape(D, D), NC, 2 * P)

    tri = np.where(np.arange(P)[None, :] <= np.arange(P)[:, None], 0.0, NEG)
    blocks = [np.where(16 * np.arange(15)[None, :] + 31 <= (qt * P + np.arange(P))[:, None], 0.0, NEG) for qt in range(2)]
    t["causal"] = np.concatenate([np.zeros((P, P)), tri] + blocks, axis=1).astype(f32)
    t["positions"] = np.ascontiguousarray(i["positions_2"][0])
    t["p"] = np.ascontiguousarray(_fmajor(i["p_2"][0, 0]))
    w = i["w_in_2"][0]
    cuts = np.cumsum([0, 512] + [128] * 6 + [24] + [512] * 3 + [D, D])
    q_n, kc_, vc_, ks_, vs_, kw_, vw_, g_n, q_m, k_m, v_m, g_a, g_b = (w[:, a:b] for a, b in zip(cuts[:-1], cuts[1:]))
    order = [half * 4 + tile for tile in range(4) for half in range(2)]
    twice = lambda a: [a[:, 0:HD], a[:, 0:HD], a[:, HD:P], a[:, HD:P]]
    cat = lambda parts: np.concatenate(parts, axis=1)
    t["w_in_a"] = _units(cat([q_n.reshape(D, 8, HD)[:, order].reshape(D, 512), q_m, k_m, ks_, kw_] + twice(kc_)), NC, 2 * P)
    t["w_in_b"] = _units(cat(twice(vc_) + [vs_, vw_]), NC, 2 * P)
    t["w_in_c"] = _units(v_m, NC, 2 * P)
    t["w_in_d"] = _units(cat([g_a, g_b]), NC, 2 * P)
    t["gate_n"] = _units(g_n, NC, 24)[0]
    t["cw1"] = np.concatenate([_units(i[n][0][a:a + D], NC, 2 * P) for n in ("nsa_ck_w1_2", "nsa_cv_w1_2") for a in (0, D)])
    up_n = i["w_up_nsa_2"][0].reshape(8, HD, D)[order].reshape(512, D)
    t["w_up"] = _units(np.concatenate([up_n, i["w_up_moba_2"][0]]), NC, 2 * P)
    t["w_out"] = _units(i["w_out_2"][0], NC, 2 * P)
    gu, dn = i["w_ffn_in_2"][0], i["w_ffn_out_2"][0]
    t["gu2"] = _units(_paired(gu[:, :D_FF], gu[:, D_FF:]), NC, 2 * P)
    t["dn2a"], t["dn2b"] = _units(dn[:n0 * P], n0, P), _units(dn[n0 * P:], n1, P)
    t["ple_gate"] = _units(i["w_ple_gate_2"][0], NC, 2 * P)
    t["ple_proj"] = _units(i["w_ple_proj_2"][0], 2, D)
    return t, vec_at


def kernel(**inputs):
    import numpy as np
    import concourse.bacc as bacc
    from concourse.bass_utils import run_bass_kernel_spmd

    arrays, vec_at = layout({k: np.asarray(v) for k, v in inputs.items()})
    nc = bacc.Bacc("TRN2", target_bir_lowering=False, num_devices=1)
    t = {n: nc.dram_tensor(f"in_{n}", a.shape, mybir.dt.from_np(a.dtype), kind="ExternalInput").ap()
         for n, a in arrays.items()}
    out = nc.dram_tensor("out", (P, NC, S), F32, kind="ExternalOutput").ap()
    build(nc, t, out, vec_at)
    r = run_bass_kernel_spmd(nc, [{f"in_{n}": a for n, a in arrays.items()}], core_ids=[0])
    return r.results[0]["out"].transpose(2, 1, 0).reshape(1, S, D)
```

```python
from contextlib import ExitStack

import concourse.bass as bass
from concourse import mybir

F32 = mybir.dt.float32
F32R = mybir.dt.float32r
I32 = mybir.dt.int32
ALU = mybir.AluOpType
ACT = mybir.ActivationFunctionType
ENG = mybir.EngineType

P = 128
D = 1024
NC = D // P
S = 256
T2 = 2 * S
D_FF = 2816
FFN_HALVES = (12, 10)
assert sum(FFN_HALVES) * P == D_FF
N_MOD = 9
HD = 64
EPS = 1e-6
CREDIT = 2
UNIT = 2048
NEG = -1e30
TWO_PI_HI = 6.28125
TWO_PI_MID = 0.0019350051879882812
TWO_PI_LO = 3.019916050561733e-07
PI_SAFE = 3.1415925


class Count:

    def __init__(self, nc, name):
        self.sem = nc.alloc_semaphore(name)
        self.n = 0

    def inc(self, ins, by=1):
        ins.then_inc(self.sem, by)
        self.n += by
        return self.n


def wait(eng, count, value=None):
    value = count.n if value is None else value
    if not isinstance(value, int) or value > 0:
        eng.wait_ge(count.sem, value)


def build(nc, t, out, vec_at):
    pe, dve, act, sp, pool = nc.tensor, nc.vector, nc.scalar, nc.sync, nc.gpsimd
    mem = ExitStack()

    def sb(name, shape, dt=F32, stack=None):
        return (stack or mem).enter_context(nc.sbuf_tensor(name, list(shape), dt))

    n_vec = t["vecs"].shape[1]
    vecs = sb("vecs", [P, n_vec])
    mats = sb("mats", [P, 4, P])
    swap2 = sb("swap2", [P, P])
    ident, ones, head_ones, swap1 = (mats[:, j, :] for j in range(4))
    w_raw = [sb(f"w_raw{j}", [P, UNIT]) for j in range(2)]
    w_hi = [sb(f"w_hi{j}", [P, UNIT], F32R) for j in range(2)]
    w_lo = [sb(f"w_lo{j}", [P, UNIT], F32R) for j in range(2)]
    x = sb("x", [P, NC, T2])
    gate_tmp = sb("gate_tmp", [P, 2, T2])
    prod = sb("prod", [P, 2, T2])
    sq = sb("sq", [P, 2, T2])
    ssum = sb("ssum", [P, T2])
    tok = sb("tok", [P, 9])
    mod_acc = sb("mod_acc", [P, 2, 2, P])
    stats = mod_acc[:].rearrange("p a b n -> p (a b n)")[:, 0:5 * 64].rearrange("p (a n) -> p a n", n=64)
    y = sb("y", [P, NC, T2])
    ps_g = mem.enter_context(nc.psum_tensor("ps_g", [P, 4, 512], F32))
    ps_s = mem.enter_context(nc.psum_tensor("ps_s", [P, 4, 512], F32))

    def vec(name, j=0, n=1):
        a = vec_at[name] + j
        return vecs[:, a:a + n]

    loaded = [Count(nc, f"loaded{j}") for j in range(2)]
    split_hi = Count(nc, "split_hi")
    split_lo = Count(nc, "split_lo")
    unit_done = Count(nc, "unit_done")
    evac = Count(nc, "evac")
    gate_made = Count(nc, "gate_made")
    out_hi = Count(nc, "out_hi")
    out_lo = Count(nc, "out_lo")
    consts_in = Count(nc, "consts_in")
    v_ = Count(nc, "vector_steps")
    a_ = Count(nc, "scalar_steps")
    p_ = Count(nc, "tensor_steps")
    g_ = Count(nc, "pool_steps")
    mod_loaded = [Count(nc, f"mod_loaded{j}") for j in range(2)]
    mod_done = Count(nc, "mod_done")
    mod_kept = Count(nc, "mod_kept")
    mod_step = Count(nc, "mod_step")
    sq_made = Count(nc, "sq_made")
    sq_added = Count(nc, "sq_added")
    pool_half = Count(nc, "pool_half")

    def V(ins):
        return v_.inc(ins)

    def A(ins):
        return a_.inc(ins)

    def PEs(ins):
        return p_.inc(ins)

    for c in (evac, out_lo):
        for _ in range(CREDIT):
            c.inc(dve.memset(stats[:, 0, 0:1], 0.0))
            wait(dve, c)
    for _ in range(CREDIT):
        wait(pool, sq_added, sq_added.inc(pool.memset(ssum[:, 0:1], 0.0)))
    V(dve.memset(tok[:], 1.0))

    x_in = Count(nc, "x_in")
    for dst, src in ((vecs[:], t["vecs"]), (mats[:], t["mats"]), (swap2[:], t["swap2"])):
        consts_in.inc(sp.dma_start(dst, src), 16)
    for e in (pe, dve, act):
        wait(e, consts_in)

    class Phase:

        def __init__(self, w, n_units, elems, pe_unit, empty, finish=None, pool=None, mods=False):
            self.w, self.n, self.elems, self.pe_unit = w, n_units, elems, pe_unit
            self.empty, self.finish, self.pool, self.mods = empty, finish, pool, mods
            self.ready = None
            self.u0 = loaded[0].n // 16 * 2
            self.nb = (n_units + 1) // 2
            self.slots = min(2, n_units)
            self.load()

        def load(self):
            g0 = mods_sent[0]

            def body(i):
                for j in range(self.slots):
                    wait(sp, split_lo, 2 * (self.u0 + 2 * i + j) - 2)
                    sp.dma_start(w_raw[j][:, 0:self.elems], self.w[2 * i + j]).then_inc(loaded[j].sem, 16)
                    while mods_pending:
                        mod_load(*mods_pending.pop())
                    g = g0 + 2 * i + j
                    if self.mods and not (isinstance(g, int) and g == mods_ahead[0]):
                        mod_load(g, 1 - j)
            body(0)
            if self.nb > 1:
                with nc.Fori(1, self.nb, engines=(ENG.SP,)) as i:
                    body(i)
            for j in range(2):
                loaded[j].n += 16 * self.nb
            if self.mods:
                mods_sent[0] += self.n
            if self.mods == "then a gap":
                mods_ahead[0] = mods_sent[0]
                mods_pending.append((mods_ahead[0], mods_ahead[0] % 2))

        def split(self, ul, slot):
            u = self.u0 + ul
            half = self.elems // 2
            wait(act, loaded[slot], (u - slot) * 8 + 16)
            wait(act, unit_done, u - 1)
            for n in range(2):
                cols = slice(n * half, (n + 1) * half)
                act.activation(w_hi[slot][:, cols], w_raw[slot][:, cols], ACT.Copy).then_inc(split_hi.sem, 1)
            for n in range(2):
                cols = slice(n * half, (n + 1) * half)
                wait(dve, split_hi, 2 * u + n + 1)
                dve.tensor_tensor(w_lo[slot][:, cols], w_raw[slot][:, cols], w_hi[slot][:, cols].bitcast(F32),
                                  ALU.subtract).then_inc(split_lo.sem, 1)

        def multiply(self):
            g0 = N_FIRST + mod_kept.n

            def body(i, ready=None):
                for j in range(self.slots):
                    u = self.u0 + 2 * i + j
                    wait(pe, split_lo, 2 * u + 2)
                    wait(pe, evac, CREDIT + u - 1)
                    self.pe_unit(2 * i + j, j, ready if j == 0 else None).then_inc(unit_done.sem, 1)
                    if self.mods:
                        mod_sum(g0 + 2 * i + j, 1 - j)
            body(0, self.ready)
            if self.nb > 1:
                with nc.Fori(1, self.nb, engines=(ENG.PE,)) as i:
                    body(i)

        def run(self, after=None, put_off=False):
            self.multiply()
            g0 = N_FIRST + mod_kept.n

            def slot_work(ul, j, following, ul_following, last=False):
                self.empty(ul, self.u0 + ul, j)
                if following is not None:
                    if last and put_off:
                        deferred.append(lambda: following.split(ul_following, j))
                    else:
                        following.split(ul_following, j)
                if self.finish is not None:
                    self.finish(ul, self.u0 + ul, j)
                if self.mods:
                    mod_keep(g0 + ul, 1 - j)
                    if last and put_off:
                        deferred.append(lambda: mod_products(g0 + ul + 1, j))
                    else:
                        mod_products(g0 + ul + 1, j)
            if self.nb > 1:
                with nc.Fori(0, self.nb - 1, engines=(ENG.DVE, ENG.Activation)) as i:
                    for j in range(2):
                        slot_work(2 * i + j, j, self, 2 * i + 2 + j)
            split_hi.n = split_lo.n = 2 * (self.u0 + self.n)
            unit_done.n = self.u0 + self.n
            for j in range(self.slots):
                ul = 2 * self.nb - 2 + j
                slot_work(ul, j, after if after is not None and j < after.n else None, j, j == 1)
            if self.pool is not None:
                if self.nb > 1:
                    with nc.Fori(0, self.nb, engines=(ENG.Pool,)) as i:
                        for j in range(2):
                            self.pool(2 * i + j, j)
                else:
                    for j in range(self.slots):
                        self.pool(j, j)
                sq_made.n += self.n
                sq_added.n += self.n
            evac.n = CREDIT + self.u0 + self.n
            if self.mods:
                mod_done.n += self.n
                mod_kept.n += self.n

        def run_beside(self, sides, after):
            for ul in range(self.n):
                u, j = self.u0 + ul, ul % 2
                wait(pe, split_lo, 2 * u + 2)
                wait(pe, evac, CREDIT + u - 1)
                self.pe_unit(ul, j, None).then_inc(unit_done.sem, 1)
                self.empty(ul, u, j)
                assert self.finish is None
                if ul + 2 < self.n:
                    self.split(ul + 2, j)
                else:
                    after.split(ul + 2 - self.n, j)
                sides[ul]()
            split_hi.n = split_lo.n = 2 * (self.u0 + self.n)
            unit_done.n = self.u0 + self.n
            evac.n = CREDIT + self.u0 + self.n

        def first_splits(self):
            for j in range(self.slots):
                self.split(j, j)

    N_FIRST = 2 * NC + 1
    N_MODS = 2 * N_MOD * NC
    STEPS = 2 * NC
    BY_PE = 12
    SUMMED = N_FIRST - BY_PE
    mods_pending = []
    mod_raw_free = []
    deferred = []

    def catch_up():
        while deferred:
            deferred.pop(0)()

    mods_sent = [N_FIRST]
    mods_ahead = [N_FIRST]
    mod_raw = [sb(f"mod_raw{j}", [P, NC, P]) for j in range(2)]
    mod_sb = sb("mod_sb", [P, N_MODS, 2])
    cond = sb("cond", [P, NC, 2])
    b_mod = vecs[:, vec_at["b_mod"]:vec_at["b_mod"] + 2 * N_MODS].rearrange("p (m s) -> p m s", s=2)

    def mod_load(g, slot):
        if isinstance(g, int) and g == N_FIRST + 1:
            wait(sp, v_, mod_raw_free[0])
        wait(sp, mod_step, STEPS * (g - N_FIRST - 1))
        sp.dma_start(mod_raw[slot][:], t["w_mod"][g]).then_inc(mod_loaded[slot].sem, 16)

    def accumulate(slot, w, signal, signalled):
        for k in range(NC):
            for s in range(2):
                acc = mod_acc[:, slot, s, :]
                if k == 0:
                    ins = dve.tensor_scalar(acc, w[:, 0, :], cond[:, 0, s:s + 1], None, ALU.mult)
                else:
                    wait(dve, signal, signalled + 2 * (k - 1) + s + 1)
                    ins = dve.scalar_tensor_tensor(acc, w[:, k, :], cond[:, k, s:s + 1], acc, ALU.mult, ALU.add)
                ins.then_inc(signal.sem, 1)

    def partition_sum(bank, col, slot):
        for s in range(2):
            mm = pe.matmul(ps_s[:, bank, col + s:col + s + 1], mod_acc[:, slot, s, :], ones[:, 0:1],
                           start=True, stop=True)
        return mm

    def mod_products(g, slot):
        wait(dve, mod_loaded[slot], (g - N_FIRST - 1 - slot) * 8 + 16)
        wait(dve, mod_done, SUMMED + g - N_FIRST - 1)
        accumulate(slot, mod_raw[slot][:], mod_step, STEPS * (g - N_FIRST))

    def mod_sum(g, slot):
        wait(pe, mod_step, STEPS * (g - N_FIRST + 1))
        wait(pe, mod_kept, g - N_FIRST - 1)
        partition_sum(2 + slot, 0, slot).then_inc(mod_done.sem, 1)

    def mod_keep(g, slot):
        wait(dve, mod_done, SUMMED + g - N_FIRST + 1)
        dve.tensor_tensor(mod_sb[:, g, :], ps_s[:, 2 + slot, 0:2], b_mod[:, g, :], ALU.add).then_inc(mod_kept.sem, 1)

    def mod_first(buffers, turn, start, between):
        def load(dst, g, n):
            c = Count(nc, f"w_mod_in{g}")
            c.inc(sp.dma_start(dst, t["w_mod"][g:g + n].rearrange("m p k n -> p m k n")), 16)
            return c
        src = [(buffers[3][:, m], load(buffers[3], BY_PE, 4) if m == 0 else None) for m in range(4)]
        src += [(mod_raw[m][:], load(mod_raw[m][:].unsqueeze(1), BY_PE + 4 + m, 1)) for m in range(2)]
        assert len(src) == SUMMED + 1
        arrived = [load(buffers[0], 0, 4), load(buffers[1], 4, 4)]
        for dst, half in ((x[:, :, 0:S], t["x"]), (x[:, :, S:T2], t["ctx"])):
            x_in.inc(sp.dma_start(dst, half), 16)
        arrived.append(load(buffers[2], 8, 4))
        ready = []
        for n, (w, c) in enumerate(src):
            if c is not None:
                wait(dve, c)
            wait(dve, mod_done, n - 1)
            last = n == SUMMED
            accumulate(n % 2, w, mod_step if last else v_, 0 if last else v_.n)
            if not last:
                v_.n += STEPS
                ready.append(v_.n)

        mod_raw_free.append(v_.n)
        start()

        def add_up(n):
            wait(pe, v_, ready[n])
            mod_done.inc(partition_sum(2, 2 * (BY_PE + n), n % 2))

        add_up(0)
        for n, due in enumerate(((1, 2), (3,), (4,))):
            wait(pe, arrived[n])
            for k in range(NC):
                mm = pe.matmul(ps_s[0:2, n % 2, :], cond[:, k, :], buffers[n][:, :, k, :],
                               start=(k == 0), stop=(k == NC - 1))
            wait(act, p_, PEs(mm))
            turned = A(act.activation(turn[0:2, n, :], ps_s[0:2, n % 2, :], ACT.Copy))
            between[n]()
            for m in due:
                add_up(m)
            wait(pe, a_, turned)
            for m in range(4):
                mm = pe.transpose(ps_s[:, 2, 2 * (4 * n + m):2 * (4 * n + m) + 2], turn[0:2, n, m * P:(m + 1) * P],
                                  ident[0:2, 0:2])
        wait(dve, p_, PEs(mm))
        wait(dve, mod_done)
        V(dve.tensor_tensor(mod_sb[:, 0:N_FIRST, :], ps_s[:, 2, 0:2 * N_FIRST].rearrange("p (m s) -> p m s", s=2),
                            b_mod[:, 0:N_FIRST, :], ALU.add))
        wait(dve, v_)

    ring = [gate_tmp[:, 0, :], gate_tmp[:, 1, :], prod[:, 0, :], prod[:, 1, :]]

    def squares_of(c, T, hist):
        if c == 0:
            wait(act, sq_added)
            sq_made.inc(act.activation(ssum[:, 0:T], x[:, 0, 0:T], ACT.Square))
            hist.append(sq_added.n)
            return
        wait(act, sq_added, hist[max(c - 2, 0)])
        sq_made.inc(act.activation(sq[:, c % 2, 0:T], x[:, c, 0:T], ACT.Square))
        wait(pool, sq_made)
        wait(pool, sq_added)
        hist.append(sq_added.inc(pool.tensor_tensor(ssum[:, 0:T], ssum[:, 0:T], sq[:, c % 2, 0:T], ALU.add)))

    def rstd_from_sums(T, meanwhile=None):
        nt = T // P
        A(act.activation(tok[:, 8:9], tok[:, 8:9], ACT.Sqrt))
        if meanwhile is not None:
            meanwhile()
        wait(pe, sq_added)
        for j in range(nt):
            mm = pe.matmul(ps_s[:, 0, j:j + 1], ssum[:, j * P:(j + 1) * P], ones[:, 0:1], start=True, stop=True)
        wait(dve, p_, PEs(mm))
        wait(act, v_, V(dve.tensor_scalar(tok[:, 0:nt], ps_s[:, 0, 0:nt], 1.0 / D, EPS, ALU.mult, ALU.add)))
        wait(dve, a_, A(act.activation(tok[:, 0:nt], tok[:, 0:nt], ACT.Sqrt)))
        wait(pe, v_, V(dve.reciprocal(tok[:, 4:4 + nt], tok[:, 0:nt])))
        for j in range(nt):
            mm = pe.matmul(ps_s[:, 1, j * P:(j + 1) * P], tok[:, 4 + j:5 + j].to_broadcast([P, P]), ident,
                           start=True, stop=True)
        wait(dve, p_, PEs(mm))
        return ps_s[:, 1, 0:T]

    def norm_in(h_hi, h_lo, streams, scale, shift=None):
        T = S * streams
        r = rstd_from_sums(T)
        wait(dve, out_lo)
        wait(dve, evac)
        wait(dve, v_)
        wait(dve, a_)
        multiplied, high, low = [], [], []

        def multiply(c):
            if c >= 4:
                wait(dve, v_, low[c - 4])
            if shift is not None:
                ins = dve.tensor_tensor(ring[c % 4][:, 0:T], x[:, c, 0:T], r, ALU.mult)
            else:
                ins = dve.scalar_tensor_tensor(ring[c % 4][:, 0:T], x[:, c, 0:T], scale(c, 0), r, ALU.mult, ALU.mult)
            multiplied.append(V(ins))

        def to_high(c):
            buf = ring[c % 4]
            wait(act, v_, multiplied[c])
            if shift is not None:
                if streams == 2:
                    wait(pool, v_, multiplied[c])
                    z = buf[:, S:T2]
                    g_.inc(pool.tensor_scalar(z, z, scale(c, 1), shift(c, 1), ALU.mult, ALU.add))
                z_n = g_.n
                A(act.activation(buf[:, 0:S], buf[:, 0:S], ACT.Identity, bias=shift(c, 0), scale=scale(c, 0)))
                wait(act, a_)
                wait(act, g_, z_n)
            high.append(A(act.activation(h_hi[:, c, 0:T], buf[:, 0:T], ACT.Copy)))

        def to_low(c):
            wait(dve, a_, high[c])
            low.append(V(dve.tensor_tensor(h_lo[:, c, 0:T], ring[c % 4][:, 0:T], h_hi[:, c, 0:T].bitcast(F32),
                                           ALU.subtract)))
        multiply(0)
        for c in range(NC + 1):
            if c + 1 < NC:
                multiply(c + 1)
            if c < NC:
                to_high(c)
            if c > 0:
                to_low(c - 1)
        return lambda k: wait(pe, v_, low[k])

    def norm_out(streams, scale):
        T = S * streams
        wait(act, evac)
        wait(act, out_lo)
        parts = [slice(S * s, S * s + S) for s in range(streams)]
        scaled, multiplied, added, hist = [], [], [], []

        def to_scaled(c):
            if c >= 4:
                wait(act, v_, added[c - 4])
            for s, cols in enumerate(parts):
                A(act.activation(ring[c % 4][:, cols], y[:, c, cols], ACT.Copy, scale=scale(c, s)))
            scaled.append(a_.n)

        def multiply(c):
            buf = ring[c % 4][:, 0:T]
            wait(dve, a_, scaled[c])
            multiplied.append(V(dve.tensor_tensor(buf, buf, r, ALU.mult)))

        def ahead():
            wait(act, v_)
            to_scaled(0)
            to_scaled(1)
        r = rstd_from_sums(T, ahead)
        wait(act, p_)
        multiply(0)
        for c in range(NC):
            if c + 1 < NC:
                multiply(c + 1)
            wait(dve, v_, multiplied[c])
            added.append(V(dve.tensor_tensor(x[:, c, 0:T], x[:, c, 0:T], ring[c % 4][:, 0:T], ALU.add)))
            if c + 2 < NC:
                to_scaled(c + 2)
            wait(act, v_, added[c])
            squares_of(c, T, hist)

    PARTS = ((0, 0), (0, 1), (1, 0))

    def features(acts, kc, mt, T, k0=0):
        def unit(ul, slot, ready=None):
            w = [w_[slot][:, 0:kc * mt * P].rearrange("p (k n) -> p k n", k=kc) for w_ in (w_hi, w_lo)]
            for m in range(mt):
                for k in range(kc):
                    if ready is not None and m == 0:
                        ready(k)
                    for n, (wp, ap) in enumerate(PARTS):
                        mm = pe.matmul(ps_g[:, 2 * slot + m, 0:T], w[wp][:, k, m * P:(m + 1) * P],
                                       acts[ap][:, k0 + k, 0:T], start=(k == 0 and n == 0),
                                       stop=(k == kc - 1 and n == 2))
            return mm
        return unit

    def tokens(acts, n_tiles):
        def unit(ul, slot, ready=None):
            w = [w_[slot][:, 0:UNIT].rearrange("p (k n) -> p k n", k=NC) for w_ in (w_hi, w_lo)]
            for i in range(n_tiles):
                for k in range(NC):
                    for n, (wp, ap) in enumerate(PARTS):
                        mm = pe.matmul(ps_g[:, 2 * slot + i // 2, S * (i % 2):S * (i % 2) + S],
                                       acts[ap][:, k, i * P:(i + 1) * P], w[wp][:, k, :],
                                       start=(k == 0 and n == 0), stop=(k == NC - 1 and n == 2))
            return mm
        return unit

    def gated_split(dst, T, func):
        made, lo, hi = gate_made.n, out_lo.n, out_hi.n

        def empty(ul, u, slot):
            wait(act, unit_done, u + 1)
            wait(act, evac, CREDIT + u - 1)
            act.activation(gate_tmp[:, slot, 0:T], ps_g[:, 2 * slot, 0:T], func).then_inc(gate_made.sem, 1)
            wait(dve, gate_made, made + ul + 1)
            wait(dve, out_lo, lo + ul - 1)
            dve.tensor_tensor(prod[:, slot, 0:T], gate_tmp[:, slot, 0:T], ps_g[:, 2 * slot + 1, 0:T],
                              ALU.mult).then_inc(evac.sem, 1)

        def finish(ul, u, slot):
            wait(act, evac, CREDIT + u + 1)
            act.activation(dst[0][:, ul, 0:T], prod[:, slot, 0:T], ACT.Copy).then_inc(out_hi.sem, 1)
            wait(dve, out_hi, hi + ul + 1)
            dve.tensor_tensor(dst[1][:, ul, 0:T], prod[:, slot, 0:T], dst[0][:, ul, 0:T].bitcast(F32),
                              ALU.subtract).then_inc(out_lo.sem, 1)
        return empty, finish

    def keep(dst, T, mt=2, func=ACT.Copy):
        def empty(ul, u, slot):
            wait(act, unit_done, u + 1)
            act.activation(dst[:, bass.ds(ul * mt, mt), 0:T], ps_g[:, 2 * slot:2 * slot + mt, 0:T],
                           func).then_inc(evac.sem, 1)
        return empty

    def add_to(dst, T, mt=1):
        def empty(ul, u, slot):
            wait(dve, unit_done, u + 1)
            d = dst[:, bass.ds(ul * mt, mt), 0:T]
            dve.tensor_tensor(d, d, ps_g[:, 2 * slot:2 * slot + mt, 0:T], ALU.add).then_inc(evac.sem, 1)
        return empty

    def sum_squares(dst, T, mt):
        made, added = sq_made.n, sq_added.n
        whole = mt * T == 2 * T2

        def where(slot):
            if whole:
                return sq[:]
            return sq[:, slot, 0:mt * T].rearrange("p (m n) -> p m n", m=mt)
        wait(pool, p_)
        wait(pool, v_)
        wait(pool, g_, g_.inc(pool.memset(ssum[:, 0:T], 0.0)))

        def finish(ul, u, slot):
            wait(act, evac, CREDIT + u + 1)
            wait(act, sq_added, added + ul - (0 if whole else 1))
            act.activation(where(slot), dst[:, bass.ds(ul * mt, mt), 0:T], ACT.Square).then_inc(sq_made.sem, 1)

        def pool_add(ul, slot):
            wait(pool, sq_made, made + ul + 1)
            for m in range(mt):
                ins = pool.tensor_tensor(ssum[:, 0:T], ssum[:, 0:T], where(slot)[:, m, :], ALU.add)
                if m == mt - 1:
                    ins.then_inc(sq_added.sem, 1)
                else:
                    ins.then_inc(pool_half.sem, 1)
                    wait(pool, pool_half, half0 + ul + 1)
            wait(pool, sq_added, added + ul + 1)
        half0 = pool_half.n
        if mt == 2:
            pool_half.n += NC // 2
        return finish, pool_add

    def ffn_first(w_gu, acts, hid, streams, mods=False):
        return Phase(t[w_gu], FFN_HALVES[0], UNIT, features(acts, NC, 2, S * streams),
                     *gated_split(hid, S * streams, ACT.Silu), mods=mods)

    def ffn(gu0, w_gu, w_down, acts, hid, streams, following, mods=False, into=None):
        T = S * streams
        n0, n1 = FFN_HALVES
        dst = y if into is None else into

        def hidden(n):
            base = out_lo.n

            def ready(k):
                wait(pe, out_lo, base + k + 1)
            gate_made.n += n
            out_hi.n += n
            out_lo.n += n
            return ready
        dn0 = Phase(t[w_down + "a"], NC, n0 * P, features(hid, n0, 1, T),
                    keep(y, T, 1) if into is None else add_to(into, T, 1), mods=mods)
        gu0.run(dn0)
        dn0.ready = hidden(n0)
        gu1 = Phase(t[w_gu][n0:n0 + n1], n1, UNIT, features(acts, NC, 2, T), *gated_split(hid, T, ACT.Silu),
                    mods=mods)
        dn0.run(gu1)
        dn1 = Phase(t[w_down + "b"], NC, n1 * P, features(hid, n1, 1, T), add_to(dst, T, 1),
                    *sum_squares(dst, T, 1), mods=mods)
        gu1.run(dn1)
        dn1.ready = hidden(n1)
        first = following()
        dn1.run(first, put_off=True)
        return first

    ab = sb("ab", [P, 2, NC, 2])
    b1 = ExitStack()
    h = [sb(f"h{j}", [P, NC, T2], F32R, b1) for j in range(2)]
    wide = sb("wide", [P, NC, 2, S + 2], F32, b1)
    band = mod_raw[0][:].rearrange("p a b -> p (a b)").rearrange("p (q n) -> p q n", q=2)
    rope1 = mod_raw[1][:, 0:4, :].rearrange("p a b -> p (a b)").rearrange("p (q n) -> p q n", q=2)
    score_slots = [gate_tmp[:, 0, :], gate_tmp[:, 1, :], sq[:, 0, :], sq[:, 1, :]]

    wait(pe, a_, A(act.activation(cond[:], vec("cond", 0, 2 * NC).rearrange("p (k s) -> p k s", s=2), ACT.Silu)))
    wait(dve, a_)
    wait(act, v_)
    with ExitStack() as early:
        by_four = [y[:].rearrange("p a (b n) -> p (a b) n", n=P).rearrange("p (m k) n -> p m k n", m=4)]
        by_four += [sb(f"w_mod{j}", [P, 4, NC, P], F32, early)[:] for j in range(3)]
        first, hist = [], []

        def start():
            first.append(Phase(t["gu00"], FFN_HALVES[0], UNIT, None, None, mods=True))

        def some_squares(chunks):
            wait(act, x_in)
            for c in chunks:
                squares_of(c, T2, hist)
        mod_first(by_four, wide[:].rearrange("p a b c -> p (a b c)")[:, 0:3 * 4 * P]
                  .rearrange("p (n m) -> p n m", n=3), start,
                  (lambda: some_squares(range(4)), lambda: some_squares(range(4, NC)), lambda: first[0].first_splits()))

    hid = [sb(f"hid{j}", [P, FFN_HALVES[0], T2], F32R, b1) for j in range(2)]

    def mod_at(layer, k):
        a = (layer * N_MOD + k) * NC
        return mod_sb[:, a:a + NC, :]

    def g_at(layer, n):
        a = vec_at["norm_g"] + (layer * 6 + n) * 2 * NC
        return vecs[:, a:a + 2 * NC].rearrange("p (c s) -> p c s", s=2)

    def adaln(layer, k, n, weight, streams):
        def before():
            wait(dve, mod_kept)
            V(dve.scalar_tensor_tensor(ab[:, 0], mod_at(layer, k + 1), 1.0, g_at(layer, n), ALU.add, ALU.mult))
            wait(act, v_)
            ready = norm_in(h[0], h[1], streams, lambda c, s: ab[:, 0, c, s:s + 1],
                            lambda c, s: mod_at(layer, k)[:, c, s:s + 1])
            catch_up()
            return ready

        def after(streams=streams):
            wait(dve, mod_kept)
            V(dve.scalar_tensor_tensor(ab[:, 1], mod_at(layer, k + 2), weight, g_at(layer, n + 1),
                                       ALU.mult, ALU.mult))
            norm_out(streams, lambda c, s: ab[:, 1, c, s:s + 1])
        return before, after

    first = first[0]
    first.pe_unit = features(h, NC, 2, T2)
    first.empty, first.finish = gated_split(hid, T2, ACT.Silu)
    wait(dve, x_in)
    before, after = adaln(0, 0, 0, 0.5, 2)
    first.ready = before()

    conv_step = Count(nc, "conv_step")

    def conv_first():
        made, steps = gate_made.n, conv_step.n

        def product_wide(ul, u, slot):
            wait(act, unit_done, u + 1)
            wait(act, evac, CREDIT + u - 1)
            act.activation(gate_tmp[:, slot, :], ps_g[:, 2 * slot, :], ACT.Copy).then_inc(gate_made.sem, 1)
            wait(dve, gate_made, made + ul + 1)
            dve.tensor_tensor(wide[:, ul, :, 1:S + 1],
                              gate_tmp[:, slot, :].rearrange("p (s n) -> p s n", s=2),
                              ps_g[:, 2 * slot + 1, :].rearrange("p (s n) -> p s n", s=2),
                              ALU.mult).then_inc(evac.sem, 1)

        def convolve(ul, u, slot):
            wait(dve, evac, CREDIT + u + 1)
            yc = y[:, ul, :].rearrange("p (s n) -> p s n", s=2)
            for n, tap in enumerate((1, 0, 2)):
                src = wide[:, ul, :, tap:tap + S]
                w_tap = vecs[:, bass.ds(ul + (vec_at["conv_w"] + tap * NC), 1)]
                if n == 0:
                    ins = dve.tensor_scalar(yc, src, w_tap, None, ALU.mult)
                else:
                    wait(dve, conv_step, steps + 3 * ul + n)
                    ins = dve.scalar_tensor_tensor(yc, src, w_tap, yc, ALU.mult, ALU.add)
                ins.then_inc(conv_step.sem, 1)
        return Phase(t["conv_cu"], NC, UNIT, features(h, NC, 2, T2), product_wide, convolve,
                     mods="then a gap")

    def conv_layer(c1, following):
        before, after = adaln(0, 3, 2, 1.0, 2)
        c1.ready = before()
        V(dve.memset(wide[:, :, :, 0:1], 0.0))
        V(dve.memset(wide[:, :, :, S + 1:S + 2], 0.0))
        wait(dve, v_)
        base, base_hi = out_lo.n, out_hi.n

        def times_b(ul, u, slot):
            wait(dve, unit_done, u + 1)
            wait(dve, out_lo, base + ul)
            dve.tensor_tensor(prod[:], y[:, bass.ds(2 * ul, 2), :], ps_g[:, 2 * slot:2 * slot + 2, :],
                              ALU.mult).then_inc(evac.sem, 1)

        def in_parts(ul, u, slot):
            wait(act, evac, CREDIT + u + 1)
            act.activation(hid[0][:, bass.ds(2 * ul, 2), :], prod[:], ACT.Copy).then_inc(out_hi.sem, 1)
            wait(dve, out_hi, base_hi + ul + 1)
            dve.tensor_tensor(hid[1][:, bass.ds(2 * ul, 2), :], prod[:],
                              hid[0][:, bass.ds(2 * ul, 2), :].bitcast(F32), ALU.subtract).then_inc(out_lo.sem, 1)
        c2 = Phase(t["conv_b"], NC // 2, UNIT, features(h, NC, 2, T2), times_b, in_parts)
        c1.run(c2)
        gate_made.n += NC
        conv_step.n += 3 * NC
        wait(dve, conv_step)
        c3 = Phase(t["conv_out"], NC // 2, UNIT, features(hid, NC, 2, T2), keep(y, T2), *sum_squares(y, T2, 2),
                   mods=True)
        c2.run(c3)
        out_hi.n += NC // 2
        out_lo.n += NC // 2
        wait(act, out_lo)
        c3.ready = lambda k: wait(pe, out_lo, base + k // 2 + 1)
        first = following()
        c3.run(first, put_off=True)
        after()
        return first

    first = ffn(first, "gu00", "dn00", h, hid, 2, conv_first, True)
    after()
    first = conv_layer(first, lambda: ffn_first("gu01", h, hid, 2, True))
    before, after = adaln(0, 6, 4, 0.5, 2)
    first.ready = before()
    first = ffn(first, "gu01", "dn01", h, hid, 2, lambda: ffn_first("gu10", h, hid, 2, True), True)
    after()

    before, after = adaln(1, 0, 0, 0.5, 2)
    first.ready = before()
    wf = wide[:].rearrange("p a b c -> p (a b c)")
    k_raw = wf[:, 0:4 * S].rearrange("p (a n) -> p a n", a=2)
    v_tok = wf[:, 4 * S:8 * S].rearrange("p (a n) -> p a n", a=4)
    q_raw = wf[:, 8 * S:16 * S].rearrange("p (a n) -> p a n", a=8)

    def kv_first():
        units = features(h, NC, 2, T2), tokens(h, 4)
        dst = k_raw, v_tok.rearrange("p (a b) n -> p a (b n)", a=2)

        def kv_keep(ul, u, slot):
            wait(act, unit_done, u + 1)
            act.activation(dst[slot], ps_g[:, 2 * slot:2 * slot + 2, :], ACT.Copy).then_inc(evac.sem, 1)
        mods_pending.append((N_MODS - 1, 1))
        return Phase(t["attn_kv"], 2, UNIT, lambda ul, slot, ready: units[slot](ul, slot, ready), kv_keep)
    first = ffn(first, "gu10", "dn10", h, hid, 2, kv_first, True)
    after()

    sem_s = Count(nc, "item_scores")
    sem_m = Count(nc, "item_max")
    sem_e = Count(nc, "item_exp")
    sem_r = Count(nc, "item_normed")
    sem_t = Count(nc, "item_turned")
    sem_c = Count(nc, "item_copied")
    sem_o = Count(nc, "item_out")
    sem_k = Count(nc, "tile_kept")

    def attention(items, o_dst, scratch, probs):
        N = len(items)
        turned = [ps_g[:, 3, :], ps_s[:, 2, :], ps_s[:, 3, :]]
        b_s, b_m, b_e, b_r, b_t, b_c, b_o, b_k = (c.n for c in (sem_s, sem_m, sem_e, sem_r, sem_t, sem_c, sem_o, sem_k))
        tiles_done = {}
        order = []
        for i, it in enumerate(items):
            if it["close"]:
                tiles_done[i] = len(order)
                order.append(it["tile"])

        def s_scores(i):
            it = items[i]
            if i >= 3:
                wait(pe, sem_m, b_m + i - 2)
            sem_s.inc(pe.matmul(ps_g[:, i % 3, 0:it["n"]], it["q"], it["k"], start=True, stop=True))

        max_at, sum_at = {}, {}

        def s_max(i):
            it = items[i]
            n = it["n"]
            wait(dve, sem_s, b_s + i + 1)
            if i >= 4:
                wait(dve, sem_t, b_t + i - 3)
            max_at[i] = V(dve.tensor_tensor_reduce(scratch[i % 4][:, 0:n], ps_g[:, i % 3, 0:n], it["mask"], 1.0,
                                                   -3.0e38, ALU.add, ALU.max, stats[:, 0, i:i + 1]))

        def s_bias(i):
            it = items[i]
            wait(dve, v_, max_at[i])
            if it["sink"] is None:
                sem_m.inc(dve.tensor_scalar(stats[:, 1, i:i + 1], stats[:, 0, i:i + 1], -0.125, None, ALU.mult))
            else:
                sem_m.inc(dve.tensor_scalar(stats[:, 1, i:i + 1], stats[:, 0, i:i + 1], -0.125,
                                            it["neg_sink"], ALU.mult, ALU.min))

        def s_exp(i):
            it = items[i]
            n = it["n"]
            wait(act, sem_m, b_m + i + 1)
            ins = act.activation(scratch[i % 4][:, 0:n], scratch[i % 4][:, 0:n], ACT.Exp,
                                 bias=stats[:, 1, i:i + 1], scale=0.125, accum_out=stats[:, 2, i:i + 1])
            if it["sink"] is not None:
                A(ins)
                ins = act.activation(stats[:, 3, i:i + 1], it["sink"], ACT.Exp, bias=stats[:, 1, i:i + 1])
            sem_e.inc(ins)

        def s_sum(i):
            wait(dve, sem_e, b_e + i + 1)
            if items[i]["sink"] is None:
                sum_at[i] = V(dve.reciprocal(stats[:, 4, i:i + 1], stats[:, 2, i:i + 1]))
            else:
                sum_at[i] = V(dve.tensor_tensor(stats[:, 2, i:i + 1], stats[:, 2, i:i + 1], stats[:, 3, i:i + 1],
                                                ALU.add))

        def s_norm(i):
            it = items[i]
            n = it["n"]
            wait(dve, v_, sum_at[i])
            if it["sink"] is not None:
                wait(dve, v_, V(dve.reciprocal(stats[:, 4, i:i + 1], stats[:, 2, i:i + 1])))
            p = scratch[i % 4][:, 0:n]
            if it["weight"] is None:
                sem_r.inc(dve.tensor_scalar(p, p, stats[:, 4, i:i + 1], None, ALU.mult))
            else:
                sem_r.inc(dve.tensor_scalar(p, p, stats[:, 4, i:i + 1], it["weight"], ALU.mult, ALU.mult))

        def s_turn(i):
            it = items[i]
            wait(pe, sem_r, b_r + i + 1)
            if i >= 3:
                wait(pe, sem_c, b_c + i - 2)
            k = 0
            while k * P < it["n"]:
                w = min(P, it["n"] - k * P)
                ins = pe.transpose(turned[i % 3][0:w, k * P:(k + 1) * P],
                                   scratch[i % 4][:, k * P:k * P + w], ident)
                k += 1
            sem_t.inc(ins)

        def s_copy(i):
            it = items[i]
            n = it["n"]
            w = min(P, n)
            m = -(-n // P) * P
            wait(act, sem_t, b_t + i + 1)
            if i >= 2:
                wait(act, sem_o, b_o + i - 1)
            sem_c.inc(act.activation(probs[0:w, i % 2, 0:m], turned[i % 3][0:w, 0:m], ACT.Copy))

        def s_out(i):
            it = items[i]
            n = it["n"]
            w = min(P, n)
            wait(pe, sem_c, b_c + i + 1)
            closed = [j for j in tiles_done if j < i]
            if it["open"] and len(closed) >= 2:
                wait(pe, sem_k, b_k + len(closed) - 1)
            bank = len(closed) % 2
            last = -(-n // P)
            for k in range(last):
                ins = pe.matmul(ps_s[it["half"] * HD:(it["half"] + 1) * HD, bank, it["qt"] * P:(it["qt"] + 1) * P],
                                it["v"](k), probs[0:w, i % 2, k * P:(k + 1) * P],
                                start=(it["first"] and k == 0), stop=(it["last"] and k == last - 1))
            sem_o.inc(ins)

        def s_keep(i):
            if i not in tiles_done:
                return
            n = tiles_done[i]
            tile = order[n]
            wait(act, sem_o, b_o + i + 1)
            A(act.activation(o_dst[0][:, tile, 0:S], ps_s[:, n % 2, 0:S], ACT.Copy))
            wait(dve, a_)
            sem_k.inc(dve.tensor_tensor(o_dst[1][:, tile, 0:S], ps_s[:, n % 2, 0:S],
                                        o_dst[0][:, tile, 0:S].bitcast(F32), ALU.subtract))

        for e in (v_, a_, evac):
            wait(pe, e)
        for e in (a_, evac):
            wait(dve, e)
        for e in (v_, p_):
            wait(act, e)
        for s in range(N + 8):
            for stage, lag in ((s_scores, 0), (s_max, 0), (s_sum, 1), (s_bias, 0), (s_exp, 0), (s_norm, 1), (s_turn, 3), (s_copy, 3),
                               (s_out, 5), (s_keep, 6)):
                if 0 <= s - lag < N:
                    stage(s - lag)
        wait(pe, sem_k)

    def attn_layer(kv, following):
        before, after = adaln(1, 3, 2, 1.0, 2)
        kv.ready = before()
        yf = y[:].rearrange("p a b -> p (a b)")
        q = yf[:, 0:8 * S].rearrange("p (a n) -> p a n", a=8)
        k = yf[:, 8 * S:12 * S].rearrange("p (a n) -> p a n", a=2)
        m1 = yf[:, 12 * S:14 * S].rearrange("p (a n) -> p a n", a=2)
        qp = Phase(t["attn_q"], NC // 2, UNIT, features(h, NC, 2, S), keep(q_raw, S))
        kv.run(qp)
        assert mod_kept.n + N_FIRST == N_MODS - 1
        mod_sum(N_MODS - 1, 1)
        mod_keep(N_MODS - 1, 1)
        mod_done.n += 1
        mod_kept.n += 1
        wait(act, mod_done)
        for dst, src in ((band, t["band"]), (rope1, t["rope1"])):
            consts_in.inc(act.dma_start(dst, src), 16)
        wo = Phase(t["attn_o"], NC // 2, UNIT, features(hid, NC, 2, S), keep(y, S), *sum_squares(y, S, 2))
        wait(dve, consts_in)
        wait(pe, evac)
        wait(dve, evac)
        cos = rope1[:, 0:1, :].to_broadcast([P, 2, S])
        sin = rope1[:, 1:2, :].to_broadcast([P, 2, S])

        def rotate(src, dst, made):
            bank = ps_s[:, 0, :].rearrange("p (a n) -> p a n", a=2)
            for e in (pe, dve):
                wait(e, evac, made)
            wait(pe, v_)
            wait(dve, p_, PEs(pe.matmul(bank, swap1, src, start=True, stop=True)))
            V(dve.tensor_tensor(dst, src, cos, ALU.mult))
            wait(dve, v_, V(dve.tensor_tensor(m1, bank, sin, ALU.mult)))
            V(dve.tensor_tensor(dst, dst, m1, ALU.add))

        u0 = CREDIT + qp.u0

        def keys():
            rotate(k_raw[:, :, 0:S], k[:, :, 0:S], u0)
            V(dve.tensor_copy(k[:, :, S:T2], k_raw[:, :, S:T2]))

        def queries(n):
            rotate(q_raw[:, 2 * n:2 * n + 2, :], q[:, 2 * n:2 * n + 2, :], u0 + n + 1)
        qp.run_beside([keys] + [lambda n=n: queries(n) for n in range(3)], wo)
        queries(3)

        items = []
        for tile in range(NC):
            for half in range(2):
                head = (tile // 4) * 8 + half * 4 + tile % 4
                kvh = head // 4
                for qt in range(2):
                    rows = slice(half * HD, (half + 1) * HD)
                    items.append(dict(
                        q=q[rows, tile, qt * P:(qt + 1) * P], k=k[rows, kvh // 2, :], n=T2, mask=band[:, qt, :],
                        sink=vec("sink", head), neg_sink=vec("neg_sink", head), weight=None,
                        v=lambda kt, kvh=kvh: v_tok[:, kt, kvh * HD:(kvh + 1) * HD],
                        tile=tile, half=half, qt=qt, first=True, last=True,
                        open=(half == 0 and qt == 0), close=(half == 1 and qt == 1)))
        assert len(items) <= 64
        V(dve.tensor_scalar(vec("neg_sink", 0, 16), vec("sink", 0, 16), -1.0, None, ALU.mult))
        attention(items, hid, score_slots, prod)
        wait(act, sem_k)
        wait(dve, sem_o)
        first = following()
        wo.run(first, put_off=True)
        after(1)
        return first

    first = attn_layer(first, lambda: ffn_first("gu11", h, hid, 1))
    before, after = adaln(1, 6, 4, 0.5, 1)
    first.ready = before()
    first = ffn(first, "gu11", "dn11", h, hid, 1, lambda: Phase(t["w_in_a"], 8, UNIT, None, None))
    after()

    for e in (v_, a_, evac):
        wait(act, e)
    b1.close()
    b2 = ExitStack()
    h = [sb(f"b2_h{j}", [P, NC, S], F32R, b2) for j in range(2)]
    qk = sb("qk", [P, 18, S], F32, b2)
    gates = sb("gates", [P, 2 * NC, S], F32, b2)
    v_tok = sb("v_tok", [P, 2, 3 * S], F32, b2)
    flat = sb("flat", [P, 2, 16, 2, 15], F32, b2)
    rope2 = sb("rope2", [P, 2, S], F32, b2)
    causal = sb("causal", [P, S + 30], F32, b2)
    gn = [sb(f"gn{j}", [P, NC * 24], F32R, b2) for j in range(2)]
    small = sb("small", [P, 320], F32, b2)
    whole_turns = sb("whole_turns", [P, S], I32, b2)
    gate_n = sb("gate_n", [P, NC * 24], F32, b2)
    pos_i = sb("pos_i", [P, S], I32, b2)
    p_in = sb("p_in", [P, 2, S], F32, b2)
    branch = small[:, 0:48].rearrange("p (q n) -> p q n", q=2)
    hid_c = small[:, 48:168].rearrange("p (k m n) -> p k m n", k=2, m=2)
    kc = small[:, 168:183]
    kc_tmp = small[:, 184:199]
    yt = y[:].rearrange("p a b -> p (a b)").rearrange("p (a n) -> p a n", n=S)
    NT = 14
    early = ExitStack()
    to_row = sb("to_row", [P, NT, 2 * NT], F32, early)
    from_row = sb("from_row", [2 * NT, NT, P], F32, early)
    gate_t = sb("gate_t", [24, S], F32, early)
    hid_t = sb("hid_t", [30, 2, S], F32, early)
    rows = sb("rows", [2 * NT, S], F32, early)

    loads2 = [
        (x[:, :, S:T2], t["cw1"][0].rearrange("p (k n) -> p k n", k=8)),
        (mod_raw[0][:].rearrange("p a b -> p (a b)"), t["cw1"][1][:, 0:1024]),
        (mod_raw[1][:].rearrange("p a b -> p (a b)"), t["cw1"][1][:, 1024:2048]),
        (y[:, 0:4, :].rearrange("p a b -> p (a b)"), t["cw1"][2]),
        (y[:, 4:8, :].rearrange("p a b -> p (a b)"), t["cw1"][3]),
        (causal[:], t["causal"]),
        (to_row[:], t["to_row"]),
        (from_row[:], t["from_row"]),
        (gate_n[:], t["gate_n"]),
        (p_in[:], t["p"]),
        (pos_i[:], t["positions"].partition_broadcast(P)),
    ]
    for dst, src in loads2:
        consts_in.inc(act.dma_start(dst, src), 16)

    def compress_w(kv, jp):
        if kv == 1:
            return yt[:, jp, :]
        if jp < 8:
            return x[:, jp, S:T2]
        return mod_raw[(jp - 8) // 4][:, 2 * (jp % 4):2 * (jp % 4) + 2, :].rearrange("p a b -> p (a b)")

    def norm2(name):
        ready = norm_in(h[0], h[1], 1, lambda c, s: vec(name, c))
        catch_up()
        return ready

    feat = features(h, NC, 2, S)
    tok2 = tokens(h, 2)

    def tok_keep(col):
        def go(ul, u, slot):
            wait(act, unit_done, u + 1)
            c = col(ul)
            act.activation(v_tok[:, :, c:c + S], ps_g[:, 2 * slot, :].rearrange("p (a n) -> p a n", a=2),
                           ACT.Copy).then_inc(evac.sem, 1)
        return go

    qk_keep = keep(qk, S)
    ph_a = first
    ph_a.pe_unit, ph_a.empty, ph_a.ready = feat, qk_keep, norm2("g_mix")

    vs_keep = tok_keep(lambda ul: 0)

    def b_keep(ul, u, slot):
        if slot == 0:
            wait(act, unit_done, u + 1)
            act.activation(qk[:, 16:18, :], ps_g[:, 0:2, 0:S], ACT.Copy).then_inc(evac.sem, 1)
        else:
            vs_keep(ul, u, slot)
    ph_b = Phase(t["w_in_b"], 2, UNIT, lambda ul, slot, ready: (feat, tok2)[slot](ul, slot), b_keep)
    ph_a.run(ph_b)
    ph_c = Phase(t["w_in_c"], 2, UNIT, tok2, tok_keep(lambda ul: S + ul * S))
    ph_b.run(ph_c)
    ph_d = Phase(t["w_in_d"], 8, UNIT, feat, keep(gates, S, 2, ACT.Sigmoid))
    wait(act, consts_in)
    wait(dve, consts_in)
    wait(dve, evac)

    def branch_matmuls():
        wait(pe, v_)
        for k in range(NC):
            for n, (wp, ap) in enumerate(PARTS):
                mm = pe.matmul(ps_s[0:24, 2, 0:S], gn[wp][:, k * 24:(k + 1) * 24], h[ap][:, k, :],
                               start=(k == 0 and n == 0), stop=(k == NC - 1 and n == 2))
        wait(act, p_, PEs(mm))
        A(act.activation(gate_t[:], ps_s[0:24, 2, 0:S], ACT.Sigmoid))

    def branch_gates():
        wait(pe, a_)
        for qt in range(2):
            mm = pe.transpose(ps_s[:, 3, qt * 24:(qt + 1) * 24], gate_t[:, qt * P:(qt + 1) * P], ident[0:24, 0:24])
        wait(act, p_, PEs(mm))
        wait(dve, a_, A(act.activation(branch, ps_s[:, 3, 0:48].rearrange("p (q n) -> p q n", q=2), ACT.Copy)))
        comp = branch.rearrange("p q (h b) -> p q h b", b=3)
        V(dve.tensor_scalar(comp[:, 0, :, 0], comp[:, 0, :, 0], vec("any_block"), None, ALU.mult))

    pos_f, turns, kf, ang = (sq[:, 0, 0:S], sq[:, 0, S:T2], sq[:, 1, 0:S], sq[:, 1, S:T2])
    k_int = whole_turns[:]

    def step(ins):
        V(ins)
        wait(dve, v_)

    def angles(n, quarter_turn, shift):
        rope = rope2[:, n, :]
        step(dve.tensor_scalar(turns, ang, 0.15915494309189535, quarter_turn, ALU.mult, ALU.add))
        step(dve.tensor_copy(k_int, turns))
        step(dve.tensor_copy(kf, k_int))
        step(dve.scalar_tensor_tensor(rope, kf, -TWO_PI_HI, ang, ALU.mult, ALU.add))
        step(dve.scalar_tensor_tensor(rope, kf, -TWO_PI_MID, rope, ALU.mult, ALU.add))
        step(dve.scalar_tensor_tensor(rope, kf, -TWO_PI_LO, rope, ALU.mult, ALU.add))
        step(dve.tensor_scalar(rope, rope, shift, PI_SAFE, ALU.add, ALU.min))
        step(dve.tensor_scalar(rope, rope, -PI_SAFE, None, ALU.max))

    def flatten(kv):
        pe_col = vec("pe_k" if kv == 0 else "pe_v", 0, 16)
        for g in range(2):
            for odd in range(2):
                half = slice(odd * HD, (odd + 1) * HD)
                by16 = qk[half, 14 + 2 * kv + g, :].rearrange("p (c j) -> p j c", j=16)
                for late in range(2):
                    V(dve.tensor_tensor(flat[half, kv, 8 * late:8 * late + 8, g, :],
                                        by16[:, odd:16:2, late:late + 15],
                                        pe_col[half, 8 * late:8 * late + 8].unsqueeze(2).to_broadcast([HD, 8, 15]),
                                        ALU.add))

    def compress(kv):
        wait(pe, a_)
        wait(pe, v_)
        for jp in range(16):
            mm = pe.matmul(ps_s[0:30, 1, 0:S], flat[:, kv, jp, :, :].rearrange("p g c -> p (g c)"), compress_w(kv, jp),
                           start=(jp == 0), stop=(jp == 15))
        wait(act, p_, PEs(mm))
        A(act.activation(hid_t[:, kv, :], ps_s[0:30, 1, 0:S], ACT.Silu))

    def turn_hidden():
        wait(pe, a_)
        for kv in range(2):
            for m in range(2):
                mm = pe.transpose(ps_s[:, 1, 30 * (2 * kv + m):30 * (2 * kv + m) + 30], hid_t[:, kv, m * P:(m + 1) * P],
                                  ident[0:30, 0:30])
        wait(act, p_, PEs(mm))
        A(act.activation(hid_c[:].rearrange("p k m n -> p (k m n)"), ps_s[:, 1, 0:120], ACT.Copy))

    v_cmp = flat[0:15, 1, 0:5, :, :].rearrange("p a b c -> p (a b c)")[:, 0:2 * HD]
    KC = slice(128, 143)

    def compress_second():
        wait(pe, a_)
        for g in range(2):
            for m in range(2):
                mm = pe.matmul(ps_s[g * HD:(g + 1) * HD, 1, KC], vec("cw2_k", m * HD, HD),
                               hid_c[:, 0, m, g * 15:g * 15 + 15], start=(m == 0), stop=(m == 1))
        for g in range(2):
            for m in range(2):
                mm = pe.matmul(ps_s[0:15, 1, S + g * HD:S + (g + 1) * HD], hid_c[:, 1, m, g * 15:g * 15 + 15],
                               vec("cw2_v", m * HD, HD), start=(m == 0), stop=(m == 1))
        PEs(mm)

    def square(pair):
        A(act.activation(ring[pair % 4].rearrange("p (a n) -> p a n", a=2), qk[:, 2 * pair:2 * pair + 2, :],
                         ACT.Square))

    def sum_rows(pairs):
        wait(pe, a_)
        for j in [2 * pair + n for pair in pairs for n in range(2)]:
            mm = pe.matmul(ps_s[0:2 * NT, 0, 0:S], to_row[:, j, :], ring[j // 2 % 4][:, S * (j % 2):S * (j % 2) + S],
                           start=(j == 0), stop=(j == NT - 1))
        PEs(mm)

    def rstd_rows():
        wait(dve, p_)
        wait(act, v_, V(dve.tensor_scalar(rows[:], ps_s[0:2 * NT, 0, 0:S], 1.0 / HD, EPS, ALU.mult, ALU.add)))
        wait(dve, a_, A(act.activation(rows[:], rows[:], ACT.Sqrt)))
        V(dve.reciprocal(rows[:], rows[:]))

    BANKS = (2, 3, 0)

    def spread(pairs):
        wait(pe, v_)
        for n, pair in enumerate(pairs):
            for j in (2 * pair, 2 * pair + 1):
                mm = pe.matmul(ps_s[:, BANKS[n], S * (j % 2):S * (j % 2) + S], from_row[:, j, :], rows[:],
                               start=True, stop=True)
            PEs(mm)

    def normalise(pairs):
        wait(dve, p_)
        for n, pair in enumerate(pairs):
            for j in (2 * pair, 2 * pair + 1):
                V(dve.scalar_tensor_tensor(qk[:, j, :], qk[:, j, :], vec("qk_gain", j),
                                           ps_s[:, BANKS[n], S * (j % 2):S * (j % 2) + S], ALU.mult, ALU.mult))

    cos2, sin2 = rope2[:, 0:1, :], rope2[:, 1:2, :]

    def swap(pairs, n0=0):
        wait(pe, v_)
        for n, pair in enumerate(pairs):
            PEs(pe.matmul(ps_s[:, BANKS[n0 + n], :], swap2[:], qk[:, 2 * pair:2 * pair + 2, :], start=True, stop=True))

    def rotate(pairs, n0=0):
        wait(pool, p_)
        wait(pool, v_)
        wait(pool, a_)
        wait(dve, p_)
        sines = []
        for n, pair in enumerate(pairs):
            two = qk[:, 2 * pair:2 * pair + 2, :]
            g_.inc(pool.tensor_tensor(two, two, cos2.to_broadcast([P, 2, S]), ALU.mult))
            m1 = ring[pair % 4].rearrange("p (a n) -> p a n", a=2)
            V(dve.tensor_tensor(m1, ps_s[:, BANKS[n0 + n], :].rearrange("p (a n) -> p a n", a=2),
                                sin2.to_broadcast([P, 2, S]), ALU.mult))
            sines.append((two, m1))
        wait(dve, v_)
        g0 = g_.n - len(pairs)
        for n, (two, m1) in enumerate(sines):
            wait(dve, g_, g0 + n + 1)
            V(dve.tensor_tensor(two, two, m1, ALU.add))

    def kc_first():
        wait(act, p_)
        A(act.activation(kc, ps_s[:, 1, KC], ACT.Copy))
        A(act.activation(v_cmp, ps_s[0:15, 1, S:S + 2 * HD], ACT.Copy))
        wait(act, a_)
        A(act.activation(kc_tmp, kc, ACT.Square))

    def kc_sum():
        wait(pe, a_)
        PEs(pe.matmul(ps_s[:, 1, KC], head_ones, kc_tmp, start=True, stop=True))

    def kc_norm():
        wait(dve, p_)
        wait(act, v_, V(dve.tensor_scalar(kc_tmp, ps_s[:, 1, KC], 1.0 / HD, EPS, ALU.mult, ALU.add)))
        wait(dve, a_, A(act.activation(kc_tmp, kc_tmp, ACT.Sqrt)))
        step(dve.reciprocal(kc_tmp, kc_tmp))
        V(dve.scalar_tensor_tensor(kc, kc, vec("kc_gain"), kc_tmp, ALU.mult, ALU.mult))

    def kc_swap():
        wait(pe, v_)
        PEs(pe.matmul(ps_s[:, 1, KC], swap2[:], kc, start=True, stop=True))

    def kc_rotate():
        ends = slice(31, S, 16)
        wait(dve, p_)
        V(dve.tensor_tensor(kc_tmp, ps_s[:, 1, KC], rope2[:, 1, ends], ALU.mult))
        step(dve.tensor_tensor(kc, kc, rope2[:, 0, ends], ALU.mult))
        V(dve.tensor_tensor(kc, kc, kc_tmp, ALU.add))

    def side_c0():
        wait(dve, a_, A(act.activation(gn[0][:], gate_n[:], ACT.Copy)))
        V(dve.tensor_tensor(gn[1][:], gate_n[:], gn[0][:].bitcast(F32), ALU.subtract))
        flatten(0)
        step(dve.tensor_copy(pos_f, pos_i[:]))
        step(dve.tensor_scalar(ang, pos_f, vec("inv_freq"), None, ALU.mult))

    def side_c1():
        branch_matmuls()
        angles(0, 0.25, 1.5707963267948966)
        for pair in range(4):
            square(pair)

    def side_d0():
        sum_rows(range(4))
        angles(1, 0.0, 0.0)
        flatten(1)
        wait(act, p_)
        for pair in range(4, 7):
            square(pair)

    def side_d1():
        branch_gates()
        sum_rows(range(4, 7))
        rstd_rows()

    def side_d2():
        compress(0)

    def side_d3():
        spread((0, 1, 2))
        normalise((0, 1, 2))
        wait(act, v_)
        A(act.activation(rope2[:], rope2[:], ACT.Sin))

    def side_d4():
        compress(1)
        spread((3, 4, 5))
        normalise((3, 4, 5))

    def side_d5():
        spread((6,))
        normalise((6,))
        swap((0, 1), 1)
        turn_hidden()
        rotate((0, 1), 1)

    def side_d6():
        compress_second()
        kc_first()
        swap((2, 3, 4))
        rotate((2, 3, 4))
        kc_sum()
        kc_norm()

    def side_d7():
        swap((5, 6))
        kc_swap()
        rotate((5, 6))
        kc_rotate()

    ph_c.run_beside([side_c0, side_c1], ph_d)

    def up_unit(ul, slot, ready):
        w = [w_[slot][:].rearrange("p (k n) -> p k n", k=NC) for w_ in (w_hi, w_lo)]
        for m in range(2):
            for src in range(2):
                for k in range(4):
                    for n, (wp, ap) in enumerate(PARTS):
                        mm = pe.matmul(ps_g[:, 2 * slot + m, src * S:(src + 1) * S],
                                       w[wp][:, 4 * src + k, m * P:(m + 1) * P], hid[ap][:, 4 * src + k, 0:S],
                                       start=(k == 0 and n == 0), stop=(k == 3 and n == 2))
        return mm

    merge = Count(nc, "merge")
    merge.inc(dve.memset(small[:, 319:320], 0.0))

    merged = gate_tmp[:, 0, :].rearrange("p (m n) -> p m n", m=2)

    def merge_products(ul, u, slot):
        pa, pb = (prod[:, n, :].rearrange("p (m n) -> p m n", m=2) for n in range(2))
        wait(dve, unit_done, u + 1)
        wait(dve, merge, 3 * ul + 1)
        dve.tensor_tensor(pa, gates[:, bass.ds(2 * ul, 2), :], ps_g[:, 2 * slot:2 * slot + 2, 0:S],
                          ALU.mult).then_inc(merge.sem, 1)
        dve.tensor_tensor(pb, gates[:, bass.ds(2 * ul + NC, 2), :], ps_g[:, 2 * slot:2 * slot + 2, S:T2],
                          ALU.mult).then_inc(evac.sem, 1)
        wait(dve, merge, 3 * ul + 2)
        wait(dve, evac, CREDIT + u + 1)
        dve.tensor_tensor(merged, pa, pb, ALU.add).then_inc(merge.sem, 1)

    def merge_parts(ul, u, slot):
        wait(act, merge, 3 * ul + 3)
        act.activation(h[0][:, bass.ds(2 * ul, 2), :], merged, ACT.Copy).then_inc(out_hi.sem, 1)
        wait(dve, out_hi, hi0 + ul + 1)
        dve.tensor_tensor(h[1][:, bass.ds(2 * ul, 2), :], merged, h[0][:, bass.ds(2 * ul, 2), :].bitcast(F32),
                          ALU.subtract).then_inc(merge.sem, 1)
    hi0 = out_hi.n
    ph_up = Phase(t["w_up"], 4, UNIT, up_unit, merge_products, merge_parts)
    wait(pool, evac)
    ph_d.run_beside([side_d0, side_d1, side_d2, side_d3, side_d4, side_d5, side_d6, side_d7], ph_up)
    for e in (pe, dve, act):
        wait(e, v_)
    early.close()
    hid = [sb(f"b2_hid{j}", [P, FFN_HALVES[0], S], F32R, b2) for j in range(2)]

    items = []
    no_sink = dict(sink=None, neg_sink=None)
    for tile in range(4):
        for half in range(2):
            head = half * 4 + tile
            rows = slice(half * HD, (half + 1) * HD)
            for qt in range(2):
                n = (qt + 1) * P
                common = dict(q=qk[rows, tile, qt * P:(qt + 1) * P], tile=tile, half=half, qt=qt, **no_sink)
                wgt = [branch[:, qt, 3 * head + b:3 * head + b + 1] for b in range(3)]
                items.append(dict(common, k=kc[rows, :], n=15, mask=causal[:, S + 15 * qt:S + 15 * qt + 15],
                                  weight=wgt[0], v=lambda kt, half=half: v_cmp[:, half * HD:(half + 1) * HD],
                                  first=True, last=False, open=(half == 0 and qt == 0), close=False))
                for b, (kt_, vc_) in enumerate(((12, 0), (13, P))):
                    items.append(dict(common, k=qk[rows, kt_, 0:n], n=n, mask=causal[:, S - n:S], weight=wgt[1 + b],
                                      v=lambda kt, c=vc_ + half * HD: v_tok[:, kt, c:c + HD],
                                      first=False, last=(b == 1), open=False,
                                      close=(b == 1 and half == 1 and qt == 1)))
    for j in range(4):
        for half in range(2):
            rows = slice(half * HD, (half + 1) * HD)
            for qt in range(2):
                n = (qt + 1) * P
                items.append(dict(q=qk[rows, 4 + j, qt * P:(qt + 1) * P], tile=4 + j, half=half, qt=qt,
                                  k=qk[rows, 8 + j, 0:n], n=n, mask=causal[:, S - n:S], weight=None, **no_sink,
                                  v=lambda kt, c=S + (2 * j + half) * HD: v_tok[:, kt, c:c + HD],
                                  first=True, last=True, open=(half == 0 and qt == 0),
                                  close=(half == 1 and qt == 1)))
    attention(items, hid, score_slots, prod)
    wait(act, sem_k)
    wait(dve, sem_c)
    wait(dve, sem_o)
    wait(dve, sem_t)

    ph_o = Phase(t["w_out"], 4, UNIT, features(h, NC, 2, S), add_to(x, S, 2),
                 *sum_squares(x, S, 2))
    ph_up.run(ph_o)
    merge.n += 12
    out_hi.n += 4
    ph_o.ready = lambda k: wait(pe, merge, 3 * (k // 2) + 4)
    first = ffn_first("gu2", h, hid, 1)
    ph_o.run(first, put_off=True)
    wait(dve, evac)
    wait(act, evac)
    first.ready = norm2("g_ffn")
    ph_g = ffn(first, "gu2", "dn2", h, hid, 1,
               lambda: Phase(t["ple_gate"], 4, UNIT, feat, keep(gates, S, 2, ACT.Sigmoid)), into=x)
    wait(dve, evac)
    wait(act, evac)

    ph_g.ready = norm2("g_ple")
    wait(dve, a_, A(act.activation(hid[0][:, 0:2, :], p_in[:], ACT.Copy)))
    V(dve.tensor_tensor(hid[1][:, 0:2, :], p_in[:], hid[0][:, 0:2, :].bitcast(F32), ALU.subtract))

    ph_p = Phase(t["ple_proj"], 1, UNIT, None, None)
    ph_g.run(ph_p)
    wait(dve, evac)
    wait(pe, evac)
    wait(pe, v_)
    wait(pe, split_lo, 2 * ph_p.u0 + 2)
    w = [w_[0][:].rearrange("p (k n) -> p k n", k=2) for w_ in (w_hi, w_lo)]
    stored = Count(nc, "stored")
    for pair in range(NC // 2):
        for m in (2 * pair, 2 * pair + 1):
            for k in range(2):
                for n, (wp, ap) in enumerate(PARTS):
                    mm = pe.matmul(ps_g[:, pair, S * (m % 2):S * (m % 2) + S], w[wp][:, k, m * P:(m + 1) * P],
                                   hid[ap][:, k, 0:S], start=(k == 0 and n == 0), stop=(k == 1 and n == 2))
        two = slice(2 * pair, 2 * pair + 2)
        wait(dve, p_, PEs(mm))
        wait(dve, v_, V(dve.tensor_tensor(yt[:, two, :], gates[:, two, :],
                                          ps_g[:, pair, :].rearrange("p (b n) -> p b n", b=2), ALU.mult)))
        wait(sp, v_, V(dve.tensor_tensor(x[:, two, 0:S], x[:, two, 0:S], yt[:, two, :], ALU.add)))
        stored.inc(sp.dma_start(out[:, two, :], x[:, two, 0:S]), 16)
    wait(sp, stored)
    b2.close()
    mem.close()


def _units(w, kc, cols):
    import numpy as np
    K, N = w.shape
    assert K == kc * P and N % cols == 0
    return np.ascontiguousarray(w.reshape(kc, P, N // cols, cols).transpose(2, 1, 0, 3)
                                .reshape(N // cols, P, kc * cols))


def _chunked(v):
    return v.reshape(-1, P).T


def _fmajor(a):
    return a.T.reshape(-1, P, a.shape[0]).transpose(1, 0, 2)


def _paired(a, b):
    import numpy as np
    K = a.shape[0]
    return np.stack([a.reshape(K, -1, P), b.reshape(K, -1, P)], axis=2).reshape(K, -1)


def layout(i):
    import numpy as np
    f32 = np.float32
    t, cols, vec_at = {}, [], {}

    def add(name, a):
        vec_at[name] = sum(c.shape[1] for c in cols)
        cols.append(np.asarray(a, f32).reshape(P, -1))

    add("cond", np.stack([_chunked(i["c"][0]), _chunked(i["c_ctx"])], axis=2))
    add("b_mod", np.repeat(_chunked(i["b_mod"].reshape(-1))[:, :, None], 2, axis=2))
    add("norm_g", np.repeat(_chunked(i["norm_g"].reshape(-1))[:, :, None], 2, axis=2))
    add("conv_w", _chunked(i["conv_w"].reshape(-1)))
    add("sink", np.broadcast_to(i["attn_sink"].reshape(1, -1), (P, 16)))
    add("neg_sink", np.zeros((P, 16)))
    for name in ("g_mix", "g_ffn", "g_ple"):
        add(name, _chunked(i[name + "_2"][0]))
    two = lambda a: np.tile(a, 2)
    gains = [i["nsa_q_gain_2"][0]] * 4 + [i["moba_q_gain_2"][0]] * 4 + [i["moba_k_gain_2"][0]] * 4 \
        + [i["nsa_ks_gain_2"][0], i["nsa_kw_gain_2"][0]]
    add("qk_gain", np.stack([two(a) for a in gains], axis=1))
    add("kc_gain", two(i["nsa_kc_gain_2"][0]))
    for name in ("pe_k", "pe_v"):
        add(name, i[f"nsa_{name}_2"][0].reshape(16, P).T)
    for name in ("cw2_k", "cw2_v"):
        w2 = i["nsa_ck_w2_2" if name == "cw2_k" else "nsa_cv_w2_2"][0]
        add(name, w2.reshape(2, P, HD).transpose(1, 0, 2))
    f2 = (np.float32(500000.0) ** (-np.arange(8, dtype=f32) / np.float32(8))).astype(f32)
    add("inv_freq", np.tile(np.concatenate([f2, f2, np.zeros(HD - 16, f32)]), 2))
    add("any_block", (np.arange(P) >= 31).astype(f32))
    t["vecs"] = np.ascontiguousarray(np.concatenate(cols, axis=1))

    eye = np.eye(P, dtype=f32)
    head_ones = np.kron(np.eye(2), np.ones((HD, HD))).astype(f32)
    quarter = HD // 4

    def swap(pairs):
        m = np.zeros((P, P), f32)
        for base in (0, HD):
            for lo, hi in pairs:
                m[base + hi, base + lo] = -1.0
                m[base + lo, base + hi] = 1.0
        return m
    swap1 = swap([(b + j, b + quarter + j) for b in (0, 2 * quarter) for j in range(quarter)])
    t["mats"] = np.ascontiguousarray(np.stack([eye, np.ones((P, P), f32), head_ones, swap1], axis=1))
    to_row = np.kron(np.eye(14), np.repeat(np.eye(2), HD, axis=0)).astype(f32)
    t["to_row"] = np.ascontiguousarray(to_row.reshape(14, P, 28).transpose(1, 0, 2))
    t["from_row"] = np.ascontiguousarray(to_row.reshape(14, P, 28).transpose(2, 0, 1))
    t["swap2"] = swap([(j, 8 + j) for j in range(8)])
    tok = np.arange(S)
    inv = (np.float32(10000.0) ** (-np.arange(quarter, dtype=f32) / np.float32(quarter))).astype(f32)
    ang = np.stack([(tok // 64).astype(f32)[:, None] * inv, (tok % 64).astype(f32)[:, None] * inv], axis=1)
    ang = np.repeat(ang[:, :, None, :], 2, axis=2).reshape(S, HD)
    t["rope1"] = np.ascontiguousarray(np.stack([np.tile(np.cos(ang).T, (2, 1)), np.tile(np.sin(ang).T, (2, 1))], axis=1)).astype(f32)
    band = np.zeros((P, 2, T2), f32)
    for qt in range(2):
        off = np.abs(np.arange(S)[None, :] - (qt * P + np.arange(P))[:, None])
        band[:, qt, 0:S] = np.where(off <= 128, 0.0, NEG)
    t["band"] = band

    t["x"] = np.ascontiguousarray(_fmajor(i["x"][0]))
    t["ctx"] = np.ascontiguousarray(_fmajor(i["ctx"][0]))

    t["w_mod"] = np.concatenate([_units(i["w_mod"][l], NC, P) for l in range(2)]).reshape(-1, P, NC, P)
    n0, n1 = FFN_HALVES
    for l in range(2):
        for j in range(2):
            gu, dn = i["ffn_w_gu"][l, j], i["ffn_w_down"][l, j]
            t[f"gu{l}{j}"] = _units(_paired(gu[:, :D_FF], gu[:, D_FF:]), NC, 2 * P)
            t[f"dn{l}{j}a"] = _units(dn[:n0 * P], n0, P)
            t[f"dn{l}{j}b"] = _units(dn[n0 * P:], n1, P)
    cw = i["conv_w_in"][0]
    t["conv_cu"] = _units(_paired(cw[:, D:2 * D], cw[:, 2 * D:]), NC, 2 * P)
    t["conv_b"] = _units(cw[:, :D], NC, 2 * P)
    t["conv_out"] = _units(i["conv_w_out"][0], NC, 2 * P)
    wq = i["attn_w_qkv"][0]
    heads = [(tile // 4) * 8 + half * 4 + tile % 4 for tile in range(8) for half in range(2)]
    t["attn_q"] = _units(wq[:, :D].reshape(D, 16, HD)[:, heads].reshape(D, D), NC, 2 * P)
    t["attn_kv"] = _units(wq[:, D:], NC, 2 * P)
    t["attn_o"] = _units(i["attn_w_o"][0].reshape(16, HD, D)[heads].reshape(D, D), NC, 2 * P)

    tri = np.where(np.arange(P)[None, :] <= np.arange(P)[:, None], 0.0, NEG)
    blocks = [np.where(16 * np.arange(15)[None, :] + 31 <= (qt * P + np.arange(P))[:, None], 0.0, NEG) for qt in range(2)]
    t["causal"] = np.concatenate([np.zeros((P, P)), tri] + blocks, axis=1).astype(f32)
    t["positions"] = np.ascontiguousarray(i["positions_2"][0])
    t["p"] = np.ascontiguousarray(_fmajor(i["p_2"][0, 0]))
    w = i["w_in_2"][0]
    cuts = np.cumsum([0, 512] + [128] * 6 + [24] + [512] * 3 + [D, D])
    q_n, kc_, vc_, ks_, vs_, kw_, vw_, g_n, q_m, k_m, v_m, g_a, g_b = (w[:, a:b] for a, b in zip(cuts[:-1], cuts[1:]))
    order = [half * 4 + tile for tile in range(4) for half in range(2)]
    twice = lambda a: [a[:, 0:HD], a[:, 0:HD], a[:, HD:P], a[:, HD:P]]
    cat = lambda parts: np.concatenate(parts, axis=1)
    t["w_in_a"] = _units(cat([q_n.reshape(D, 8, HD)[:, order].reshape(D, 512), q_m, k_m, ks_, kw_] + twice(kc_)), NC, 2 * P)
    t["w_in_b"] = _units(cat(twice(vc_) + [vs_, vw_]), NC, 2 * P)
    t["w_in_c"] = _units(v_m, NC, 2 * P)
    t["w_in_d"] = _units(cat([g_a, g_b]), NC, 2 * P)
    t["gate_n"] = _units(g_n, NC, 24)[0]
    t["cw1"] = np.concatenate([_units(i[n][0][a:a + D], NC, 2 * P) for n in ("nsa_ck_w1_2", "nsa_cv_w1_2") for a in (0, D)])
    up_n = i["w_up_nsa_2"][0].reshape(8, HD, D)[order].reshape(512, D)
    t["w_up"] = _units(np.concatenate([up_n, i["w_up_moba_2"][0]]), NC, 2 * P)
    t["w_out"] = _units(i["w_out_2"][0], NC, 2 * P)
    gu, dn = i["w_ffn_in_2"][0], i["w_ffn_out_2"][0]
    t["gu2"] = _units(_paired(gu[:, :D_FF], gu[:, D_FF:]), NC, 2 * P)
    t["dn2a"], t["dn2b"] = _units(dn[:n0 * P], n0, P), _units(dn[n0 * P:], n1, P)
    t["ple_gate"] = _units(i["w_ple_gate_2"][0], NC, 2 * P)
    t["ple_proj"] = _units(i["w_ple_proj_2"][0], 2, D)
    return t, vec_at


def kernel(**inputs):
    import numpy as np
    import concourse.bacc as bacc
    from concourse.bass_utils import run_bass_kernel_spmd

    arrays, vec_at = layout({k: np.asarray(v) for k, v in inputs.items()})
    nc = bacc.Bacc("TRN2", target_bir_lowering=False, num_devices=1)
    t = {n: nc.dram_tensor(f"in_{n}", a.shape, mybir.dt.from_np(a.dtype), kind="ExternalInput").ap()
         for n, a in arrays.items()}
    out = nc.dram_tensor("out", (P, NC, S), F32, kind="ExternalOutput").ap()
    build(nc, t, out, vec_at)
    r = run_bass_kernel_spmd(nc, [{f"in_{n}": a for n, a in arrays.items()}], core_ids=[0])
    return r.results[0]["out"].transpose(2, 1, 0).reshape(1, S, D)
```
